# Optimizing a Trainium2 kernel written in Bass

```python
import math
import jax, jax.numpy as jnp
from jax import lax
import numpy as np

D_MODEL = 1024
BATCH = 1
SEQ = 256
DEPTH = 1

CHUNK = 64
MEM_LEN = 256
Q_BLOCK = 128
ROPE_THETA = 10000.0
NORM_EPS = 1e-6

SB_HEADS = D_MODEL // 128
SB_HEAD_DIM = 64
SB_WIDTH = SB_HEADS * SB_HEAD_DIM
DIFF_HEADS = D_MODEL // 256
DIFF_HEAD_DIM = 64
DIFF_V_DIM = 2 * DIFF_HEAD_DIM
DIFF_QK_WIDTH = DIFF_HEADS * 2 * DIFF_HEAD_DIM
DIFF_WIDTH = DIFF_HEADS * DIFF_V_DIM
N_BRANCH = 2
N_IN = 3 * SB_WIDTH + 2 * DIFF_QK_WIDTH + DIFF_WIDTH + N_BRANCH * D_MODEL
MEM_HEADS = 4
MEM_HEAD_DIM = D_MODEL // MEM_HEADS
N_EXPERTS = 32
TOP_K = 4
D_FF = D_MODEL
SWIGLU_LIMIT = 7.0
SWIGLU_ALPHA = 1.702
MOE_BLOCK = 128

kernel_name = "hybrid_stickbreak_diffattn_moe_block"

def rms_norm(x, g):
    xf = x.astype(jnp.float32)
    y = xf * lax.rsqrt(jnp.mean(xf * xf, axis=-1, keepdims=True) + NORM_EPS)
    return (y * g.astype(jnp.float32)).astype(x.dtype)

def split_heads(t, n_heads):
    b, s, _ = t.shape
    return t.reshape(b, s, n_heads, -1).transpose(0, 2, 1, 3)

def merge_heads(t):
    b, n, s, d = t.shape
    return t.transpose(0, 2, 1, 3).reshape(b, s, n * d)

def rope(t, positions):
    half = t.shape[-1] // 2
    inv = ROPE_THETA ** (-jnp.arange(half, dtype=jnp.float32) / half)
    ang = positions.astype(jnp.float32)[:, None, :, None] * inv
    cos, sin = jnp.cos(ang), jnp.sin(ang)
    tf = t.astype(jnp.float32)
    t1, t2 = tf[..., :half], tf[..., half:]
    return jnp.concatenate([t1 * cos - t2 * sin, t2 * cos + t1 * sin], axis=-1).astype(t.dtype)

def to_blocks(t):
    b, h, s, d = t.shape
    return t.reshape(b, h, s // Q_BLOCK, Q_BLOCK, d).transpose(2, 0, 1, 3, 4)

def from_blocks(t):
    nb, b, h, qb, d = t.shape
    return t.transpose(1, 2, 0, 3, 4).reshape(b, h, nb * qb, d)

def stick_breaking_attention(q, k, v):
    s_len = q.shape[2]
    scale = 1.0 / math.sqrt(q.shape[-1])
    key_pos = jnp.arange(s_len)

    def block(args):
        qb, start = args
        z = jnp.einsum('bhqd,bhkd->bhqk', qb, k, preferred_element_type=jnp.float32) * scale
        q_pos = start + jnp.arange(Q_BLOCK)
        mask = key_pos[None, :] < q_pos[:, None]
        log_rem = jnp.where(mask, jax.nn.log_sigmoid(-z), 0.0)
        after = lax.cumsum(log_rem, axis=log_rem.ndim - 1, reverse=True) - log_rem
        w = jnp.where(mask, jnp.exp(jax.nn.log_sigmoid(z) + after), 0.0)
        return jnp.einsum('bhqk,bhkd->bhqd', w.astype(v.dtype), v)

    starts = jnp.arange(s_len // Q_BLOCK) * Q_BLOCK
    return from_blocks(lax.map(block, (to_blocks(q), starts)))

def differential_attention(q1, q2, k1, k2, v, lam):
    s_len = q1.shape[2]
    scale = 1.0 / math.sqrt(q1.shape[-1])
    key_chunk = jnp.arange(s_len) // CHUNK

    def block(args):
        q1b, q2b, start = args
        q_chunk = (start + jnp.arange(Q_BLOCK)) // CHUNK
        mask = key_chunk[None, :] <= q_chunk[:, None]

        def probs(qb, kk):
            z = jnp.einsum('bhqd,bhkd->bhqk', qb, kk, preferred_element_type=jnp.float32) * scale
            return jax.nn.softmax(jnp.where(mask, z, -jnp.inf), axis=-1)

        p = probs(q1b, k1) - lam * probs(q2b, k2)
        return jnp.einsum('bhqk,bhkd->bhqd', p.astype(v.dtype), v)

    starts = jnp.arange(s_len // Q_BLOCK) * Q_BLOCK
    return from_blocks(lax.map(block, (to_blocks(q1), to_blocks(q2), starts)))

def memory_cross_attention(h, hm, w_q, w_kv, w_o):
    q = split_heads(h @ w_q, MEM_HEADS)
    k, v = jnp.split(hm @ w_kv, 2, axis=-1)
    k, v = split_heads(k, MEM_HEADS), split_heads(v, MEM_HEADS)
    z = jnp.einsum('bhqd,bhkd->bhqk', q, k, preferred_element_type=jnp.float32) / math.sqrt(MEM_HEAD_DIM)
    p = jax.nn.softmax(z, axis=-1)
    o = jnp.einsum('bhqk,bhkd->bhqd', p.astype(v.dtype), v)
    return merge_heads(o) @ w_o

def moe_ffn(h, w_router, b_router, w_gu, b_gu, w_down, b_down):
    b, s, d = h.shape
    n_tok = b * s
    xf = h.reshape(n_tok, d)
    logits = (xf @ w_router).astype(jnp.float32) + b_router.astype(jnp.float32)
    top_val, top_idx = lax.top_k(logits, TOP_K)
    gate = jax.nn.softmax(top_val, axis=-1)

    n_assign = n_tok * TOP_K
    flat_e = top_idx.reshape(-1)
    order = jnp.argsort(flat_e)
    sorted_e = flat_e[order]
    sorted_tok = (order // TOP_K).astype(jnp.int32)
    sorted_gate = gate.reshape(-1)[order]
    counts = jnp.bincount(flat_e, length=N_EXPERTS)
    padded = (counts + MOE_BLOCK - 1) // MOE_BLOCK * MOE_BLOCK
    start = jnp.cumsum(counts) - counts
    pend = jnp.cumsum(padded)
    pstart = pend - padded
    dest = pstart[sorted_e] + jnp.arange(n_assign) - start[sorted_e]
    n_blocks = n_assign // MOE_BLOCK + N_EXPERTS
    n_rows = n_blocks * MOE_BLOCK
    row_tok = jnp.zeros((n_rows,), jnp.int32).at[dest].set(sorted_tok)
    row_gate = jnp.zeros((n_rows,), jnp.float32).at[dest].set(sorted_gate)
    block_expert = jnp.clip(jnp.searchsorted(pend, jnp.arange(n_blocks) * MOE_BLOCK, side='right'),
                            0, N_EXPERTS - 1)

    def run_block(args):
        tok, g, e = args
        xb = xf[tok]
        hgu = xb @ w_gu[e] + b_gu[e]
        glu, lin = jnp.split(hgu, 2, axis=-1)
        glu = jnp.minimum(glu, SWIGLU_LIMIT)
        lin = jnp.clip(lin, -SWIGLU_LIMIT, SWIGLU_LIMIT)
        act = glu * jax.nn.sigmoid(SWIGLU_ALPHA * glu) * (lin + 1.0)
        y = act @ w_down[e] + b_down[e]
        return y.astype(jnp.float32) * g[:, None]

    ys = lax.map(run_block, (row_tok.reshape(n_blocks, MOE_BLOCK),
                             row_gate.reshape(n_blocks, MOE_BLOCK), block_expert))
    out = jnp.zeros((n_tok, d), jnp.float32).at[row_tok].add(ys.reshape(n_rows, d))
    return out.astype(h.dtype).reshape(b, s, d)

def setup_inputs(seed: int = 0) -> dict:
    key = jax.random.key(seed)
    ks = jax.random.split(key, 28)
    f32 = jnp.float32

    def nrm(k, shape, scale):
        return jax.random.normal(k, shape, f32) * scale

    def gain(k, shape):
        return 1.0 + 0.05 * jax.random.normal(k, shape, f32)

    offset = jax.random.randint(ks[2], (BATCH, 1), 0, 4096, dtype=jnp.int32)
    positions = (offset + jnp.arange(SEQ, dtype=jnp.int32)[None, :]).astype(jnp.int32)
    return {
        "x": nrm(ks[0], (BATCH, SEQ, D_MODEL), 1.0),
        "mem": nrm(ks[1], (BATCH, MEM_LEN, D_MODEL), 1.0),
        "positions": positions,
        "norm_mix": gain(ks[3], (DEPTH, D_MODEL)),
        "w_in": nrm(ks[4], (DEPTH, D_MODEL, N_IN), D_MODEL ** -0.5),
        "lambda_q1": nrm(ks[5], (DEPTH, DIFF_HEAD_DIM), 0.1),
        "lambda_k1": nrm(ks[6], (DEPTH, DIFF_HEAD_DIM), 0.1),
        "lambda_q2": nrm(ks[7], (DEPTH, DIFF_HEAD_DIM), 0.1),
        "lambda_k2": nrm(ks[8], (DEPTH, DIFF_HEAD_DIM), 0.1),
        "diff_subln": gain(ks[9], (DEPTH, DIFF_V_DIM)),
        "w_up_sb": nrm(ks[10], (DEPTH, SB_WIDTH, D_MODEL), SB_WIDTH ** -0.5),
        "w_up_diff": nrm(ks[11], (DEPTH, DIFF_WIDTH, D_MODEL), DIFF_WIDTH ** -0.5),
        "w_out": nrm(ks[12], (DEPTH, D_MODEL, D_MODEL), D_MODEL ** -0.5),
        "norm_mem_q": gain(ks[13], (DEPTH, D_MODEL)),
        "norm_mem_kv": gain(ks[14], (DEPTH, D_MODEL)),
        "w_mem_q": nrm(ks[15], (DEPTH, D_MODEL, D_MODEL), D_MODEL ** -0.5),
        "w_mem_kv": nrm(ks[16], (DEPTH, D_MODEL, 2 * D_MODEL), D_MODEL ** -0.5),
        "w_mem_o": nrm(ks[17], (DEPTH, D_MODEL, D_MODEL), D_MODEL ** -0.5),
        "norm_ffn": gain(ks[18], (DEPTH, D_MODEL)),
        "w_router": nrm(ks[19], (DEPTH, D_MODEL, N_EXPERTS), D_MODEL ** -0.5),
        "b_router": nrm(ks[20], (DEPTH, N_EXPERTS), 0.01),
        "w_gate_up": nrm(ks[21], (DEPTH, N_EXPERTS, D_MODEL, 2 * D_FF), D_MODEL ** -0.5),
        "b_gate_up": nrm(ks[22], (DEPTH, N_EXPERTS, 2 * D_FF), 0.02),
        "w_down": nrm(ks[23], (DEPTH, N_EXPERTS, D_FF, D_MODEL), D_FF ** -0.5),
        "b_down": nrm(ks[24], (DEPTH, N_EXPERTS, D_MODEL), 0.02),
        "norm_final": gain(ks[25], (D_MODEL,)),
    }

def reference(x, mem, positions, norm_mix, w_in, lambda_q1, lambda_k1, lambda_q2, lambda_k2,
              diff_subln, w_up_sb, w_up_diff, w_out, norm_mem_q, norm_mem_kv, w_mem_q,
              w_mem_kv, w_mem_o, norm_ffn, w_router, b_router, w_gate_up, b_gate_up,
              w_down, b_down, norm_final):
    splits = [SB_WIDTH, 2 * SB_WIDTH, 3 * SB_WIDTH,
              3 * SB_WIDTH + DIFF_QK_WIDTH,
              3 * SB_WIDTH + 2 * DIFF_QK_WIDTH,
              3 * SB_WIDTH + 2 * DIFF_QK_WIDTH + DIFF_WIDTH,
              3 * SB_WIDTH + 2 * DIFF_QK_WIDTH + DIFF_WIDTH + D_MODEL]
    b, s, _ = x.shape
    for l in range(DEPTH):
        h = rms_norm(x, norm_mix[l])
        proj = h @ w_in[l]
        sb_q, sb_k, sb_v, d_q, d_k, d_v, g_sb, g_diff = jnp.split(proj, splits, axis=-1)

        o_sb = stick_breaking_attention(split_heads(sb_q, SB_HEADS),
                                        split_heads(sb_k, SB_HEADS),
                                        split_heads(sb_v, SB_HEADS))

        dq = d_q.reshape(b, s, DIFF_HEADS, 2, DIFF_HEAD_DIM).transpose(0, 2, 3, 1, 4)
        dk = d_k.reshape(b, s, DIFF_HEADS, 2, DIFF_HEAD_DIM).transpose(0, 2, 3, 1, 4)
        q1, q2 = rope(dq[:, :, 0], positions), rope(dq[:, :, 1], positions)
        k1, k2 = rope(dk[:, :, 0], positions), rope(dk[:, :, 1], positions)
        lambda_init = 0.8 - 0.6 * math.exp(-0.3 * l)
        lam = (jnp.exp(jnp.sum(lambda_q1[l].astype(jnp.float32) * lambda_k1[l].astype(jnp.float32)))
               - jnp.exp(jnp.sum(lambda_q2[l].astype(jnp.float32) * lambda_k2[l].astype(jnp.float32)))
               + lambda_init)
        o_diff = differential_attention(q1, q2, k1, k2, split_heads(d_v, DIFF_HEADS), lam)
        o_diff = rms_norm(o_diff, diff_subln[l]) * (1.0 - lambda_init)

        y_sb = merge_heads(o_sb) @ w_up_sb[l]
        y_diff = merge_heads(o_diff) @ w_up_diff[l]
        mixed = jax.nn.sigmoid(g_sb) * y_sb + jax.nn.sigmoid(g_diff) * y_diff
        x = x + mixed @ w_out[l]

        x = x + memory_cross_attention(rms_norm(x, norm_mem_q[l]), rms_norm(mem, norm_mem_kv[l]),
                                       w_mem_q[l], w_mem_kv[l], w_mem_o[l])

        x = x + moe_ffn(rms_norm(x, norm_ffn[l]), w_router[l], b_router[l], w_gate_up[l],
                        b_gate_up[l], w_down[l], b_down[l])
    return rms_norm(x, norm_final)


_drawn_inputs = setup_inputs


def setup_inputs(seed=0):
    import zlib

    import numpy as np

    out = dict(_drawn_inputs(seed))
    spreads = {}
    factors = {'lambda_q1': 7.025, 'norm_mem_q': 3.017, 'b_gate_up': 5.688, 'b_down': 6.531}
    for name, (base, spread) in spreads.items():
        noise = np.random.default_rng([zlib.crc32(name.encode()), seed]).standard_normal(out[name].shape)
        drawn = base * np.exp(spread * noise) if base else spread * noise
        out[name] = __import__('jax').numpy.asarray(drawn.astype(out[name].dtype))
    for name, factor in factors.items():
        out[name] = (out[name] * factor).astype(out[name].dtype)
    return out
```

```python
import math
from contextlib import ExitStack

import numpy as np

import concourse.bass as bass
from concourse import mybir

F32 = mybir.dt.float32
I32 = mybir.dt.int32
U32 = mybir.dt.uint32
ALU = mybir.AluOpType
ACT = mybir.ActivationFunctionType
AX = mybir.AxisListType.X

P = 128
D = 1024
T = 256
TT = T // P
KC = D // P
HALF = 512
CHUNK = 64
EPS = 1e-6
SB_HEADS, DIFF_HEADS, MEM_HEADS = 8, 4, 4
HEAD = 64
MEM_HEAD = D // MEM_HEADS
LAMBDA_INIT = 0.8 - 0.6 * math.exp(0.0)
E = 32
TOP_K = 4
SLOTS = 64
ROUNDS = T // SLOTS
LIMIT, ALPHA = 7.0, 1.702
NOT_CHOSEN = 1024.0
STEPS = 4

(U_SBQ, U_SBK, U_SBV, U_DQ, U_DK, U_DV, U_GSB, _, U_GDF, _, U_MK, _, U_MV, _,
 U_UPS, U_UPD, U_OUT, _, U_MQ, _, U_MO, _) = range(22)
UNITS = 22
DENSE_SLOTS = 4
RING = 8
UNIT = 4096
MOE_SLOT = [4, 5, 6, 7, 2, 3, 0, 1]

C_ID, C_NTRI, C_NONE, C_ROT, C_STRI, C_ONE, C_SLOT, C_DMASK = (P * i for i in range(8))
C_IOTA = 8 * P
C_EIDX = C_IOTA + E
C_R64 = C_EIDX + ROUNDS * E
C_BLK = C_R64 + ROUNDS * E
C_INV = C_BLK + 4
C_COLS = C_INV + 1

TWO_PI_A = 6.28125
TWO_PI_B = float(np.float32(2 * math.pi - TWO_PI_A) // 2.0 ** -20 * 2.0 ** -20)
TWO_PI_C = float(np.float32(2 * math.pi - TWO_PI_A - TWO_PI_B))
ROUNDER = 1.5 * 2.0 ** 23


def constants():
    c = np.zeros((P, C_COLS), np.float32)
    p = np.arange(P)
    c[:, C_ID:C_ID + P] = np.eye(P)
    c[:, C_NTRI:C_NTRI + P] = -(p[:, None] >= p[None, :]).astype(np.float32)
    c[:, C_NONE:C_NONE + P] = -1.0
    for m in range(P):
        if m % HEAD < HEAD // 2:
            c[m + HEAD // 2, C_ROT + m] = -1.0
        else:
            c[m - HEAD // 2, C_ROT + m] = 1.0
    c[:, C_STRI:C_STRI + P] = p[:, None] < p[None, :]
    c[:, C_ONE:C_ONE + P] = 1.0
    c[:, C_SLOT:C_SLOT + P] = p[None, :] % SLOTS
    c[:, C_DMASK:C_DMASK + P] = np.where(p[None, :] // CHUNK > p[:, None] // CHUNK, -1e30, 0.0)
    c[:, C_IOTA:C_IOTA + E] = np.arange(E)
    i = np.arange(ROUNDS * E)
    c[:, C_EIDX:C_EIDX + ROUNDS * E] = i % E
    c[:, C_R64:C_R64 + ROUNDS * E] = SLOTS * (i // E)
    c[:, C_BLK:C_BLK + 4] = p[:, None] - 32 * np.arange(4)[None, :]
    half = HEAD // 2
    c[:, C_INV] = np.float32(10000.0) ** (-(p % half).astype(np.float32) / np.float32(half))
    return c


def layer(nc, consts, x, mem, positions, norm_mix, w_in, lambda_q1, lambda_k1, lambda_q2,
          lambda_k2, diff_subln, w_up_sb, w_up_diff, w_out, norm_mem_q, norm_mem_kv, w_mem_q,
          w_mem_kv, w_mem_o, norm_ffn, w_router, b_router, w_gate_up, b_gate_up, w_down, b_down,
          norm_final, out):
    ctx = ExitStack()

    def sb(name, shape, dt=F32):
        return ctx.enter_context(nc.sbuf_tensor(name, shape, dt))

    def sem(name):
        return ctx.enter_context(nc.semaphore(name))

    with ctx:
        ring = sb("ring", [P, RING, UNIT])
        cst = sb("cst", [P, C_COLS])
        xs = sb("xs", [P, TT, D])
        xn = sb("xn", [P, TT, D])
        hT = sb("hT", [P, KC, T])
        oT = sb("oT", [P, KC, T])
        kTm = sb("kTm", [P, KC, T])
        vm = sb("vm", [P, TT, D])
        scr = sb("scr", [P, 5632])
        wr = sb("wr", [P, KC, E])
        gT = sb("gT", [P, 33])
        gperm = sb("gperm", [P, KC])
        brow = sb("brow", [1, E])
        st = sb("st", [P, 96])
        middle_count = sb("middle_count", [1, 2], I32)
        topi = sb("topi", [P, TT, 8], U32)

        def region(slot, at, n):
            return ring[:, slot, at:at + n]

        hmT = region(4, 0, 2048).rearrange("p (k t) -> p k t", k=KC)
        ms = region(4, 2048, 2048).rearrange("p (a d) -> p a d", a=TT)
        qT = region(5, 0, 1024).rearrange("p (c t) -> p c t", c=4)
        kT = region(5, 1024, 1024).rearrange("p (c t) -> p c t", c=4)
        vs = region(5, 2048, 1024).rearrange("p (a d) -> p a d", a=TT)
        vd = region(5, 3072, 1024).rearrange("p (a d) -> p a d", a=TT)
        dqk = region(6, 0, 2048).rearrange("p (n c t) -> p n c t", n=2, c=4)
        raw = region(6, 2048, 2048).rearrange("p (n c t) -> p n c t", n=2, c=4)
        sg = ring[:, 7, :].rearrange("p (n k t) -> p n k t", n=2, k=KC)

        lamr = scr[:, 4736:4992].rearrange("p (r d) -> p r d", r=4)
        gffn = scr[0:4, 4992:5248]
        posi = scr[0:1, 5248:5504].bitcast(I32)
        grows = scr[0:33, 5504:5632]
        sp_t = scr[:, 0:768].rearrange("p (h n) -> p h n", h=2)
        sp_l = scr[:, 768:1536].rearrange("p (h n) -> p h n", h=2)
        sp_w = scr[:, 1536:2304].rearrange("p (h n) -> p h n", h=2)
        cosT = scr[:, 2304:2560]
        sinT = scr[:, 2560:2816]
        ang = scr[:, 2816:3328]
        angn = scr[:, 3328:3840]
        rtmp = scr[:, 2816:3840].rearrange("p (a c t) -> p a c t", a=2, c=2)
        d_e = scr[:, 3840:4608].rearrange("p (c n) -> p c n", c=2)
        d_p = scr[:, 4608:4992]
        d_pT = scr[:, 4992:5376]
        od = scr[:, 0:1024].rearrange("p (a d) -> p a d", a=TT)
        odn = scr[:, 1024:2048].rearrange("p (a d) -> p a d", a=TT)
        m_p = scr[:, 0:1024].rearrange("p (g a m) -> p g a m", g=2, a=TT)
        m_pT = scr[:, 1024:2048].rearrange("p (g m t) -> p g m t", g=2, m=TT)
        xe = scr[:, 0:1024].rearrange("p (g k s) -> p g k s", g=2, k=KC)
        glu = scr[:, 1024:1536]
        lin = scr[:, 1536:2048]
        sig = scr[:, 2048:2560]
        act = scr[:, 2560:3072]
        actT = scr[:, 3072:3584]
        yb = scr[:, 3584:4096]
        comb = scr[:, 4096:4608].rearrange("p (g t) -> p g t", g=2)
        pick = scr[:, 4608:4736].rearrange("p (a s) -> p a s", a=TT)
        pickg = scr[:, 4736:4992].rearrange("p (a s) -> p a s", a=TT)
        esel = scr[:, 4992:5008].rearrange("p (g b) -> p g b", g=4)
        gfin = kTm[:, 0:4, :].rearrange("p k t -> p (k t)")
        bgu = vm[:, 0, 0:HALF]
        bdn = vm[:, 0, HALF:2 * HALF]
        slot_of = vm[:, 1, 0:256].rearrange("p (a i) -> p a i", a=TT)
        gate_of = vm[:, 1, 256:512].rearrange("p (a i) -> p a i", a=TT)
        lg = vm[:, 1, 512:576].rearrange("p (a e) -> p a e", a=TT)
        chosen = vm[:, 1, 576:640].rearrange("p (a e) -> p a e", a=TT)
        gates = vm[:, 1, 640:704].rearrange("p (a e) -> p a e", a=TT)
        hot = vm[:, 1, 704:736]
        hotg = vm[:, 1, 736:768]
        cnt = vm[:, 1, 768:800]
        topv = vm[:, 1, 800:816].rearrange("p (a k) -> p a k", a=TT)
        topf = vm[:, 1, 816:832].rearrange("p (a k) -> p a k", a=TT)
        tope = vm[:, 1, 832:840].rearrange("p (a k) -> p a k", a=TT)
        few = vm[:, 1, 840:856]

        ident = cst[:, C_ID:C_ID + P]
        ones = cst[:, C_ONE:C_ONE + P]
        one = cst[:, C_ONE:C_ONE + 1]
        posf = scr[0:1, 3840:4096]

        bank = [ctx.enter_context(nc.psum_tensor(f"bank{i}", [P, HALF], F32)) for i in range(8)]

        const_in, small_in = sem("const_in"), sem("small_in")
        x_in, mem_in, late_in = sem("x_in"), sem("mem_in"), sem("late_in")
        unit_in = [sem(f"unit_in{k}") for k in range(DENSE_SLOTS)]
        expert_in = [sem(f"expert_in{k}") for k in range(RING)]
        expert_used = sem("expert_used")
        out_done = sem("out_done")
        dve_step, act_step = sem("dve_step"), sem("act_step")
        gain_rows_T, gain_ready = sem("gain_rows_T"), sem("gain_ready")
        pos_ready, pos_spread, ang_ready, rope_ready = (
            sem("pos_ready"), sem("pos_spread"), sem("ang_ready"), sem("rope_ready"))
        lam_dots, lam_exp, lam_ready = sem("lam_dots"), sem("lam_exp"), sem("lam_ready")
        sq_ready, ms_ready, rt_ready, xn_ready = (
            sem("sq_ready"), sem("ms_ready"), sem("rt_ready"), sem("xn_ready"))
        turned, turned_act, turned_dve = sem("turned"), sem("turned_act"), sem("turned_dve")
        bank0_full, bank1_full = sem("bank0_full"), sem("bank1_full")
        bank0_read, bank1_read = sem("bank0_read"), sem("bank1_read")
        rot_full, rot_read = sem("rot_full"), sem("rot_read")
        z_full, soft_ready, l_ready, l_masked = (
            sem("z_full"), sem("soft_ready"), sem("l_ready"), sem("l_masked"))
        after_full, w_ready, w_masked = sem("after_full"), sem("w_ready"), sem("w_masked")
        sbo_full, sbo_read = sem("sbo_full"), sem("sbo_read")
        dz_full, dmax_ready, dexp_ready, dp_ready = (
            sem("dz_full"), sem("dmax_ready"), sem("dexp_ready"), sem("dp_ready"))
        dpT_full, dpT_read, do_full, do_read = (
            sem("dpT_full"), sem("dpT_read"), sem("do_full"), sem("do_read"))
        dsq_ready, dms_ready, drt_ready, don_ready = (
            sem("dsq_ready"), sem("dms_ready"), sem("drt_ready"), sem("don_ready"))
        doT_full, doT_read = sem("doT_full"), sem("doT_read")
        gate_ready, mixed_ready = sem("gate_ready"), sem("mixed_ready")
        mz_full, mmax_ready, mexp_ready, mp_ready = (
            sem("mz_full"), sem("mmax_ready"), sem("mexp_ready"), sem("mp_ready"))
        mpT_full, mpT_read, mo_full, mo_read = (
            sem("mpT_full"), sem("mpT_read"), sem("mo_full"), sem("mo_read"))
        logit_full, top_ready, gexp_ready, chosen_ready = (
            sem("logit_full"), sem("top_ready"), sem("gexp_ready"), sem("chosen_ready"))
        rank_full, route_ready = sem("rank_full"), sem("route_ready")
        pick_ready, pickg_ready, esel_ready = sem("pick_ready"), sem("pickg_ready"), sem("esel_ready")
        xe_full, xe_ready = sem("xe_full"), sem("xe_ready")
        glu_ready, sig_ready, gated_ready, act_ready = (
            sem("glu_ready"), sem("sig_ready"), sem("gated_ready"), sem("act_ready"))
        actT_full, actT_ready = sem("actT_full"), sem("actT_ready")
        comb_full, comb_ready, y_ready = sem("comb_full"), sem("comb_ready"), sem("y_ready")
        spread_full, added = sem("spread_full"), sem("added")

        block = ctx.enter_context(nc.Block())

        def used(n):
            return n + 1 if n < U_UPS else 2 * n - 12 if n < U_OUT else n + 3

        @block.sync
        def _(sp):
            sp.dma_start(xs[:, :, :], x[0].rearrange("(a p) d -> p a d", p=P)).then_inc(x_in, 16)
            sp.dma_start(cst[:, :], consts).then_inc(const_in, 16)
            for r, g in enumerate((norm_mix, norm_mem_q, norm_mem_kv, norm_ffn)):
                sp.dma_start(grows[8 * r:8 * r + 8, :],
                             g.rearrange("a (k p) -> (a k) p", p=P)).then_inc(small_in, 16)
            sp.dma_start(grows[32:33, :], diff_subln).then_inc(small_in, 16)
            sp.dma_start(gffn[:, :], norm_ffn.rearrange("a (u n) -> (a u) n", u=4)).then_inc(small_in, 16)
            sp.dma_start(posi[:, :], positions).then_inc(small_in, 16)
            for r, g in enumerate((lambda_q1, lambda_k1, lambda_q2, lambda_k2)):
                sp.dma_start(lamr[:, r, :], g.partition_broadcast(P).rearrange("p a d -> p (a d)")
                             ).then_inc(small_in, 16)
            sp.dma_start(brow[:, :], b_router).then_inc(small_in, 16)
            sp.dma_start(wr[:, :, :], w_router[0].rearrange("(k p) e -> p k e", p=P)).then_inc(small_in, 16)

            def by_columns(w, c0):
                return w.rearrange("(k p) n -> p k n", p=P)[:, :, c0:c0 + HALF]

            for n in range(UNITS):
                if n < U_MK:
                    src = by_columns(w_in[0], HALF * n)
                elif n < U_UPS:
                    src = by_columns(w_mem_kv[0], HALF * (n - U_MK))
                elif n < U_OUT:
                    src = (w_up_sb if n == U_UPS else w_up_diff)[0].rearrange("(k p) n -> p k n", p=P)
                elif n < U_MQ:
                    src = by_columns(w_out[0], HALF * (n - U_OUT))
                elif n < U_MO:
                    src = by_columns(w_mem_q[0], HALF * (n - U_MQ))
                else:
                    src = by_columns(w_mem_o[0], HALF * (n - U_MO))
                if n >= DENSE_SLOTS:
                    sp.wait_ge(bank1_full, used(n - DENSE_SLOTS))
                dst = ring[:, n % DENSE_SLOTS, :].rearrange("p (k n) -> p k n", k=src.shape[1])
                sp.dma_start(dst, src).then_inc(unit_in[n % DENSE_SLOTS], 16)
                if n == 1:
                    sp.dma_start(ms[:, :, :], mem[0].rearrange("(a p) d -> p a d", p=P)).then_inc(mem_in, 16)

            def load_gate_up(m, e, q):
                sp.dma_start(ring[:, MOE_SLOT[m % 8], :],
                             w_gate_up[0, e, 256 * q:256 * q + 256, :].rearrange("(p j) n -> p (j n)", j=2)
                             ).then_inc(expert_in[MOE_SLOT[m % 8]], 16)

            def load_down(m, e, q):
                sp.dma_start(ring[:, MOE_SLOT[m % 8], :],
                             w_down[0, e, HALF * q:HALF * q + HALF, :].rearrange("(p j) n -> p (j n)", j=4)
                             ).then_inc(expert_in[MOE_SLOT[m % 8]], 16)

            sp.wait_ge(bank1_full, used(U_OUT + 1))
            for q in range(4):
                load_gate_up(q, 0, q)
            late = [(bgu[32 * k:32 * k + 32, :], b_gate_up[0, :, HALF * k:HALF * k + HALF])
                    for k in range(4)]
            late += [(bdn[32 * k:32 * k + 32, :], b_down[0, :, HALF * k:HALF * k + HALF])
                     for k in range(2)]
            late += [(gfin, norm_final.rearrange("(a d) -> a d", a=1).partition_broadcast(P)
                      .rearrange("p a d -> p (a d)"))]

            def steps(b, first, last):
                for j in range(STEPS):
                    if not (last and j == STEPS - 1):
                        for q in range(4):
                            m = 24 * b + 6 * j + 4 + q
                            if first and j == 0:
                                sp.wait_ge(bank1_full, used(U_MQ + q))
                            else:
                                sp.wait_ge(expert_used, m - 7)
                            load_gate_up(6 * j + 4 + q, (STEPS * b + j + 1) % E, q)
                    if first and j == 0:
                        sp.wait_ge(mo_read, MEM_HEADS)
                        for to, of in late:
                            sp.dma_start(to, of).then_inc(late_in, 16)
                    for q in range(2):
                        m = 24 * b + 6 * j + 8 + q
                        sp.wait_ge(expert_used, m - 7)
                        load_down(6 * j + 8 + q, (STEPS * b + j) % E, q)

            steps(0, True, False)
            sp.wait_ge(route_ready, 1)
            middle = sp.value_load(middle_count[0:1, 0:1], min_val=E // STEPS - 2,
                                   max_val=ROUNDS * E // STEPS - 2)
            with sp.Fori(1, middle + 1) as b:
                steps(b, False, False)
            steps(middle + 1, False, True)
            sp.wait_ge(xn_ready, 5)
            sp.dma_start(out[0].rearrange("(a p) d -> p a d", p=P), xn[:, :, :]).then_inc(out_done, 16)
            sp.wait_ge(out_done, 16)

        def await_unit(eng, n):
            eng.wait_ge(unit_in[n % DENSE_SLOTS], 16 * (n // DENSE_SLOTS + 1))

        @block.tensor
        def _(pe):
            def turn(k, src):
                pe.wait_ge(xn_ready, k + 1)
                for c in range(KC):
                    if k > 0 and c % 2 == 0:
                        if c // 2 < 2:
                            pe.wait_ge(turned_act, 2 * (k - 1) + c // 2 + 1)
                        else:
                            pe.wait_ge(turned_dve, 2 * (k - 1) + c // 2 - 1)
                    for a in range(TT):
                        at = (c % 2) * T + a * P
                        i = pe.transpose(bank[2 + c // 2][:, at:at + P],
                                         src[:, a, c * P:c * P + P], ident)
                    if c % 2:
                        i.then_inc(turned, 1)

            uses = [0]

            def dense(n, k0, chunks, cols, lhsT, rhs, ready=None):
                u = uses[0]
                uses[0] += 1
                outs = 2 * HALF // cols
                for o in range(outs):
                    b, at = (o * cols) // HALF, (o * cols) % HALF
                    if u > 0 and at == 0:
                        pe.wait_ge((bank0_read, bank1_read)[b], u)
                    for k in range(chunks):
                        i = pe.matmul(bank[b][:, at:at + cols], lhsT(k0 + k, o), rhs(k0 + k, o),
                                      start=(k == 0), stop=(k == chunks - 1))
                    if at + cols == HALF:
                        i.then_inc((bank0_full, bank1_full)[b], 1)
                return i

            def unit(n):
                return ring[:, n % DENSE_SLOTS, :].rearrange("p (k n) -> p k n", k=KC)

            def project_T(n, h):
                await_unit(pe, n)
                w = unit(n)
                dense(n, 0, KC, T, lambda k, o: w[:, k, o * P:o * P + P], lambda k, o: h[:, k, :])

            def project(n, h):
                await_unit(pe, n)
                w = unit(n)
                dense(n, 0, KC, HALF, lambda k, o: h[:, k, o * P:o * P + P], lambda k, o: w[:, k, :])

            def sb_scores(p):
                for hh in range(2):
                    h = 2 * p + hh
                    zb = bank[2 + 2 * (p % 2) + hh]
                    rows = slice(HEAD * hh, HEAD * hh + HEAD)
                    if p >= 2:
                        pe.wait_ge(w_ready, h - 3)
                    if p == 0:
                        pe.wait_ge(turned_act, 4)
                        pe.wait_ge(turned_dve, 4)
                        pe.wait_ge(bank0_read, U_SBV + 1)
                        pe.wait_ge(bank1_read, U_SBV + 1)
                    pe.matmul(zb[:, 0:T], kT[rows, p, 0:P], qT[rows, p, :],
                              start=True, stop=False, skip_group_check=True)
                    pe.matmul(zb[:, T:T + P], kT[rows, p, P:T], qT[rows, p, P:T], start=False,
                              stop=False, skip_group_check=True).then_inc(z_full, 1)

            def sb_after(p):
                for hh in range(2):
                    h = 2 * p + hh
                    zb = bank[2 + 2 * (p % 2) + hh]
                    pe.wait_ge(l_masked, h + 1)
                    ntri, nones = cst[:, C_NTRI:C_NTRI + P], cst[:, C_NONE:C_NONE + P]
                    pe.matmul(zb[:, 0:T], ntri, sp_l[:, hh, 0:T], start=False, stop=False,
                              skip_group_check=True)
                    pe.matmul(zb[:, P:T], nones, sp_l[:, hh, T:T + P], start=False, stop=False,
                              skip_group_check=True)
                    pe.matmul(zb[:, T:T + P], ntri, sp_l[:, hh, T:T + P], start=False, stop=True,
                              skip_group_check=True).then_inc(after_full, 1)

            def sb_values(p):
                if p > 0:
                    pe.wait_ge(sbo_read, p)
                for hh in range(2):
                    h = 2 * p + hh
                    pe.wait_ge(w_masked, h + 1)
                    rows = slice(HEAD * hh, HEAD * hh + HEAD)
                    pe.matmul(bank[7][rows, 0:T], vs[:, 0, HEAD * h:HEAD * h + HEAD],
                              sp_w[:, hh, 0:T], start=True, stop=False, skip_group_check=True)
                    i = pe.matmul(bank[7][rows, P:T], vs[:, 1, HEAD * h:HEAD * h + HEAD],
                                  sp_w[:, hh, T:T + P], start=False, stop=True,
                                  skip_group_check=True)
                i.then_inc(sbo_full, 1)

            def rotate(n):
                for g in range(2):
                    if n or g:
                        pe.wait_ge(rot_read, 2 * n + g)
                    else:
                        pe.wait_ge(gain_ready, 1)
                    pe.wait_ge((bank0_read, bank1_read)[g], (U_DQ, U_DK)[n] + 1)
                    pe.matmul(bank[6][:, :], cst[:, C_ROT:C_ROT + P],
                              raw[:, n, 2 * g:2 * g + 2, :].rearrange("p c t -> p (c t)"),
                              start=True, stop=True).then_inc(rot_full, 1)

            def diff_scores(h):
                pe.wait_ge(rot_read, 4)
                if h == 0:
                    pe.wait_ge(w_ready, 6)
                else:
                    pe.wait_ge(dexp_ready, h)
                for c in range(2):
                    zb = bank[2 + c]
                    rows = slice(HEAD * c, HEAD * c + HEAD)
                    mask = cst[:, C_DMASK:C_DMASK + P]
                    pe.matmul(zb[:, 0:P], dqk[rows, 0, h, 0:P], dqk[rows, 1, h, 0:P],
                              start=True, stop=False, skip_group_check=True)
                    pe.matmul(zb[:, P:P + T], dqk[rows, 0, h, P:T], dqk[rows, 1, h, :],
                              start=False, stop=False, skip_group_check=True)
                    pe.matmul(zb[:, 0:P], ident, mask, start=False, stop=False,
                              skip_group_check=True)
                    i = pe.matmul(zb[:, T:T + P], ident, mask, start=False, stop=True,
                                  skip_group_check=True)
                i.then_inc(dz_full, 1)

            def diff_turn(h):
                pe.wait_ge(dp_ready, h + 1)
                if h == 0:
                    pe.wait_ge(w_ready, 8)
                else:
                    pe.wait_ge(dpT_read, h)
                for k in range(3):
                    i = pe.transpose(bank[4][:, k * P:k * P + P], d_p[:, k * P:k * P + P], ident)
                i.then_inc(dpT_full, 1)

            def diff_values(h):
                pe.wait_ge(dpT_read, h + 1)
                if h > 0:
                    pe.wait_ge(do_read, h)
                cols = slice(P * h, P * h + P)
                pe.matmul(bank[5][:, 0:P], d_pT[:, 0:P], vd[:, 0, cols], start=True, stop=True)
                pe.matmul(bank[5][:, P:T], d_pT[:, P:T], vd[:, 0, cols], start=True, stop=False)
                pe.matmul(bank[5][:, P:T], d_pT[:, T:T + P], vd[:, 1, cols], start=False,
                          stop=True).then_inc(do_full, 1)

            pe.wait_ge(const_in, 16)
            pe.wait_ge(small_in, 16 * 13)
            pe.transpose(bank[6][:, 0:33], grows[:, :], cst[0:33, C_ID:C_ID + 33])
            for j in range(2):
                i = pe.transpose(bank[6][:, 40 + 4 * j:44 + 4 * j], gffn[:, j:T:2],
                                 cst[0:4, C_ID:C_ID + 4])
            i.then_inc(gain_rows_T, 1)
            pe.wait_ge(pos_ready, 1)
            pe.matmul(bank[7][:, 0:T], cst[0:1, C_ONE:C_ONE + P], posf, start=True,
                      stop=True).then_inc(pos_spread, 1)
            turn(0, xn)
            pe.wait_ge(turned_act, 2)
            pe.wait_ge(turned_dve, 2)
            for n in range(U_UPS):
                if n in (U_SBQ, U_SBK, U_DQ, U_DK) or U_GSB <= n < U_MK:
                    project_T(n, hT)
                elif n in (U_SBV, U_DV):
                    project(n, hT)
                elif n < U_MV:
                    project_T(n, hmT)
                else:
                    project(n, hmT)
                if n == 0:
                    turn(1, ms)
                if n == 4:
                    rotate(0)
                if n == 5:
                    rotate(1)
                if 4 <= n < 8:
                    sb_values(n - 4)
                if 3 <= n < 7:
                    sb_after(n - 3)
                if 2 <= n < 6:
                    sb_scores(n - 2)
                if 8 <= n < 12:
                    diff_values(n - 8)
                if 7 <= n < 11:
                    diff_turn(n - 7)
                if 6 <= n < 10:
                    diff_scores(n - 6)
            pe.wait_ge(don_ready, 1)
            for h in range(DIFF_HEADS):
                for a in range(TT):
                    b = 4 + 2 * (h // 2)
                    at = (h % 2) * T + a * P
                    i = pe.transpose(bank[b][:, at:at + P], odn[:, a, P * h:P * h + P], ident)
            i.then_inc(doT_full, 1)
            for n in (U_UPS, U_UPD):
                await_unit(pe, n)
                if n == U_UPS:
                    pe.wait_ge(sbo_read, 4)
                else:
                    pe.wait_ge(doT_read, 2)
                w = ring[:, n % DENSE_SLOTS, :].rearrange("p (k n) -> p k n", k=4)
                base = 0 if n == U_UPS else 4
                for g in range(2):
                    dense(n, 0, 4, T, lambda k, o: w[:, k, (4 * g + o) * P:(4 * g + o + 1) * P],
                          lambda k, o: oT[:, base + k, :])
            pe.wait_ge(mixed_ready, 2)
            for n in (U_OUT, U_OUT + 1):
                project(n, sg[:, 0])
            turn(2, xn)
            pe.wait_ge(turned_act, 6)
            pe.wait_ge(turned_dve, 6)
            for n in (U_MQ, U_MQ + 1):
                project_T(n, hT)
            def mem_scores(h):
                for a in range(TT):
                    zb = bank[2 + 2 * (h % 2) + a]
                    if h >= 2:
                        pe.wait_ge(mexp_ready, h - 1)
                    for c in range(2):
                        i = pe.matmul(zb[:, 0:T], oT[:, 2 * h + c, a * P:a * P + P],
                                      kTm[:, 2 * h + c, :], start=(c == 0), stop=(c == 1))
                i.then_inc(mz_full, 1)

            def mem_values(h):
                pe.wait_ge(mp_ready, h + 1)
                if h > 0:
                    pe.wait_ge(mpT_read, h)
                for m in range(TT):
                    for a in range(TT):
                        i = pe.transpose(bank[6][:, m * T + a * P:m * T + a * P + P],
                                         m_p[:, h % 2, a, m * P:m * P + P], ident)
                i.then_inc(mpT_full, 1)
                pe.wait_ge(mpT_read, h + 1)
                if h > 0:
                    pe.wait_ge(mo_read, h)
                for c in range(2):
                    for m in range(TT):
                        d0 = MEM_HEAD * h + P * c
                        i = pe.matmul(bank[7][:, c * T:c * T + T], vm[:, m, d0:d0 + P],
                                      m_pT[:, h % 2, m, :], start=(m == 0), stop=(m == TT - 1))
                i.then_inc(mo_full, 1)

            pe.wait_ge(bank0_read, 22)
            pe.wait_ge(bank1_read, 22)
            mem_scores(0)
            mem_scores(1)
            for h in range(MEM_HEADS):
                mem_values(h)
                if h + 2 < MEM_HEADS:
                    mem_scores(h + 2)
            pe.wait_ge(mo_read, MEM_HEADS)
            for n in (U_MO, U_MO + 1):
                project(n, hT)
            turn(3, xn)
            pe.wait_ge(turned_act, 8)
            pe.wait_ge(turned_dve, 8)
            for a in range(TT):
                at = a * E
                pe.matmul(bank[6][:, at:at + E], cst[0:1, C_ONE:C_ONE + P], brow[:, :], start=True,
                          stop=False)
                for k in range(KC):
                    i = pe.matmul(bank[6][:, at:at + E], hT[:, k, a * P:a * P + P], wr[:, k, :],
                                  start=False, stop=(k == KC - 1))
            i.then_inc(logit_full, 1)
            pe.wait_ge(chosen_ready, 1)
            stri = cst[:, C_STRI:C_STRI + P]
            pe.matmul(bank[7][:, 0:E], stri, chosen[:, 0, :], start=True, stop=True)
            pe.matmul(bank[7][:, E:2 * E], stri, chosen[:, 1, :], start=True, stop=False)
            pe.matmul(bank[7][:, E:2 * E], ones, chosen[:, 0, :], start=False, stop=True)
            pe.matmul(bank[7][:, 2 * E:3 * E], ones, chosen[:, 0, :], start=True, stop=False)
            pe.matmul(bank[7][:, 2 * E:3 * E], ones, chosen[:, 1, :], start=False,
                      stop=True).then_inc(rank_full, 1)

            def gather(i):
                pe.wait_ge(pick_ready, i + 1)
                for c in range(KC):
                    cols = slice(256 * (c // 2) + c % 2, 256 * (c // 2) + 256, 2)
                    for a in range(TT):
                        ins = pe.matmul(bank[4][:, c * SLOTS:(c + 1) * SLOTS], xn[:, a, cols],
                                        pick[:, a, :], start=(a == 0), stop=(a == TT - 1))
                ins.then_inc(xe_full, 1)

            def spread(i, a, buf):
                for h in range(2):
                    rows = slice(SLOTS * h, SLOTS * h + SLOTS)
                    ins = pe.matmul(bank[6 + h][:, :], comb[rows, buf, a * P:a * P + P],
                                    yb[rows, :], start=True, stop=True)
                ins.then_inc(spread_full, 1)

            def step(b, j, i, prev, cur, nxt, nxt2):
                if cur:
                    pe.wait_ge(act_ready, i + 1)
                    if prev:
                        pe.wait_ge(actT_ready, i)
                    for r in range(4):
                        ins = pe.transpose(bank[3][:, r * P:r * P + P], act[:, r:HALF:4], ident)
                    ins.then_inc(actT_full, 1)
                    pe.wait_ge(pickg_ready, i + 1)
                    if prev:
                        pe.wait_ge(comb_ready, i)
                    for a in range(TT):
                        ins = pe.transpose(bank[5][:, a * P:a * P + P], pickg[:, a, :], ident)
                    ins.then_inc(comb_full, 1)
                if prev:
                    pe.wait_ge(y_ready, i)
                    pe.wait_ge(comb_ready, i)
                    if prev == "second":
                        pe.wait_ge(added, 2 * i - 2)
                    spread(i - 1, 0, (j - 1) % 2)
                if nxt:
                    pe.wait_ge(esel_ready, i + 2)
                    for k in range(4):
                        pe.matmul(bank[k // 2][SLOTS * (k % 2):SLOTS * (k % 2) + SLOTS, :],
                                  esel[:, (j + 1) % 4, k:k + 1].broadcast_to([P, SLOTS]), bgu,
                                  start=True, stop=False)
                    pe.wait_ge(xe_ready, i + 2)
                    for q in range(4):
                        m = 6 * j + 4 + q if j >= 0 else q
                        pe.wait_ge(expert_in[MOE_SLOT[m % 8]], 48 * b + 16 * (m // 8 + 1))
                        w = ring[:, MOE_SLOT[m % 8], :].rearrange("p (j n) -> p j n", j=2)
                        for r in range(2):
                            for k in range(4):
                                ins = pe.matmul(
                                    bank[k // 2][SLOTS * (k % 2):SLOTS * (k % 2) + SLOTS, :],
                                    xe[:, (j + 1) % 2, 2 * q + r, :], w[:, r, HALF * k:HALF * k + HALF],
                                    start=False, stop=(q == 3 and r == 1))
                        ins.then_inc(expert_used, 1)
                        if q == 1 and prev:
                            pe.wait_ge(added, 2 * i - 1)
                            spread(i - 1, 1, (j - 1) % 2)
                elif prev:
                    pe.wait_ge(added, 2 * i - 1)
                    spread(i - 1, 1, (j - 1) % 2)
                if nxt2:
                    pe.wait_ge(xe_ready, i + 2)
                    gather(i + 2)
                if cur:
                    if prev:
                        pe.wait_ge(y_ready, i)
                    for h in range(2):
                        pe.matmul(bank[2][SLOTS * h:SLOTS * h + SLOTS, :],
                                  esel[:, j % 4, h:h + 1].broadcast_to([P, SLOTS]), bdn,
                                  start=True, stop=False)
                    pe.wait_ge(actT_ready, i + 1)
                    for q in range(2):
                        m = 6 * j + 8 + q
                        pe.wait_ge(expert_in[MOE_SLOT[m % 8]], 48 * b + 16 * (m // 8 + 1))
                        w = ring[:, MOE_SLOT[m % 8], :].rearrange("p (j n) -> p j n", j=4)
                        for r in range(4):
                            for h in range(2):
                                ins = pe.matmul(bank[2][SLOTS * h:SLOTS * h + SLOTS, :],
                                                actT[:, P * r + SLOTS * q:P * r + SLOTS * q + SLOTS],
                                                w[:, r, HALF * h:HALF * h + HALF],
                                                start=False, stop=(q == 1 and r == 3))
                        ins.then_inc(expert_used, 1)

            pe.wait_ge(late_in, 16 * 7)
            gather(0)
            step(0, -1, -1, None, False, True, True)
            for j in range(STEPS):
                step(0, j, j, (None, "first", "second", "second")[j], True, True, True)
            middle = pe.value_load(middle_count[0:1, 0:1], min_val=E // STEPS - 2,
                                   max_val=ROUNDS * E // STEPS - 2)
            with pe.Fori(1, middle + 1) as b:
                for j in range(STEPS):
                    step(b, j, STEPS * b + j, "second", True, True, True)
            b = middle + 1
            for j in range(STEPS):
                step(b, j, STEPS * b + j, "second", True, j < STEPS - 1, j < STEPS - 2)
            n = STEPS * b + STEPS
            pe.wait_ge(y_ready, n)
            for a in range(TT):
                pe.wait_ge(added, 2 * n - 2 + a)
                spread(n - 1, a, 1)

        @block.scalar
        def _(act_e):
            steps_done = [0]

            def link(ins):
                steps_done[0] += 1
                ins.then_inc(act_step, 1)
                act_e.wait_ge(act_step, steps_done[0])

            def norm(k, src, dst):
                for a in range(TT):
                    i = act_e.activation(dst[:, a, :], src[:, a, :], ACT.Square,
                                         accum_out=st[:, 4 * k + a:4 * k + a + 1])
                i.then_inc(sq_ready, 1)
                act_e.wait_ge(ms_ready, k + 1)
                act_e.activation(st[:, 4 * k + 2:4 * k + 4], st[:, 4 * k:4 * k + 2],
                                 ACT.Sqrt).then_inc(rt_ready, 1)

            def turned_to(dst, k, g0):
                for c in range(4):
                    if c % 2 == 0:
                        act_e.wait_ge(turned, 4 * k + c // 2 + 1)
                    i = act_e.activation(dst[:, c, :], bank[2 + c // 2][:, (c % 2) * T:(c % 2) * T + T],
                                         ACT.Copy, scale=gT[:, g0 + c:g0 + c + 1])
                    if c % 2:
                        i.then_inc(turned_act, 1)

            def from_bank0(u, dst, scale=1.0):
                act_e.wait_ge(bank0_full, u + 1)
                act_e.activation(dst, bank[0][:, :], ACT.Copy, scale=scale).then_inc(bank0_read, 1)

            def mem_turned(h):
                act_e.wait_ge(mpT_full, h + 1)
                if h >= 2:
                    act_e.wait_ge(mo_full, h - 1)
                act_e.activation(m_pT[:, h % 2].rearrange("p m t -> p (m t)"), bank[6][:, :],
                                 ACT.Copy).then_inc(mpT_read, 1)

            act_e.wait_ge(x_in, 16)
            norm(0, xs, xn)
            act_e.wait_ge(gain_ready, 1)
            turned_to(hT, 0, 0)
            act_e.wait_ge(mem_in, 16)
            for a in range(TT):
                i = act_e.activation(kTm[:, 4 * a:4 * a + 4, :].rearrange("p k t -> p (k t)"),
                                     ms[:, a, :], ACT.Square, accum_out=st[:, 4 + a:5 + a])
            i.then_inc(sq_ready, 1)
            act_e.wait_ge(ms_ready, 2)
            act_e.activation(st[:, 6:8], st[:, 4:6], ACT.Sqrt).then_inc(rt_ready, 1)
            act_e.wait_ge(ang_ready, 1)
            act_e.activation(scr[:, 2304:2816], ang, ACT.Sin).then_inc(rope_ready, 1)
            act_e.wait_ge(lam_dots, 1)
            act_e.activation(st[:, 82:84], st[:, 80:82], ACT.Exp).then_inc(lam_exp, 1)

            def fold(ap):
                return ap.rearrange("p c t -> p (c t)")

            for n in range(U_UPS):
                if n == U_SBQ:
                    from_bank0(n, fold(qT[:, 0:2, :]), HEAD ** -0.5)
                elif n == U_SBK:
                    from_bank0(n, fold(kT[:, 0:2, :]))
                elif n == U_SBV:
                    from_bank0(n, vs[:, 0, :])
                elif n == U_DQ:
                    from_bank0(n, fold(raw[:, 0, 0:2, :]), HEAD ** -0.5)
                elif n == U_DK:
                    from_bank0(n, fold(raw[:, 1, 0:2, :]))
                elif n == U_DV:
                    from_bank0(n, vd[:, 0, :])
                elif n < U_MK:
                    g = n - U_GSB
                    from_bank0(n, fold(sg[:, g // 2, 4 * (g % 2):4 * (g % 2) + 2, :]))
                elif n < U_MV:
                    if n == U_MK:
                        act_e.wait_ge(xn_ready, 2)
                    from_bank0(n, fold(kTm[:, 4 * (n - U_MK):4 * (n - U_MK) + 2, :]))
                else:
                    from_bank0(n, vm[:, 0, HALF * (n - U_MV):HALF * (n - U_MV) + HALF])
                if n == 0:
                    turned_to(hmT, 1, 16)
                if 3 <= n < 7:
                    for hh in range(2):
                        h = 2 * (n - 3) + hh
                        act_e.wait_ge(after_full, h + 1)
                        if n > 3:
                            act_e.wait_ge(sbo_full, n - 3)
                        act_e.activation(sp_w[:, hh, :], bank[2 + 2 * ((n - 3) % 2) + hh][:, 0:384],
                                         ACT.Exp).then_inc(w_ready, 1)
                if 2 <= n < 6:
                    for hh in range(2):
                        h = 2 * (n - 2) + hh
                        act_e.wait_ge(z_full, h + 1)
                        if n > 2:
                            act_e.wait_ge(l_ready, h - 1)
                        t = sp_t[:, hh, :]
                        link(act_e.activation(t, bank[2 + 2 * ((n - 2) % 2) + hh][:, 0:384], ACT.Abs))
                        link(act_e.activation(t, t, ACT.Exp, scale=-1.0))
                        act_e.activation(t, t, ACT.Ln, bias=one).then_inc(soft_ready, 1)
                if 7 <= n < 11:
                    act_e.wait_ge(dpT_full, n - 6)
                    if n > 7:
                        act_e.wait_ge(do_full, n - 7)
                    act_e.activation(d_pT, bank[4][:, 0:384], ACT.Copy).then_inc(dpT_read, 1)
                if 6 <= n < 10:
                    h = n - 6
                    act_e.wait_ge(dmax_ready, h + 1)
                    for c in range(2):
                        for a in range(TT):
                            k = 24 + 2 * c + a
                            cols = slice(0, P) if a == 0 else slice(P, P + T)
                            i = act_e.activation(d_e[:, c, cols], bank[2 + c][:, cols], ACT.Exp,
                                                 bias=st[:, k:k + 1], accum_out=st[:, k + 4:k + 5])
                    i.then_inc(dexp_ready, 1)
                if 8 <= n < 12:
                    h = n - 8
                    act_e.wait_ge(do_read, h + 1)
                    for a in range(TT):
                        i = act_e.activation(odn[:, a, P * h:P * h + P], od[:, a, P * h:P * h + P],
                                             ACT.Square, accum_out=st[:, 40 + 2 * h + a:41 + 2 * h + a])
                    i.then_inc(dsq_ready, 1)
            act_e.wait_ge(dms_ready, 1)
            act_e.activation(st[:, 48:56], st[:, 40:48], ACT.Sqrt).then_inc(drt_ready, 1)
            act_e.wait_ge(bank1_read, U_MK)
            for g in range(2):
                i = act_e.activation(sg[:, g], sg[:, g], ACT.Sigmoid)
            i.then_inc(gate_ready, 1)
            act_e.wait_ge(doT_full, 1)
            act_e.activation(fold(oT[:, 4:6, :]), bank[4][:, :], ACT.Copy,
                             scale=st[:, 88:89]).then_inc(doT_read, 1)
            act_e.wait_ge(bank0_read, 20)
            act_e.wait_ge(bank1_read, 20)
            norm(2, xs, xn)
            turned_to(hT, 2, 8)
            for n in range(2):
                from_bank0(20 + n, fold(oT[:, 4 * n:4 * n + 2, :]), MEM_HEAD ** -0.5)
            for h in range(MEM_HEADS):
                act_e.wait_ge(mmax_ready, h + 1)
                if h >= 2:
                    act_e.wait_ge(mpT_full, h - 1)
                for a in range(TT):
                    k = 60 + 4 * (h % 2) + a
                    i = act_e.activation(m_p[:, h % 2, a, :], bank[2 + 2 * (h % 2) + a][:, 0:T], ACT.Exp,
                                         bias=st[:, k:k + 1], accum_out=st[:, k + 2:k + 3])
                i.then_inc(mexp_ready, 1)
                if h >= 1:
                    mem_turned(h - 1)
            mem_turned(MEM_HEADS - 1)
            act_e.wait_ge(bank0_read, 24)
            act_e.wait_ge(bank1_read, 24)
            norm(3, xs, xn)
            turned_to(hT, 3, 24)
            act_e.wait_ge(top_ready, 1)
            for a in range(TT):
                i = act_e.activation(tope[:, a, :], topv[:, a, 0:TOP_K], ACT.Exp,
                                     bias=few[:, a:a + 1], accum_out=few[:, 2 + a:3 + a])
            i.then_inc(gexp_ready, 1)

            def step(b, j, i, prev, cur, nxt):
                if cur:
                    act_e.wait_ge(actT_full, i + 1)
                    if prev:
                        act_e.wait_ge(expert_used, 6 * i + 4)
                    act_e.activation(actT, bank[3][:, :], ACT.Copy).then_inc(actT_ready, 1)
                    act_e.wait_ge(comb_full, i + 1)
                    act_e.activation(comb[:, j % 2, :], bank[5][:, 0:T], ACT.Copy).then_inc(comb_ready, 1)
                if nxt:
                    act_e.wait_ge(glu_ready, i + 2)
                    act_e.activation(sig, glu, ACT.Sigmoid, scale=ALPHA).then_inc(sig_ready, 1)
                if cur:
                    act_e.wait_ge(expert_used, 6 * i + (10 if nxt else 6))
                    if prev:
                        act_e.wait_ge(spread_full, 2 * i)
                    act_e.activation(yb, bank[2][:, :], ACT.Copy).then_inc(y_ready, 1)

            step(0, -1, -1, False, False, True)
            for j in range(STEPS):
                step(0, j, j, j > 0, True, True)
            act_e.wait_ge(route_ready, 1)
            middle = act_e.value_load(middle_count[0:1, 0:1], min_val=E // STEPS - 2,
                                   max_val=ROUNDS * E // STEPS - 2)
            with act_e.Fori(1, middle + 1) as b:
                for j in range(STEPS):
                    step(b, j, STEPS * b + j, True, True, True)
            b = middle + 1
            for j in range(STEPS):
                step(b, j, STEPS * b + j, True, True, j < STEPS - 1)
            act_e.wait_ge(added, 2 * STEPS * b + 2 * STEPS)
            norm(4, xs, xn)

        @block.gpsimd
        def _(pool):
            def keep_past(t):
                v = t.rearrange("p (b n) -> p b n", b=3)[:, 0:3:2, :]
                return pool.affine_select(out=v, in_=v, pattern=[[0, 2], [1, P]],
                                          compare_op=ALU.is_gt, fill=0.0, base=0,
                                          channel_multiplier=-1)

            for n in range(2, 7):
                if n >= 3:
                    for hh in range(2):
                        pool.wait_ge(w_ready, 2 * (n - 3) + hh + 1)
                        keep_past(sp_w[:, hh, :]).then_inc(w_masked, 1)
                if n < 6:
                    for hh in range(2):
                        pool.wait_ge(l_ready, 2 * (n - 2) + hh + 1)
                        keep_past(sp_l[:, hh, :]).then_inc(l_masked, 1)

        @block.vector
        def _(dve):
            steps_done = [0]

            def link(ins):
                steps_done[0] += 1
                ins.then_inc(dve_step, 1)
                dve.wait_ge(dve_step, steps_done[0])

            def fold(ap):
                return ap.rearrange("p c t -> p (c t)")

            def mean_square(k):
                dve.wait_ge(sq_ready, k + 1)
                dve.tensor_scalar(st[:, 4 * k:4 * k + 2], st[:, 4 * k:4 * k + 2], 1.0 / D, EPS,
                                  ALU.mult, ALU.add).then_inc(ms_ready, 1)
                dve.wait_ge(rt_ready, k + 1)
                link(dve.reciprocal(st[:, 4 * k + 2:4 * k + 4], st[:, 4 * k + 2:4 * k + 4]))

            def norm(k, src, dst):
                mean_square(k)
                for a in range(TT):
                    i = dve.tensor_scalar(dst[:, a, :], src[:, a, :], st[:, 4 * k + 2 + a:4 * k + 3 + a],
                                          None, ALU.mult)
                i.then_inc(xn_ready, 1)

            def turned_to(dst, k, g0):
                for c in range(4, KC):
                    if c % 2 == 0:
                        dve.wait_ge(turned, 4 * k + c // 2 + 1)
                    i = dve.tensor_scalar(dst[:, c, :], bank[2 + c // 2][:, (c % 2) * T:(c % 2) * T + T],
                                          gT[:, g0 + c:g0 + c + 1], None, ALU.mult)
                    if c % 2:
                        i.then_inc(turned_dve, 1)

            def from_bank1(u, dst, scale=None):
                dve.wait_ge(bank1_full, u + 1)
                if scale is None:
                    dve.tensor_copy(dst, bank[1][:, :]).then_inc(bank1_read, 1)
                else:
                    dve.tensor_scalar(dst, bank[1][:, :], scale, None, ALU.mult).then_inc(bank1_read, 1)

            dve.wait_ge(small_in, 16 * 13)
            dve.tensor_copy(posf, posi[:, :]).then_inc(pos_ready, 1)
            for r in range(2):
                i = dve.tensor_tensor_reduce(scr[:, 4608 + HEAD * r:4608 + HEAD * r + HEAD],
                                             lamr[:, 2 * r, :], lamr[:, 2 * r + 1, :], 1.0, 0.0,
                                             ALU.mult, ALU.add, st[:, 80 + r:81 + r])
            i.then_inc(lam_dots, 1)
            dve.wait_ge(gain_rows_T, 1)
            dve.tensor_copy(gT[:, :], bank[6][:, 0:33])
            dve.tensor_copy(gperm[:, :].rearrange("p (u j) -> p j u", j=2),
                            bank[6][:, 40:48].rearrange("p (j u) -> p j u", j=2)).then_inc(gain_ready, 1)
            norm(0, xs, xn)
            dve.wait_ge(gain_ready, 1)
            dve.tensor_scalar(st[:, 88:89], gT[:, 32:33], 1.0 - LAMBDA_INIT, None, ALU.mult)
            turned_to(hT, 0, 0)
            dve.wait_ge(const_in, 16)
            dve.wait_ge(pos_spread, 1)
            link(dve.tensor_scalar(ang[:, T:2 * T], bank[7][:, 0:T], cst[:, C_INV:C_INV + 1], None,
                                   ALU.mult))
            link(dve.tensor_scalar(angn[:, T:2 * T], ang[:, T:2 * T], 1.0 / (2 * math.pi), ROUNDER,
                                   ALU.mult, ALU.add))
            link(dve.tensor_scalar(angn[:, 0:T], ang[:, T:2 * T], 1.0 / (2 * math.pi), 0.25,
                                   ALU.mult, ALU.add))
            link(dve.tensor_scalar(angn[:, 0:T], angn[:, 0:T], ROUNDER, None, ALU.add))
            link(dve.tensor_scalar(angn[:, :], angn[:, :], ROUNDER, None, ALU.subtract))
            link(dve.scalar_tensor_tensor(ang[:, 0:T], angn[:, 0:T], -TWO_PI_A, ang[:, T:2 * T],
                                          ALU.mult, ALU.add))
            link(dve.scalar_tensor_tensor(ang[:, T:2 * T], angn[:, T:2 * T], -TWO_PI_A,
                                          ang[:, T:2 * T], ALU.mult, ALU.add))
            for part in (TWO_PI_B, TWO_PI_C):
                link(dve.scalar_tensor_tensor(ang[:, :], angn[:, :], -part, ang[:, :], ALU.mult,
                                              ALU.add))
            link(dve.tensor_scalar(ang[:, 0:T], ang[:, 0:T], math.pi / 2, None, ALU.add))
            dve.tensor_scalar(ang[:, :], ang[:, :], 3.1415925, -3.1415925, ALU.min,
                              ALU.max).then_inc(ang_ready, 1)
            norm(1, ms, ms)
            dve.wait_ge(lam_exp, 1)
            link(dve.tensor_tensor(st[:, 84:85], st[:, 83:84], st[:, 82:83], ALU.subtract))
            dve.tensor_scalar(st[:, 84:85], st[:, 84:85], LAMBDA_INIT, None,
                              ALU.subtract).then_inc(lam_ready, 1)

            for n in range(U_UPS):
                if n == U_SBQ:
                    from_bank1(n, fold(qT[:, 2:4, :]), HEAD ** -0.5)
                elif n == U_SBK:
                    from_bank1(n, fold(kT[:, 2:4, :]))
                elif n == U_SBV:
                    from_bank1(n, vs[:, 1, :])
                elif n == U_DQ:
                    from_bank1(n, fold(raw[:, 0, 2:4, :]), HEAD ** -0.5)
                elif n == U_DK:
                    from_bank1(n, fold(raw[:, 1, 2:4, :]))
                elif n == U_DV:
                    from_bank1(n, vd[:, 1, :])
                elif n < U_MK:
                    g = n - U_GSB
                    from_bank1(n, fold(sg[:, g // 2, 4 * (g % 2) + 2:4 * (g % 2) + 4, :]))
                elif n < U_MV:
                    from_bank1(n, fold(kTm[:, 4 * (n - U_MK) + 2:4 * (n - U_MK) + 4, :]))
                else:
                    from_bank1(n, vm[:, 1, HALF * (n - U_MV):HALF * (n - U_MV) + HALF])
                if n == 0:
                    turned_to(hmT, 1, 16)
                if n in (4, 5):
                    if n == 4:
                        dve.wait_ge(rope_ready, 1)
                        dve.wait_ge(bank0_read, U_DQ + 1)
                    else:
                        dve.wait_ge(bank0_read, U_DK + 1)
                    cos2 = cosT.unsqueeze(1).to_broadcast([P, 2, T])
                    sin2 = sinT.unsqueeze(1).to_broadcast([P, 2, T])
                    for g in range(2):
                        rot = bank[6][:, :].rearrange("p (c t) -> p c t", c=2)
                        dve.tensor_tensor(rtmp[:, 0], raw[:, n - 4, 2 * g:2 * g + 2, :], cos2, ALU.mult)
                        dve.wait_ge(rot_full, 2 * (n - 4) + g + 1)
                        link(dve.tensor_tensor(rtmp[:, 1], rot, sin2, ALU.mult))
                        dve.tensor_tensor(dqk[:, n - 4, 2 * g:2 * g + 2, :], rtmp[:, 0], rtmp[:, 1],
                                          ALU.add).then_inc(rot_read, 1)
                        dve.wait_ge(rot_read, 2 * (n - 4) + g + 1)
                if 4 <= n < 8:
                    p = n - 4
                    dve.wait_ge(sbo_full, p + 1)
                    dve.tensor_copy(oT[:, p, :], bank[7][:, 0:T]).then_inc(sbo_read, 1)
                if 2 <= n < 6:
                    for hh in range(2):
                        h = 2 * (n - 2) + hh
                        dve.wait_ge(soft_ready, h + 1)
                        if n > 2:
                            dve.wait_ge(after_full, h - 1)
                        dve.scalar_tensor_tensor(sp_l[:, hh, :], bank[2 + 2 * ((n - 2) % 2) + hh][:, 0:384],
                                                 0.0, sp_t[:, hh, :], ALU.max, ALU.add).then_inc(l_ready, 1)
                if 8 <= n < 12:
                    h = n - 8
                    dve.wait_ge(do_full, h + 1)
                    dve.tensor_copy(od[:, :, P * h:P * h + P],
                                    bank[5][:, 0:T].rearrange("p (a d) -> p a d", a=TT)).then_inc(do_read, 1)
                if 6 <= n < 10:
                    h = n - 6
                    dve.wait_ge(dz_full, h + 1)
                    if h > 0:
                        dve.wait_ge(dexp_ready, h)
                    for c in range(2):
                        for a in range(TT):
                            k = 24 + 2 * c + a
                            cols = slice(0, P) if a == 0 else slice(P, P + T)
                            i = dve.tensor_reduce(st[:, k:k + 1], bank[2 + c][:, cols], AX, ALU.max,
                                                  negate=True)
                    i.then_inc(dmax_ready, 1)
                    dve.wait_ge(dexp_ready, h + 1)
                    link(dve.reciprocal(st[:, 32:36], st[:, 28:32]))
                    link(dve.tensor_scalar(st[:, 34:36], st[:, 34:36], st[:, 84:85], None, ALU.mult))
                    if h > 0:
                        dve.wait_ge(dpT_full, h)
                    for a in range(TT):
                        cols = slice(0, P) if a == 0 else slice(P, P + T)
                        link(dve.tensor_scalar(d_e[:, 0, cols], d_e[:, 0, cols], st[:, 32 + a:33 + a],
                                               None, ALU.mult))
                        i = dve.scalar_tensor_tensor(d_p[:, cols], d_e[:, 1, cols],
                                                     st[:, 34 + a:35 + a], d_e[:, 0, cols], ALU.mult,
                                                     ALU.add)
                    i.then_inc(dp_ready, 1)
                if n == 12:
                    dve.wait_ge(dsq_ready, DIFF_HEADS)
                    dve.tensor_scalar(st[:, 40:48], st[:, 40:48], 1.0 / P, EPS, ALU.mult,
                                      ALU.add).then_inc(dms_ready, 1)
                    dve.wait_ge(drt_ready, 1)
                    link(dve.reciprocal(st[:, 48:56], st[:, 48:56]))
                    for h in range(DIFF_HEADS):
                        for a in range(TT):
                            i = dve.tensor_scalar(odn[:, a, P * h:P * h + P], od[:, a, P * h:P * h + P],
                                                  st[:, 48 + 2 * h + a:49 + 2 * h + a], None, ALU.mult)
                    i.then_inc(don_ready, 1)
            dve.wait_ge(doT_full, 1)
            dve.tensor_scalar(fold(oT[:, 6:8, :]), bank[6][:, :], st[:, 88:89], None,
                              ALU.mult).then_inc(doT_read, 1)
            dve.wait_ge(gate_ready, 1)
            for u in range(14, 18):
                n, g = (u - 14) // 2, (u - 14) % 2
                for b in range(2):
                    part = fold(sg[:, n, 4 * g + 2 * b:4 * g + 2 * b + 2, :])
                    dve.wait_ge((bank0_full, bank1_full)[b], u + 1)
                    dve.tensor_tensor(part, bank[b][:, :], part, ALU.mult).then_inc(
                        (bank0_read, bank1_read)[b], 1)
            for g in range(2):
                dve.wait_ge(bank1_read, 17 + g)
                dve.wait_ge(bank0_read, 17 + g)
                dve.tensor_tensor(fold(sg[:, 0, 4 * g:4 * g + 4, :]), fold(sg[:, 0, 4 * g:4 * g + 4, :]),
                                  fold(sg[:, 1, 4 * g:4 * g + 4, :]), ALU.add).then_inc(mixed_ready, 1)

            def add_to_x(u0):
                for g in range(2):
                    for b in range(2):
                        dve.wait_ge((bank0_full, bank1_full)[b], u0 + g + 1)
                        part = xs[:, b, HALF * g:HALF * g + HALF]
                        i = dve.tensor_tensor(part, bank[b][:, :], part, ALU.add)
                        i.then_inc((bank0_read, bank1_read)[b], 1)
                dve.wait_ge(bank0_read, u0 + 2)
                dve.wait_ge(bank1_read, u0 + 2)

            add_to_x(18)
            norm(2, xs, xn)
            turned_to(hT, 2, 8)
            for n in range(2):
                from_bank1(20 + n, fold(oT[:, 4 * n + 2:4 * n + 4, :]), MEM_HEAD ** -0.5)

            def mem_out(h):
                dve.wait_ge(mo_full, h + 1)
                dve.tensor_copy(fold(hT[:, 2 * h:2 * h + 2, :]), bank[7][:, :]).then_inc(mo_read, 1)

            for h in range(MEM_HEADS):
                dve.wait_ge(mz_full, h + 1)
                k = 60 + 4 * (h % 2)
                for a in range(TT):
                    i = dve.tensor_reduce(st[:, k + a:k + a + 1], bank[2 + 2 * (h % 2) + a][:, 0:T], AX,
                                          ALU.max, negate=True)
                i.then_inc(mmax_ready, 1)
                dve.wait_ge(mexp_ready, h + 1)
                link(dve.reciprocal(st[:, 70:72], st[:, k + 2:k + 4]))
                for a in range(TT):
                    i = dve.tensor_scalar(m_p[:, h % 2, a, :], m_p[:, h % 2, a, :],
                                          st[:, 70 + a:71 + a], None, ALU.mult)
                i.then_inc(mp_ready, 1)
                if h >= 1:
                    mem_out(h - 1)
            mem_out(MEM_HEADS - 1)
            add_to_x(22)
            norm(3, xs, xn)
            turned_to(hT, 3, 24)

            dve.wait_ge(logit_full, 1)
            link(dve.tensor_copy(fold(lg), bank[6][:, 0:2 * E]))
            for a in range(TT):
                i = dve.max(topv[:, a, :], lg[:, a, :])
            link(i)
            link(dve.tensor_scalar(few[:, 0:2], topv[:, :, 0], -1.0, None, ALU.mult))
            for a in range(TT):
                i = dve.max_index(topi[:, a, :], topv[:, a, :], lg[:, a, :])
            i.then_inc(top_ready, 1)
            dve.wait_ge(top_ready, 1)
            link(dve.tensor_copy(topf, topi[:, :, :]))
            iota = cst[:, C_IOTA:C_IOTA + E]
            for a in range(TT):
                link(dve.tensor_scalar(chosen[:, a, :], iota, topf[:, a, 0:1], None, ALU.is_equal))
                for k in range(1, TOP_K):
                    i = dve.scalar_tensor_tensor(chosen[:, a, :], iota, topf[:, a, k:k + 1],
                                                 chosen[:, a, :], ALU.is_equal, ALU.add)
                    if k < TOP_K - 1:
                        link(i)
                if a < TT - 1:
                    link(i)
            i.then_inc(chosen_ready, 1)
            dve.wait_ge(gexp_ready, 1)
            link(dve.reciprocal(few[:, 4:6], few[:, 2:4]))
            for a in range(TT):
                link(dve.tensor_scalar(tope[:, a, :], tope[:, a, :], few[:, 4 + a:5 + a], None, ALU.mult))
                link(dve.tensor_scalar(gates[:, a, :], iota, topf[:, a, 0:1], tope[:, a, 0:1],
                                       ALU.is_equal, ALU.mult))
                for k in range(1, TOP_K):
                    link(dve.tensor_scalar(hotg, iota, topf[:, a, k:k + 1], tope[:, a, k:k + 1],
                                           ALU.is_equal, ALU.mult))
                    link(dve.tensor_tensor(gates[:, a, :], gates[:, a, :], hotg, ALU.add))
                link(dve.tensor_copy(gate_of[:, a, :].rearrange("p (r e) -> p r e", e=E),
                                     gates[:, a, :].unsqueeze(1).to_broadcast([P, ROUNDS, E])))
            dve.wait_ge(rank_full, 1)
            for a in range(TT):
                link(dve.scalar_tensor_tensor(hot, bank[7][:, a * E:a * E + E], NOT_CHOSEN,
                                              chosen[:, a, :], ALU.add, ALU.mult))
                link(dve.scalar_tensor_tensor(
                    slot_of[:, a, :].rearrange("p (r e) -> p r e", e=E),
                    hot.unsqueeze(1).to_broadcast([P, ROUNDS, E]), NOT_CHOSEN,
                    cst[:, C_R64:C_R64 + ROUNDS * E].rearrange("p (r e) -> p r e", e=E),
                    ALU.subtract, ALU.subtract))
            link(dve.tensor_reduce(few[:, 6:7], bank[7][:, 2 * E:3 * E], AX, ALU.max))
            for r in range(1, ROUNDS):
                i = dve.tensor_scalar(few[:, 6 + r:7 + r], few[:, 6:7], float(SLOTS * r),
                                      float(E // STEPS), ALU.is_gt, ALU.mult)
            link(i)
            link(dve.tensor_reduce(few[:, 10:11], few[:, 7:10], AX, ALU.add))
            dve.tensor_scalar(middle_count[0:1, 0:1], few[0:1, 10:11], float(E // STEPS - 2), None,
                              ALU.add).then_inc(route_ready, 1)

            def col(ap, i):
                return ap[:, bass.ds(i, 1)]

            def picks(i, j):
                for a in range(TT):
                    ins = dve.tensor_scalar(pick[:, a, :], cst[:, C_SLOT:C_SLOT + SLOTS],
                                            col(slot_of[:, a, :], i), None, ALU.is_equal)
                ins.then_inc(pick_ready, 1)
                dve.tensor_scalar(esel[:, j % 4, :], cst[:, C_BLK:C_BLK + 4],
                                  col(cst[:, C_EIDX:C_EIDX + ROUNDS * E], i), None,
                                  ALU.is_equal).then_inc(esel_ready, 1)

            def gathered(i, j):
                dve.wait_ge(xe_full, i + 1)
                dve.tensor_tensor(xe[:, j % 2], bank[4][:, :].rearrange("p (k s) -> p k s", k=KC),
                                  gperm[:, :].unsqueeze(2).to_broadcast([P, KC, SLOTS]),
                                  ALU.mult).then_inc(xe_ready, 1)

            def add_spread(a):
                for h in range(2):
                    part = xs[:, a, HALF * h:HALF * h + HALF]
                    ins = dve.tensor_tensor(part, bank[6 + h][:, :], part, ALU.add)
                ins.then_inc(added, 1)

            def step(b, j, i, prev, cur, nxt, nxt2):
                if prev:
                    dve.wait_ge(spread_full, 2 * i - 1)
                    add_spread(0)
                if nxt2:
                    picks(i + 2, j + 2)
                if nxt:
                    if cur:
                        dve.wait_ge(comb_full, i + 1)
                    for a in range(TT):
                        ins = dve.tensor_scalar(pickg[:, a, :], cst[:, C_SLOT:C_SLOT + P],
                                                col(slot_of[:, a, :], i + 1),
                                                col(gate_of[:, a, :], i + 1), ALU.is_equal, ALU.mult)
                    ins.then_inc(pickg_ready, 1)
                if prev:
                    dve.wait_ge(spread_full, 2 * i)
                    add_spread(1)
                if nxt:
                    dve.wait_ge(expert_used, 6 * i + 8 if cur else 4)
                    dve.tensor_scalar(glu, bank[0][:, :], LIMIT, None, ALU.min).then_inc(glu_ready, 1)
                    dve.tensor_scalar(lin, bank[1][:, :], LIMIT, -LIMIT, ALU.min, ALU.max)
                    if nxt2:
                        gathered(i + 2, j + 2)
                    dve.wait_ge(sig_ready, i + 2)
                    dve.tensor_tensor(glu, glu, sig, ALU.mult).then_inc(gated_ready, 1)
                    dve.wait_ge(gated_ready, i + 2)
                    dve.scalar_tensor_tensor(act, lin, 1.0, glu, ALU.add, ALU.mult).then_inc(act_ready, 1)

            dve.wait_ge(route_ready, 1)
            picks(0, 0)
            gathered(0, 0)
            step(0, -1, -1, False, False, True, True)
            for j in range(STEPS):
                step(0, j, j, j > 0, True, True, True)
            middle = dve.value_load(middle_count[0:1, 0:1], min_val=E // STEPS - 2,
                                   max_val=ROUNDS * E // STEPS - 2)
            with dve.Fori(1, middle + 1) as b:
                for j in range(STEPS):
                    step(b, j, STEPS * b + j, True, True, True, True)
            b = middle + 1
            for j in range(STEPS):
                step(b, j, STEPS * b + j, True, True, j < STEPS - 1, j < STEPS - 2)
            n = STEPS * b + STEPS
            for a in range(TT):
                dve.wait_ge(spread_full, 2 * n - 1 + a)
                add_spread(a)
            mean_square(4)
            dve.wait_ge(late_in, 16 * 7)
            for a in range(TT):
                i = dve.scalar_tensor_tensor(xn[:, a, :], xs[:, a, :], st[:, 18 + a:19 + a], gfin,
                                             ALU.mult, ALU.mult)
            i.then_inc(xn_ready, 2)


_INS = ["x", "mem", "positions", "norm_mix", "w_in", "lambda_q1", "lambda_k1", "lambda_q2",
        "lambda_k2", "diff_subln", "w_up_sb", "w_up_diff", "w_out", "norm_mem_q", "norm_mem_kv",
        "w_mem_q", "w_mem_kv", "w_mem_o", "norm_ffn", "w_router", "b_router", "w_gate_up",
        "b_gate_up", "w_down", "b_down", "norm_final"]


def kernel(**inputs):
    import concourse.bacc as bacc
    from concourse.bass_utils import run_bass_kernel_spmd

    nc = bacc.Bacc("TRN2", target_bir_lowering=False, num_devices=1)
    arrays = {"in_consts": constants()}
    arrays.update((f"in_{name}", np.ascontiguousarray(inputs[name])) for name in _INS)
    args = [nc.dram_tensor(name, a.shape, mybir.dt.from_np(a.dtype), kind="ExternalInput").ap()
            for name, a in arrays.items()]
    out = nc.dram_tensor("out", (1, T, D), F32, kind="ExternalOutput").ap()
    layer(nc, *args, out)
    return run_bass_kernel_spmd(nc, [arrays], core_ids=[0]).results[0]["out"]
```

```python
import math
from contextlib import ExitStack

import numpy as np

import concourse.bass as bass
from concourse import mybir

F32 = mybir.dt.float32
F32R = mybir.dt.float32r
I32 = mybir.dt.int32
U32 = mybir.dt.uint32
ALU = mybir.AluOpType
ACT = mybir.ActivationFunctionType
AX = mybir.AxisListType.X

P = 128
D = 1024
T = 256
TT = T // P
KC = D // P
HALF = 512
CHUNK = 64
EPS = 1e-6
SB_HEADS, DIFF_HEADS, MEM_HEADS = 8, 4, 4
HEAD = 64
MEM_HEAD = D // MEM_HEADS
LAMBDA_INIT = 0.8 - 0.6 * math.exp(0.0)
E = 32
TOP_K = 4
SLOTS = 64
ROUNDS = T // SLOTS
LIMIT, ALPHA = 7.0, 1.702
NOT_CHOSEN = 1024.0
STEPS = 4

(U_SBQ, U_SBK, U_SBV, U_DQ, U_DK, U_DV, U_GSB, _, U_GDF, _, U_MK, _,
 U_UPS, U_UPD, U_OUT, _, U_MQ, _, U_MV, _, U_MO, _) = range(22)
UNITS = 22
RING = 8
UNIT = 4096
DENSE_SLOTS = 3
HIGH_SLOT = 3
QUARTER = UNIT // 4
MEM_PT, MEM_O = (6, 6, 6, 2), (7, 7, 7, 3)
MOE_SLOT = [5, 6, 7, 1, 4, 2, 0, 3]

C_ID, C_NTRI, C_NONE, C_ROT, C_STRI, C_ONE, C_SLOT, C_DMASK = (P * i for i in range(8))
C_IOTA = 8 * P
C_EIDX = C_IOTA + E
C_R64 = C_EIDX + ROUNDS * E
C_BLK = C_R64 + ROUNDS * E
C_INV = C_BLK + 4
C_COLS = C_INV + 1

TWO_PI_A = 6.28125
TWO_PI_B = float(np.float32(2 * math.pi - TWO_PI_A) // 2.0 ** -20 * 2.0 ** -20)
TWO_PI_C = float(np.float32(2 * math.pi - TWO_PI_A - TWO_PI_B))
ROUNDER = 1.5 * 2.0 ** 23


def constants():
    c = np.zeros((P, C_COLS), np.float32)
    p = np.arange(P)
    c[:, C_ID:C_ID + P] = np.eye(P)
    c[:, C_NTRI:C_NTRI + P] = -(p[:, None] >= p[None, :]).astype(np.float32)
    c[:, C_NONE:C_NONE + P] = -1.0
    for m in range(P):
        if m % HEAD < HEAD // 2:
            c[m + HEAD // 2, C_ROT + m] = -1.0
        else:
            c[m - HEAD // 2, C_ROT + m] = 1.0
    c[:, C_STRI:C_STRI + P] = p[:, None] < p[None, :]
    c[:, C_ONE:C_ONE + P] = 1.0
    c[:, C_SLOT:C_SLOT + P] = p[None, :] % SLOTS
    c[:, C_DMASK:C_DMASK + P] = np.where(p[None, :] // CHUNK > p[:, None] // CHUNK, -1e30, 0.0)
    c[:, C_IOTA:C_IOTA + E] = np.arange(E)
    i = np.arange(ROUNDS * E)
    c[:, C_EIDX:C_EIDX + ROUNDS * E] = i % E
    c[:, C_R64:C_R64 + ROUNDS * E] = SLOTS * (i // E)
    c[:, C_BLK:C_BLK + 4] = p[:, None] - 32 * np.arange(4)[None, :]
    half = HEAD // 2
    c[:, C_INV] = np.float32(10000.0) ** (-(p % half).astype(np.float32) / np.float32(half))
    return c


def kind(n):
    if n in (U_UPS, U_UPD):
        return "U"
    return "N" if n in (U_SBV, U_DV, U_OUT, U_OUT + 1, U_MV, U_MV + 1, U_MO, U_MO + 1) else "T"


def use(n, g=0):
    return n + g + min(max(n - U_UPS, 0), 2)


def layer(nc, consts, x, mem, positions, norm_mix, w_in, lambda_q1, lambda_k1, lambda_q2,
          lambda_k2, diff_subln, w_up_sb, w_up_diff, w_out, norm_mem_q, norm_mem_kv, w_mem_q,
          w_mem_kv, w_mem_o, norm_ffn, w_router, b_router, w_gate_up, b_gate_up, w_down, b_down,
          norm_final, out):
    ctx = ExitStack()

    def sb(name, shape, dt=F32):
        return ctx.enter_context(nc.sbuf_tensor(name, shape, dt))

    def sb_split(name, shape, slots=1):
        at = -(-nc.sbuf_base // 32) * 32
        size = 4 * int(np.prod(shape[1:])) // slots
        whole = sb(name, shape)
        split = [nc.alloc_sbuf_tensor_at(f"{name}_split{i}", shape if slots == 1 else [P, *shape[2:]],
                                         F32R, offset=at + size * i).ap() for i in range(slots)]
        return whole, split if slots > 1 else split[0]

    def sem(name):
        return ctx.enter_context(nc.semaphore(name))

    with ctx:
        ring, ring_split = sb_split("ring", [P, RING, UNIT], RING)
        cst = sb("cst", [P, C_COLS])
        xs = sb("xs", [P, TT, D])
        xn, xn_split = sb_split("xn", [P, TT, D])
        hT, hT_split = sb_split("hT", [P, KC, T])
        oT, oT_split = sb_split("oT", [P, KC, T])
        kTm = sb("kTm", [P, KC, T])
        vm = sb("vm", [P, TT, D])
        scr = sb("scr", [P, 5632])
        wr = sb("wr", [P, KC, E])
        gT = sb("gT", [P, 33])
        gperm = sb("gperm", [P, KC])
        st = sb("st", [P, 96])
        middle_count = sb("middle_count", [1, 2], I32)
        topi = sb("topi", [P, TT, 8], U32)

        def region(slot, at, n):
            return ring[:, slot, at:at + n]

        ms = region(4, 2048, 2048).rearrange("p (a d) -> p a d", a=TT)
        qT = region(5, 0, 1024).rearrange("p (c t) -> p c t", c=4)
        kT = region(5, 1024, 1024).rearrange("p (c t) -> p c t", c=4)
        vs = region(5, 2048, 1024).rearrange("p (a d) -> p a d", a=TT)
        vd = region(5, 3072, 1024).rearrange("p (a d) -> p a d", a=TT)
        dqk = region(6, 0, 2048).rearrange("p (n c t) -> p n c t", n=2, c=4)
        raw = region(6, 2048, 2048).rearrange("p (n c t) -> p n c t", n=2, c=4)
        sg = ring[:, 7, :].rearrange("p (n k t) -> p n k t", n=2, k=KC)

        def f32(ap):
            return ap.bitcast(F32)

        hT_high = hT_split
        hT_low = xn_split.rearrange("p a (k t) -> p (a k) t", t=T)
        hmT_high = ring_split[4][:, 0:2048].rearrange("p (k t) -> p k t", k=KC)
        hmT_low = ring_split[4][:, 2048:4096].rearrange("p (k t) -> p k t", k=KC)
        oT_high = oT_split
        oT_low = ring_split[5][:, 0:2048].rearrange("p (k t) -> p k t", k=KC)
        mixed_low, mixed_high = (ring_split[7][:, 2048 * n:2048 * n + 2048]
                                 .rearrange("p (k t) -> p k t", k=KC) for n in range(2))

        def quarter(n, slot, q, whole=None):
            w = ring_split[slot] if whole is None else whole[:, slot, :]
            if slot == HIGH_SLOT:
                w = w[:, QUARTER * q:QUARTER * q + QUARTER]
                return w.rearrange("p (k n) -> p k n", k={"T": KC, "N": 2, "U": 4}[kind(n)])
            if kind(n) == "U":
                return w.rearrange("p (k n) -> p k n", k=4)[:, :, T * q:T * q + T]
            w = w.rearrange("p (k n) -> p k n", k=KC)
            return w[:, :, P * q:P * q + P] if kind(n) == "T" else w[:, 2 * q:2 * q + 2, :]

        lamr = scr[:, 4736:4992].rearrange("p (r d) -> p r d", r=4)
        gffn = scr[0:4, 4992:5248]
        posi = scr[0:1, 5248:5504].bitcast(I32)
        grows = scr[0:33, 5504:5632]
        sp_t = scr[:, 0:768].rearrange("p (h n) -> p h n", h=2)
        sp_l = scr[:, 768:1536].rearrange("p (h n) -> p h n", h=2)
        sp_w = scr[:, 1536:2304].rearrange("p (h n) -> p h n", h=2)
        cosT = scr[:, 2304:2560]
        sinT = scr[:, 2560:2816]
        ang = scr[:, 2816:3328]
        angn = scr[:, 3328:3840]
        rtmp = scr[:, 2816:3840].rearrange("p (a c t) -> p a c t", a=2, c=2)
        d_e = scr[:, 3840:4608].rearrange("p (c n) -> p c n", c=2)
        d_p = scr[:, 4608:4992]
        d_pT = scr[:, 4992:5376]
        od = scr[:, 0:1024].rearrange("p (a d) -> p a d", a=TT)
        odn = scr[:, 1024:2048].rearrange("p (a d) -> p a d", a=TT)
        m_p = scr[:, 0:1024].rearrange("p (g a m) -> p g a m", g=2, a=TT)
        m_pT = scr[:, 1024:2048].rearrange("p (g m t) -> p g m t", g=2, m=TT)
        xe = scr[:, 0:1024].rearrange("p (g k s) -> p g k s", g=2, k=KC)
        glu = scr[:, 1024:1536]
        lin = scr[:, 1536:2048]
        sig = scr[:, 2048:2560]
        act = scr[:, 2560:3072]
        actT = scr[:, 3072:3584]
        yb = scr[:, 3584:4096]
        comb = scr[:, 4096:4608].rearrange("p (g t) -> p g t", g=2)
        pick = scr[:, 4608:4736].rearrange("p (a s) -> p a s", a=TT)
        pickg = scr[:, 4736:4992].rearrange("p (a s) -> p a s", a=TT)
        esel = scr[:, 4992:5008].rearrange("p (g b) -> p g b", g=4)
        gfin = kTm[:, 0:4, :].rearrange("p k t -> p (k t)")
        brow = kTm[:, 4, 0:E]
        bgu = vm[:, 0, 0:HALF]
        bdn = vm[:, 0, HALF:2 * HALF]
        slot_of = vm[:, 1, 0:256].rearrange("p (a i) -> p a i", a=TT)
        gate_of = vm[:, 1, 256:512].rearrange("p (a i) -> p a i", a=TT)
        lg = vm[:, 1, 512:576].rearrange("p (a e) -> p a e", a=TT)
        chosen = vm[:, 1, 576:640].rearrange("p (a e) -> p a e", a=TT)
        gates = vm[:, 1, 640:704].rearrange("p (a e) -> p a e", a=TT)
        hot = vm[:, 1, 704:736]
        hotg = vm[:, 1, 736:768]
        cnt = vm[:, 1, 768:800]
        topv = vm[:, 1, 800:816].rearrange("p (a k) -> p a k", a=TT)
        topf = vm[:, 1, 816:832].rearrange("p (a k) -> p a k", a=TT)
        tope = vm[:, 1, 832:840].rearrange("p (a k) -> p a k", a=TT)
        few = vm[:, 1, 840:856]

        ident = cst[:, C_ID:C_ID + P]
        ones = cst[:, C_ONE:C_ONE + P]
        one = cst[:, C_ONE:C_ONE + 1]
        posf = scr[0:1, 3840:4096]

        bank = [ctx.enter_context(nc.psum_tensor(f"bank{i}", [P, HALF], F32)) for i in range(8)]

        const_in, small_in = sem("const_in"), sem("small_in")
        x_in, mem_in, late_in = sem("x_in"), sem("mem_in"), sem("late_in")
        unit_in = [sem(f"unit_in{k}") for k in range(DENSE_SLOTS)]
        high_ready, low_ready, quarter_used = sem("high_ready"), sem("low_ready"), sem("quarter_used")
        expert_in = [sem(f"expert_in{k}") for k in range(RING)]
        expert_used = sem("expert_used")
        out_done = sem("out_done")
        dve_step, act_step = sem("dve_step"), sem("act_step")
        gain_rows_T, gain_ready = sem("gain_rows_T"), sem("gain_ready")
        pos_ready, pos_spread, ang_ready, rope_ready = (
            sem("pos_ready"), sem("pos_spread"), sem("ang_ready"), sem("rope_ready"))
        lam_dots, lam_exp, lam_ready = sem("lam_dots"), sem("lam_exp"), sem("lam_ready")
        sq_ready, ms_ready, rt_ready, xn_ready = (
            sem("sq_ready"), sem("ms_ready"), sem("rt_ready"), sem("xn_ready"))
        turned, turned_high, turned_low = sem("turned"), sem("turned_high"), sem("turned_low")
        rinv_ready = sem("rinv_ready")
        tile0_full, bank0_read, bank1_read = sem("tile0_full"), sem("bank0_read"), sem("bank1_read")
        rot_full, rot_read = sem("rot_full"), sem("rot_read")
        z_full, soft_ready, l_ready, l_masked = (
            sem("z_full"), sem("soft_ready"), sem("l_ready"), sem("l_masked"))
        after_full, w_ready, w_masked = sem("after_full"), sem("w_ready"), sem("w_masked")
        sbo_full, sbo_read = sem("sbo_full"), sem("sbo_read")
        dz_full, dmax_ready, dexp_ready, dp_ready = (
            sem("dz_full"), sem("dmax_ready"), sem("dexp_ready"), sem("dp_ready"))
        dpT_full, dpT_read, do_full, do_read = (
            sem("dpT_full"), sem("dpT_read"), sem("do_full"), sem("do_read"))
        dsq_ready, dms_ready, drt_ready, don_ready = (
            sem("dsq_ready"), sem("dms_ready"), sem("drt_ready"), sem("don_ready"))
        doT_full, doT_high, doT_read = sem("doT_full"), sem("doT_high"), sem("doT_read")
        gate_ready, mixed_sum, mixed_rounded, mixed_ready = (
            sem("gate_ready"), sem("mixed_sum"), sem("mixed_rounded"), sem("mixed_ready"))
        mz_full, mmax_ready, mexp_ready, mp_ready = (
            sem("mz_full"), sem("mmax_ready"), sem("mexp_ready"), sem("mp_ready"))
        mpT_full, mpT_read, mo_full, mo_high, mo_read = (
            sem("mpT_full"), sem("mpT_read"), sem("mo_full"), sem("mo_high"), sem("mo_read"))
        logit_full, top_ready, gexp_ready, chosen_ready = (
            sem("logit_full"), sem("top_ready"), sem("gexp_ready"), sem("chosen_ready"))
        rank_full, route_ready = sem("rank_full"), sem("route_ready")
        pick_ready, pickg_ready, esel_ready = sem("pick_ready"), sem("pickg_ready"), sem("esel_ready")
        xe_full, xe_ready = sem("xe_full"), sem("xe_ready")
        glu_ready, sig_ready, gated_ready, act_ready = (
            sem("glu_ready"), sem("sig_ready"), sem("gated_ready"), sem("act_ready"))
        actT_full, actT_ready = sem("actT_full"), sem("actT_ready")
        comb_full, comb_ready, y_ready = sem("comb_full"), sem("comb_ready"), sem("y_ready")
        spread_full, added = sem("spread_full"), sem("added")

        block = ctx.enter_context(nc.Block())


        def await_full(eng, n, b, g=0):
            if kind(n) == "N" and b == 0:
                eng.wait_ge(tile0_full, sum(kind(m) == "N" for m in range(n + 1)))
            else:
                eng.wait_ge(quarter_used, 4 * n + (2 * g + b + 1 if kind(n) == "U" else 2 * b + 2))

        @block.sync
        def _(sp):
            sp.dma_start(xs[:, :, :], x[0].rearrange("(a p) d -> p a d", p=P)).then_inc(x_in, 16)
            sp.dma_start(cst[:, :], consts).then_inc(const_in, 16)
            for r, g in enumerate((norm_mix, norm_mem_q, norm_mem_kv, norm_ffn)):
                sp.dma_start(grows[8 * r:8 * r + 8, :],
                             g.rearrange("a (k p) -> (a k) p", p=P)).then_inc(small_in, 16)
            sp.dma_start(grows[32:33, :], diff_subln).then_inc(small_in, 16)
            sp.dma_start(gffn[:, :], norm_ffn.rearrange("a (u n) -> (a u) n", u=4)).then_inc(small_in, 16)
            sp.dma_start(posi[:, :], positions).then_inc(small_in, 16)
            for r, g in enumerate((lambda_q1, lambda_k1, lambda_q2, lambda_k2)):
                sp.dma_start(lamr[:, r, :], g.partition_broadcast(P).rearrange("p a d -> p (a d)")
                             ).then_inc(small_in, 16)
            sp.dma_start(wr[:, :, :], w_router[0].rearrange("(k p) e -> p k e", p=P)).then_inc(small_in, 16)

            def by_columns(w, c0):
                return w.rearrange("(k p) n -> p k n", p=P)[:, :, c0:c0 + HALF]

            def load_gate_up(m, e, q):
                sp.dma_start(ring[:, MOE_SLOT[m % 8], :],
                             w_gate_up[0, e, 256 * q:256 * q + 256, :].rearrange("(p j) n -> p (j n)", j=2)
                             ).then_inc(expert_in[MOE_SLOT[m % 8]], 16)

            def load_down(m, e, q):
                sp.dma_start(ring[:, MOE_SLOT[m % 8], :],
                             w_down[0, e, HALF * q:HALF * q + HALF, :].rearrange("(p j) n -> p (j n)", j=4)
                             ).then_inc(expert_in[MOE_SLOT[m % 8]], 16)

            for n in range(UNITS):
                if n < U_MK:
                    src = by_columns(w_in[0], HALF * n)
                elif n < U_UPS:
                    src = by_columns(w_mem_kv[0], HALF * (n - U_MK))
                elif n < U_OUT:
                    src = (w_up_sb if n == U_UPS else w_up_diff)[0].rearrange("(k p) n -> p k n", p=P)
                elif n < U_MQ:
                    src = by_columns(w_out[0], HALF * (n - U_OUT))
                elif n < U_MV:
                    src = by_columns(w_mem_q[0], HALF * (n - U_MQ))
                elif n < U_MO:
                    src = by_columns(w_mem_kv[0], D + HALF * (n - U_MV))
                else:
                    src = by_columns(w_mem_o[0], HALF * (n - U_MO))
                if n >= DENSE_SLOTS:
                    sp.wait_ge(quarter_used, 4 * (n - DENSE_SLOTS + 1))
                dst = ring[:, n % DENSE_SLOTS, :].rearrange("p (k n) -> p k n", k=src.shape[1])
                sp.dma_start(dst, src).then_inc(unit_in[n % DENSE_SLOTS], 16)
                if n == 1:
                    sp.dma_start(ms[:, :, :], mem[0].rearrange("(a p) d -> p a d", p=P)).then_inc(mem_in, 16)
                if 18 <= n < 21:
                    load_gate_up(n - 18, 0, n - 18)

            sp.wait_ge(quarter_used, 4 * (U_MV + 2))
            load_gate_up(3, 0, 3)
            late = [(brow, b_router.partition_broadcast(P).rearrange("p a d -> p (a d)"))]
            late += [(bgu[32 * k:32 * k + 32, :], b_gate_up[0, :, HALF * k:HALF * k + HALF])
                    for k in range(4)]
            late += [(bdn[32 * k:32 * k + 32, :], b_down[0, :, HALF * k:HALF * k + HALF])
                     for k in range(2)]
            late += [(gfin, norm_final.rearrange("(a d) -> a d", a=1).partition_broadcast(P)
                      .rearrange("p a d -> p (a d)"))]

            def steps(b, first, last):
                for j in range(STEPS):
                    if not (last and j == STEPS - 1):
                        for q in range(4):
                            m = 24 * b + 6 * j + 4 + q
                            if first and j == 0:
                                sp.wait_ge(quarter_used, 4 * (20, 21, 22, 22)[q])
                                if q == 1:
                                    sp.wait_ge(mo_read, MEM_HEADS)
                                    for to, of in late:
                                        sp.dma_start(to, of).then_inc(late_in, 16)
                            else:
                                sp.wait_ge(expert_used, m - 7)
                            load_gate_up(6 * j + 4 + q, (STEPS * b + j + 1) % E, q)
                    for q in range(2):
                        m = 24 * b + 6 * j + 8 + q
                        sp.wait_ge(expert_used, m - 7)
                        load_down(6 * j + 8 + q, (STEPS * b + j) % E, q)

            steps(0, True, False)
            sp.wait_ge(route_ready, 1)
            middle = sp.value_load(middle_count[0:1, 0:1], min_val=E // STEPS - 2,
                                   max_val=ROUNDS * E // STEPS - 2)
            with sp.Fori(1, middle + 1) as b:
                steps(b, False, False)
            steps(middle + 1, False, True)
            sp.wait_ge(xn_ready, 5)
            sp.dma_start(out[0].rearrange("(a p) d -> p a d", p=P), xn[:, :, :]).then_inc(out_done, 16)
            sp.wait_ge(out_done, 16)

        @block.tensor
        def _(pe):
            def turn(k, src, half, ready):
                for a in range(TT):
                    ready(a)
                    for c in range(4 * half, 4 * half + 4):
                        if k == 1 and a == 0 and c % 2 == 0:
                            pe.wait_ge(turned_low, c // 2 + 1)
                        at = (c % 2) * T + a * P
                        i = pe.transpose(bank[2 + c // 2][:, at:at + P],
                                         src[:, a, c * P:c * P + P], ident)
                        if a == TT - 1 and c % 2:
                            i.then_inc(turned, 1)

            def three(to, lhs, rhs, start, stop):
                pe.matmul(to, lhs[0], rhs[0], start=start, stop=False, skip_group_check=True)
                pe.matmul(to, lhs[0], rhs[1], start=False, stop=False, skip_group_check=True)
                return pe.matmul(to, lhs[1], rhs[0], start=False, stop=stop,
                                 skip_group_check=True)

            def await_quarter(n, q):
                pe.wait_ge(low_ready, 4 * n + q + 1)

            def await_bank(b, u):
                if u > 0:
                    pe.wait_ge((bank0_read, bank1_read)[b], u)

            def project_T(n, h, low, ks=(0, KC)):
                for q in range(4):
                    b, at = q // 2, (q % 2) * T
                    if ks[0] == 0:
                        await_quarter(n, q)
                        if at == 0:
                            await_bank(b, use(n))
                    w = quarter(n, HIGH_SLOT, q), quarter(n, n % DENSE_SLOTS, q)
                    for k in range(*ks):
                        i = three(bank[b][:, at:at + T], [x[:, k, :] for x in w],
                                  (h[:, k, :], low[:, k, :]),
                                  k == 0 and (at == 0 or ks[1] == KC), k == KC - 1)
                    if ks[1] == KC:
                        i.then_inc(quarter_used, 1)

            def project(n, h, low, ready=None):
                for a in range(TT):
                    await_bank(a, use(n))
                    for k in range(KC):
                        if a == 0 and k % 2 == 0:
                            await_quarter(n, k // 2)
                        if a == 0 and ready:
                            ready(k)
                        w = quarter(n, HIGH_SLOT, k // 2), quarter(n, n % DENSE_SLOTS, k // 2)
                        i = three(bank[a][:, :], [x[:, k, a * P:a * P + P] for x in (h, low)],
                                  [x[:, k % 2, :] for x in w], k == 0, k == KC - 1)
                        if a == 1 and k % 2:
                            i.then_inc(quarter_used, 1)
                    if a == 0:
                        i.then_inc(tile0_full, 1)

            def project_up(n, q0, h, low, base):
                for q in (q0, q0 + 1):
                    await_quarter(n, q)
                    await_bank(q % 2, use(n, q // 2))
                    w = quarter(n, HIGH_SLOT, q), quarter(n, n % DENSE_SLOTS, q)
                    for o in range(2):
                        for k in range(4):
                            i = three(bank[q % 2][:, T * o:T * o + T],
                                      [x[:, k, P * o:P * o + P] for x in w],
                                      (h[:, base + k, :], low[:, base + k, :]), k == 0, k == 3)
                    i.then_inc(quarter_used, 1)

            def sb_scores(p):
                for hh in range(2):
                    h = 2 * p + hh
                    zb = bank[2 + 2 * (p % 2) + hh]
                    rows = slice(HEAD * hh, HEAD * hh + HEAD)
                    if p >= 2:
                        pe.wait_ge(w_ready, h - 3)
                    if p == 0:
                        pe.wait_ge(turned_low, 8)
                        pe.wait_ge(bank0_read, use(U_SBK + 1))
                        pe.wait_ge(bank1_read, use(U_SBK + 1))
                    pe.matmul(zb[:, 0:T], kT[rows, p, 0:P], qT[rows, p, :],
                              start=True, stop=False, skip_group_check=True)
                    pe.matmul(zb[:, T:T + P], kT[rows, p, P:T], qT[rows, p, P:T], start=False,
                              stop=False, skip_group_check=True).then_inc(z_full, 1)

            def sb_after(p):
                for hh in range(2):
                    h = 2 * p + hh
                    zb = bank[2 + 2 * (p % 2) + hh]
                    pe.wait_ge(l_masked, h + 1)
                    ntri, nones = cst[:, C_NTRI:C_NTRI + P], cst[:, C_NONE:C_NONE + P]
                    pe.matmul(zb[:, 0:T], ntri, sp_l[:, hh, 0:T], start=False, stop=False,
                              skip_group_check=True)
                    pe.matmul(zb[:, P:T], nones, sp_l[:, hh, T:T + P], start=False, stop=False,
                              skip_group_check=True)
                    pe.matmul(zb[:, T:T + P], ntri, sp_l[:, hh, T:T + P], start=False, stop=True,
                              skip_group_check=True).then_inc(after_full, 1)

            def sb_values(p):
                if p > 0:
                    pe.wait_ge(sbo_read, p)
                for hh in range(2):
                    h = 2 * p + hh
                    pe.wait_ge(w_masked, h + 1)
                    rows = slice(HEAD * hh, HEAD * hh + HEAD)
                    pe.matmul(bank[7][rows, 0:T], vs[:, 0, HEAD * h:HEAD * h + HEAD],
                              sp_w[:, hh, 0:T], start=True, stop=False, skip_group_check=True)
                    i = pe.matmul(bank[7][rows, P:T], vs[:, 1, HEAD * h:HEAD * h + HEAD],
                                  sp_w[:, hh, T:T + P], start=False, stop=True,
                                  skip_group_check=True)
                i.then_inc(sbo_full, 1)

            def rotate(n):
                for g in range(2):
                    if n or g:
                        pe.wait_ge(rot_read, 2 * n + g)
                    else:
                        pe.wait_ge(gain_ready, 1)
                    pe.wait_ge((bank0_read, bank1_read)[g], (U_DQ, U_DK)[n] + 1)
                    pe.matmul(bank[6][:, :], cst[:, C_ROT:C_ROT + P],
                              raw[:, n, 2 * g:2 * g + 2, :].rearrange("p c t -> p (c t)"),
                              start=True, stop=True).then_inc(rot_full, 1)

            def diff_scores(h):
                pe.wait_ge(rot_read, 4)
                if h == 0:
                    pe.wait_ge(w_ready, 6)
                else:
                    pe.wait_ge(dexp_ready, h)
                for c in range(2):
                    zb = bank[2 + c]
                    rows = slice(HEAD * c, HEAD * c + HEAD)
                    mask = cst[:, C_DMASK:C_DMASK + P]
                    pe.matmul(zb[:, 0:P], dqk[rows, 0, h, 0:P], dqk[rows, 1, h, 0:P],
                              start=True, stop=False, skip_group_check=True)
                    pe.matmul(zb[:, P:P + T], dqk[rows, 0, h, P:T], dqk[rows, 1, h, :],
                              start=False, stop=False, skip_group_check=True)
                    pe.matmul(zb[:, 0:P], ident, mask, start=False, stop=False,
                              skip_group_check=True)
                    i = pe.matmul(zb[:, T:T + P], ident, mask, start=False, stop=True,
                                  skip_group_check=True)
                i.then_inc(dz_full, 1)

            def diff_turn(h):
                pe.wait_ge(dp_ready, h + 1)
                if h == 0:
                    pe.wait_ge(w_ready, 8)
                else:
                    pe.wait_ge(dpT_read, h)
                for k in range(3):
                    i = pe.transpose(bank[4][:, k * P:k * P + P], d_p[:, k * P:k * P + P], ident)
                i.then_inc(dpT_full, 1)

            def diff_values(h):
                pe.wait_ge(dpT_read, h + 1)
                if h > 0:
                    pe.wait_ge(do_read, h)
                cols = slice(P * h, P * h + P)
                pe.matmul(bank[5][:, 0:P], d_pT[:, 0:P], vd[:, 0, cols], start=True, stop=True)
                pe.matmul(bank[5][:, P:T], d_pT[:, P:T], vd[:, 0, cols], start=True, stop=False)
                pe.matmul(bank[5][:, P:T], d_pT[:, T:T + P], vd[:, 1, cols], start=False,
                          stop=True).then_inc(do_full, 1)

            pe.wait_ge(const_in, 16)
            pe.wait_ge(small_in, 16 * 12)
            pe.transpose(bank[6][:, 0:33], grows[:, :], cst[0:33, C_ID:C_ID + 33])
            for j in range(2):
                i = pe.transpose(bank[6][:, 40 + 4 * j:44 + 4 * j], gffn[:, j:T:2],
                                 cst[0:4, C_ID:C_ID + 4])
            i.then_inc(gain_rows_T, 1)
            pe.wait_ge(pos_ready, 1)
            pe.matmul(bank[7][:, 0:T], cst[0:1, C_ONE:C_ONE + P], posf, start=True,
                      stop=True).then_inc(pos_spread, 1)
            for half in range(2):
                turn(0, xn, half, lambda a: pe.wait_ge(xn_ready, 1))
            for n in range(U_UPS):
                if n in (U_SBV, U_DV):
                    project(n, hT_high, hT_low)
                elif n < U_MK:
                    project_T(n, hT_high, hT_low)
                else:
                    project_T(n, hmT_high, hmT_low)
                if n == 1:
                    for half in range(2):
                        turn(1, ms, half, lambda a: pe.wait_ge(xn_ready, 2))
                if n == 4:
                    rotate(0)
                if n == 5:
                    rotate(1)
                if 4 <= n < 8:
                    sb_values(n - 4)
                if 3 <= n < 7:
                    sb_after(n - 3)
                if 2 <= n < 6:
                    sb_scores(n - 2)
                if 8 <= n < 12:
                    diff_values(n - 8)
                if 7 <= n < 11:
                    diff_turn(n - 7)
                if 6 <= n < 10:
                    diff_scores(n - 6)
            pe.wait_ge(sbo_read, 4)
            project_up(U_UPS, 0, oT_high, oT_low, 0)
            pe.wait_ge(don_ready, 1)
            for h in range(DIFF_HEADS):
                for a in range(TT):
                    b = 4 + 2 * (h // 2)
                    at = (h % 2) * T + a * P
                    i = pe.transpose(bank[b][:, at:at + P], odn[:, a, P * h:P * h + P], ident)
            i.then_inc(doT_full, 1)
            project_up(U_UPS, 2, oT_high, oT_low, 0)
            pe.wait_ge(doT_read, 2)
            project_up(U_UPD, 0, oT_high, oT_low, 4)
            project_up(U_UPD, 2, oT_high, oT_low, 4)

            def await_mixed(k):
                if k % 4 == 0:
                    pe.wait_ge(mixed_ready, k // 4 + 1)

            project(U_OUT, mixed_high, mixed_low, await_mixed)
            project(U_OUT + 1, mixed_high, mixed_low)

            def await_added(n):
                return lambda a: pe.wait_ge((bank0_read, bank1_read)[a], use(n) + 1)

            turn(2, xs, 0, await_added(U_OUT))
            pe.wait_ge(turned_low, 10)
            project_T(U_MQ, hT_high, hT_low, (0, 4))
            turn(2, xs, 1, await_added(U_OUT + 1))
            pe.wait_ge(turned_low, 12)
            project_T(U_MQ, hT_high, hT_low, (4, KC))
            project_T(U_MQ + 1, hT_high, hT_low)

            def mem_scores(h):
                for a in range(TT):
                    zb = bank[2 + 2 * (h % 2) + a]
                    if h >= 2:
                        pe.wait_ge(mexp_ready, h - 1)
                    for c in range(2):
                        i = pe.matmul(zb[:, 0:T], oT[:, 2 * h + c, a * P:a * P + P],
                                      kTm[:, 2 * h + c, :], start=(c == 0), stop=(c == 1))
                i.then_inc(mz_full, 1)

            def mem_turn(h):
                pe.wait_ge(mp_ready, h + 1)
                if h == 3:
                    pe.wait_ge(mexp_ready, 3)
                elif h > 0:
                    pe.wait_ge(mpT_read, h)
                for m in range(TT):
                    for a in range(TT):
                        i = pe.transpose(bank[MEM_PT[h]][:, m * T + a * P:m * T + a * P + P],
                                         m_p[:, h % 2, a, m * P:m * P + P], ident)
                i.then_inc(mpT_full, 1)

            def mem_values(h):
                pe.wait_ge(mpT_read, h + 1)
                if h in (1, 2):
                    pe.wait_ge(mo_read, h)
                for c in range(2):
                    for m in range(TT):
                        d0 = MEM_HEAD * h + P * c
                        i = pe.matmul(bank[MEM_O[h]][:, c * T:c * T + T], vm[:, m, d0:d0 + P],
                                      m_pT[:, h % 2, m, :], start=(m == 0), stop=(m == TT - 1))
                i.then_inc(mo_full, 1)

            def await_read(n):
                pe.wait_ge(bank0_read, use(n) + 1)
                pe.wait_ge(bank1_read, use(n) + 1)

            await_read(U_MQ)
            mem_scores(0)
            mem_scores(1)
            project(U_MV, hmT_high, hmT_low)
            mem_turn(0)
            await_read(U_MQ + 1)
            mem_scores(2)
            await_read(U_MV)
            mem_values(0)
            mem_turn(1)
            mem_scores(3)
            mem_values(1)
            project(U_MV + 1, hmT_high, hmT_low)
            mem_turn(2)
            mem_turn(3)
            await_read(U_MV + 1)
            mem_values(2)
            mem_values(3)

            def await_head(k):
                if k % 2 == 0:
                    pe.wait_ge(mo_read, k // 2 + 1)

            project(U_MO, hT_high, hT_low, await_head)
            project(U_MO + 1, hT_high, hT_low)
            turn(3, xs, 0, await_added(U_MO))
            turn(3, xs, 1, await_added(U_MO + 1))
            pe.wait_ge(turned_high, 14)
            pe.wait_ge(turned_low, 14)
            for a in range(TT):
                at = a * E
                for k in range(KC):
                    i = pe.matmul(bank[6][:, at:at + E], hT[:, k, a * P:a * P + P], wr[:, k, :],
                                  start=(k == 0), stop=(k == KC - 1))
            i.then_inc(logit_full, 1)
            pe.wait_ge(chosen_ready, 1)
            stri = cst[:, C_STRI:C_STRI + P]
            pe.matmul(bank[7][:, 0:E], stri, chosen[:, 0, :], start=True, stop=True)
            pe.matmul(bank[7][:, E:2 * E], stri, chosen[:, 1, :], start=True, stop=False)
            pe.matmul(bank[7][:, E:2 * E], ones, chosen[:, 0, :], start=False, stop=True)
            pe.matmul(bank[7][:, 2 * E:3 * E], ones, chosen[:, 0, :], start=True, stop=False)
            pe.matmul(bank[7][:, 2 * E:3 * E], ones, chosen[:, 1, :], start=False,
                      stop=True).then_inc(rank_full, 1)

            def gather(i):
                pe.wait_ge(pick_ready, i + 1)
                for c in range(KC):
                    cols = slice(256 * (c // 2) + c % 2, 256 * (c // 2) + 256, 2)
                    for a in range(TT):
                        ins = pe.matmul(bank[4][:, c * SLOTS:(c + 1) * SLOTS], xn[:, a, cols],
                                        pick[:, a, :], start=(a == 0), stop=(a == TT - 1))
                ins.then_inc(xe_full, 1)

            def spread(i, a, buf):
                for h in range(2):
                    rows = slice(SLOTS * h, SLOTS * h + SLOTS)
                    ins = pe.matmul(bank[6 + h][:, :], comb[rows, buf, a * P:a * P + P],
                                    yb[rows, :], start=True, stop=True)
                ins.then_inc(spread_full, 1)

            def step(b, j, i, prev, cur, nxt, nxt2):
                if cur:
                    pe.wait_ge(act_ready, i + 1)
                    if prev:
                        pe.wait_ge(actT_ready, i)
                    for r in range(4):
                        ins = pe.transpose(bank[3][:, r * P:r * P + P], act[:, r:HALF:4], ident)
                    ins.then_inc(actT_full, 1)
                    pe.wait_ge(pickg_ready, i + 1)
                    if prev:
                        pe.wait_ge(comb_ready, i)
                    for a in range(TT):
                        ins = pe.transpose(bank[5][:, a * P:a * P + P], pickg[:, a, :], ident)
                    ins.then_inc(comb_full, 1)
                if prev:
                    pe.wait_ge(y_ready, i)
                    pe.wait_ge(comb_ready, i)
                    if prev == "second":
                        pe.wait_ge(added, 2 * i - 2)
                    spread(i - 1, 0, (j - 1) % 2)
                if nxt:
                    pe.wait_ge(esel_ready, i + 2)
                    for k in range(4):
                        pe.matmul(bank[k // 2][SLOTS * (k % 2):SLOTS * (k % 2) + SLOTS, :],
                                  esel[:, (j + 1) % 4, k:k + 1].broadcast_to([P, SLOTS]), bgu,
                                  start=True, stop=False)
                    pe.wait_ge(xe_ready, i + 2)
                    for q in range(4):
                        m = 6 * j + 4 + q if j >= 0 else q
                        pe.wait_ge(expert_in[MOE_SLOT[m % 8]], 48 * b + 16 * (m // 8 + 1))
                        w = ring[:, MOE_SLOT[m % 8], :].rearrange("p (j n) -> p j n", j=2)
                        for r in range(2):
                            for k in range(4):
                                ins = pe.matmul(
                                    bank[k // 2][SLOTS * (k % 2):SLOTS * (k % 2) + SLOTS, :],
                                    xe[:, (j + 1) % 2, 2 * q + r, :], w[:, r, HALF * k:HALF * k + HALF],
                                    start=False, stop=(q == 3 and r == 1))
                        ins.then_inc(expert_used, 1)
                        if q == 1 and prev:
                            pe.wait_ge(added, 2 * i - 1)
                            spread(i - 1, 1, (j - 1) % 2)
                elif prev:
                    pe.wait_ge(added, 2 * i - 1)
                    spread(i - 1, 1, (j - 1) % 2)
                if nxt2:
                    pe.wait_ge(xe_ready, i + 2)
                    gather(i + 2)
                if cur:
                    if prev:
                        pe.wait_ge(y_ready, i)
                    for h in range(2):
                        pe.matmul(bank[2][SLOTS * h:SLOTS * h + SLOTS, :],
                                  esel[:, j % 4, h:h + 1].broadcast_to([P, SLOTS]), bdn,
                                  start=True, stop=False)
                    pe.wait_ge(actT_ready, i + 1)
                    for q in range(2):
                        m = 6 * j + 8 + q
                        pe.wait_ge(expert_in[MOE_SLOT[m % 8]], 48 * b + 16 * (m // 8 + 1))
                        w = ring[:, MOE_SLOT[m % 8], :].rearrange("p (j n) -> p j n", j=4)
                        for r in range(4):
                            for h in range(2):
                                ins = pe.matmul(bank[2][SLOTS * h:SLOTS * h + SLOTS, :],
                                                actT[:, P * r + SLOTS * q:P * r + SLOTS * q + SLOTS],
                                                w[:, r, HALF * h:HALF * h + HALF],
                                                start=False, stop=(q == 1 and r == 3))
                        ins.then_inc(expert_used, 1)

            pe.wait_ge(late_in, 16 * 8)
            pe.wait_ge(xn_ready, 3)
            gather(0)
            step(0, -1, -1, None, False, True, True)
            for j in range(STEPS):
                step(0, j, j, (None, "first", "second", "second")[j], True, True, True)
            middle = pe.value_load(middle_count[0:1, 0:1], min_val=E // STEPS - 2,
                                   max_val=ROUNDS * E // STEPS - 2)
            with pe.Fori(1, middle + 1) as b:
                for j in range(STEPS):
                    step(b, j, STEPS * b + j, "second", True, True, True)
            b = middle + 1
            for j in range(STEPS):
                step(b, j, STEPS * b + j, "second", True, j < STEPS - 1, j < STEPS - 2)
            n = STEPS * b + STEPS
            pe.wait_ge(y_ready, n)
            for a in range(TT):
                pe.wait_ge(added, 2 * n - 2 + a)
                spread(n - 1, a, 1)

        @block.scalar
        def _(act_e):
            steps_done = [0]

            def link(ins):
                steps_done[0] += 1
                ins.then_inc(act_step, 1)
                act_e.wait_ge(act_step, steps_done[0])

            def norm(k, src, dst):
                for a in range(TT):
                    i = act_e.activation(dst[:, a, :], src[:, a, :], ACT.Square,
                                         accum_out=st[:, 4 * k + a:4 * k + a + 1])
                i.then_inc(sq_ready, 1)
                act_e.wait_ge(ms_ready, k + 1)
                act_e.activation(st[:, 4 * k + 2:4 * k + 4], st[:, 4 * k:4 * k + 2],
                                 ACT.Sqrt).then_inc(rt_ready, 1)

            def high_of_unit(n, quarters):
                for q in quarters:
                    if q == 0:
                        act_e.wait_ge(unit_in[n % DENSE_SLOTS], 16 * (n // DENSE_SLOTS + 1))
                    if n > 0:
                        act_e.wait_ge(quarter_used, 4 * (n - 1) + q + 1)
                    act_e.activation(quarter(n, HIGH_SLOT, q), quarter(n, n % DENSE_SLOTS, q, ring),
                                     ACT.Copy).then_inc(high_ready, 1)

            def turned_to(dst, k, g0, pairs=range(4)):
                for p in pairs:
                    act_e.wait_ge(turned, 4 * k + p + 1)
                    for c in range(2):
                        i = act_e.activation(dst[:, 2 * p + c, :], bank[2 + p][:, c * T:c * T + T],
                                             ACT.Copy, scale=gT[:, g0 + 2 * p + c:g0 + 2 * p + c + 1])
                    i.then_inc(turned_high, 1)

            def from_bank0(n, dst, scale=1.0):
                await_full(act_e, n, 0)
                act_e.activation(dst, bank[0][:, :], ACT.Copy, scale=scale).then_inc(bank0_read, 1)

            def mem_turned(h):
                act_e.wait_ge(mpT_full, h + 1)
                if h >= 2:
                    act_e.wait_ge(mo_full, h - 1)
                act_e.activation(m_pT[:, h % 2].rearrange("p m t -> p (m t)"), bank[MEM_PT[h]][:, :],
                                 ACT.Copy).then_inc(mpT_read, 1)

            act_e.wait_ge(x_in, 16)
            norm(0, xs, xn)
            act_e.wait_ge(gain_ready, 1)
            turned_to(hT_high, 0, 0)
            high_of_unit(0, range(4))
            def fold(ap):
                return ap.rearrange("p c t -> p (c t)")

            for n in range(U_UPS):
                high_of_unit(n + 1, (0, 1))
                if n == U_SBQ:
                    from_bank0(n, fold(qT[:, 0:2, :]), HEAD ** -0.5)
                elif n == U_SBK:
                    from_bank0(n, fold(kT[:, 0:2, :]))
                elif n == U_SBV:
                    from_bank0(n, vs[:, 0, :])
                elif n == U_DQ:
                    from_bank0(n, fold(raw[:, 0, 0:2, :]), HEAD ** -0.5)
                elif n == U_DK:
                    from_bank0(n, fold(raw[:, 1, 0:2, :]))
                elif n == U_DV:
                    from_bank0(n, vd[:, 0, :])
                elif n < U_MK:
                    g = n - U_GSB
                    from_bank0(n, fold(sg[:, g // 2, 4 * (g % 2):4 * (g % 2) + 2, :]))
                else:
                    from_bank0(n, fold(kTm[:, 4 * (n - U_MK):4 * (n - U_MK) + 2, :]))
                high_of_unit(n + 1, (2, 3))
                if n == 0:
                    act_e.wait_ge(ang_ready, 1)
                    act_e.activation(scr[:, 2304:2816], ang, ACT.Sin).then_inc(rope_ready, 1)
                    act_e.wait_ge(lam_dots, 1)
                    act_e.activation(st[:, 82:84], st[:, 80:82], ACT.Exp).then_inc(lam_exp, 1)
                    act_e.wait_ge(mem_in, 16)
                    for a in range(TT):
                        i = act_e.activation(kTm[:, 4 * a:4 * a + 4, :].rearrange("p k t -> p (k t)"),
                                             ms[:, a, :], ACT.Square, accum_out=st[:, 4 + a:5 + a])
                    i.then_inc(sq_ready, 1)
                    act_e.wait_ge(ms_ready, 2)
                    act_e.activation(st[:, 6:8], st[:, 4:6], ACT.Sqrt).then_inc(rt_ready, 1)
                if n == 1:
                    turned_to(hmT_high, 1, 16)
                if n == 10:
                    act_e.wait_ge(bank1_read, use(U_MK))
                    for g in range(2):
                        i = act_e.activation(sg[:, g], sg[:, g], ACT.Sigmoid)
                    i.then_inc(gate_ready, 1)
                if 3 <= n < 7:
                    for hh in range(2):
                        h = 2 * (n - 3) + hh
                        act_e.wait_ge(after_full, h + 1)
                        if n > 3:
                            act_e.wait_ge(sbo_full, n - 3)
                        act_e.activation(sp_w[:, hh, :], bank[2 + 2 * ((n - 3) % 2) + hh][:, 0:384],
                                         ACT.Exp).then_inc(w_ready, 1)
                if 2 <= n < 6:
                    for hh in range(2):
                        h = 2 * (n - 2) + hh
                        act_e.wait_ge(z_full, h + 1)
                        if n > 2:
                            act_e.wait_ge(l_ready, h - 1)
                        t = sp_t[:, hh, :]
                        link(act_e.activation(t, bank[2 + 2 * ((n - 2) % 2) + hh][:, 0:384], ACT.Abs))
                        link(act_e.activation(t, t, ACT.Exp, scale=-1.0))
                        act_e.activation(t, t, ACT.Ln, bias=one).then_inc(soft_ready, 1)
                if 7 <= n < 11:
                    act_e.wait_ge(dpT_full, n - 6)
                    if n > 7:
                        act_e.wait_ge(do_full, n - 7)
                    act_e.activation(d_pT, bank[4][:, 0:384], ACT.Copy).then_inc(dpT_read, 1)
                if 6 <= n < 10:
                    h = n - 6
                    act_e.wait_ge(dmax_ready, h + 1)
                    for c in range(2):
                        for a in range(TT):
                            k = 24 + 2 * c + a
                            cols = slice(0, P) if a == 0 else slice(P, P + T)
                            i = act_e.activation(d_e[:, c, cols], bank[2 + c][:, cols], ACT.Exp,
                                                 bias=st[:, k:k + 1], accum_out=st[:, k + 4:k + 5])
                    i.then_inc(dexp_ready, 1)
                if 8 <= n < 12:
                    h = n - 8
                    act_e.wait_ge(do_read, h + 1)
                    for a in range(TT):
                        i = act_e.activation(odn[:, a, P * h:P * h + P], od[:, a, P * h:P * h + P],
                                             ACT.Square, accum_out=st[:, 40 + 2 * h + a:41 + 2 * h + a])
                    i.then_inc(dsq_ready, 1)
            act_e.wait_ge(dms_ready, 1)
            act_e.activation(st[:, 48:56], st[:, 40:48], ACT.Sqrt).then_inc(drt_ready, 1)
            high_of_unit(U_UPD, (0, 1))
            act_e.wait_ge(doT_full, 1)
            for g in range(2):
                act_e.activation(fold(oT_high[:, 4 + 2 * g:6 + 2 * g, :]), bank[4 + 2 * g][:, :],
                                 ACT.Copy, scale=st[:, 88:89]).then_inc(doT_high, 1)
            high_of_unit(U_UPD, (2, 3))
            high_of_unit(U_OUT, (0,))
            act_e.wait_ge(mixed_sum, 1)
            act_e.activation(fold(mixed_high[:, 0:4, :]), fold(sg[:, 0, 0:4, :]),
                             ACT.Copy).then_inc(mixed_rounded, 1)
            high_of_unit(U_OUT, (1, 2, 3))
            act_e.wait_ge(mixed_sum, 2)
            act_e.activation(fold(mixed_high[:, 4:8, :]), fold(sg[:, 0, 4:8, :]),
                             ACT.Copy).then_inc(mixed_rounded, 1)
            high_of_unit(U_OUT + 1, range(4))
            high_of_unit(U_MQ, range(4))
            turned_to(hT_high, 2, 8)
            for a in range(TT):
                act_e.wait_ge((bank0_read, bank1_read)[a], use(U_OUT + 1) + 1)
                i = act_e.activation(scr[:, D * (a + 1):D * (a + 2)], xs[:, a, :], ACT.Square,
                                     accum_out=st[:, 8 + a:9 + a])
            i.then_inc(sq_ready, 1)
            act_e.wait_ge(ms_ready, 3)
            act_e.activation(st[:, 10:12], st[:, 8:10], ACT.Sqrt).then_inc(rt_ready, 1)
            for n in (U_MQ, U_MQ + 1):
                high_of_unit(n + 1, (0, 1))
                from_bank0(n, fold(oT[:, 4 * (n - U_MQ):4 * (n - U_MQ) + 2, :]), MEM_HEAD ** -0.5)
                high_of_unit(n + 1, (2, 3))

            def mem_exp(h):
                act_e.wait_ge(mmax_ready, h + 1)
                if h >= 2:
                    act_e.wait_ge(mpT_full, h - 1)
                for a in range(TT):
                    k = 60 + 4 * (h % 2) + a
                    i = act_e.activation(m_p[:, h % 2, a, :], bank[2 + 2 * (h % 2) + a][:, 0:T], ACT.Exp,
                                         bias=st[:, k:k + 1], scale=st[:, 10 + a:11 + a],
                                         accum_out=st[:, k + 2:k + 3])
                i.then_inc(mexp_ready, 1)

            def mem_out(h):
                act_e.wait_ge(mo_full, h + 1)
                act_e.activation(fold(hT_high[:, 2 * h:2 * h + 2, :]), bank[MEM_O[h]][:, :],
                                 ACT.Copy).then_inc(mo_high, 1)

            mem_exp(0)
            mem_exp(1)
            from_bank0(U_MV, vm[:, 0, 0:HALF])
            high_of_unit(U_MV + 1, range(4))
            mem_turned(0)
            mem_exp(2)
            mem_out(0)
            mem_turned(1)
            mem_exp(3)
            mem_out(1)
            from_bank0(U_MV + 1, vm[:, 0, HALF:D])
            high_of_unit(U_MO, range(4))
            mem_turned(2)
            mem_turned(3)
            mem_out(2)
            mem_out(3)
            high_of_unit(U_MO + 1, range(4))
            turned_to(hT, 3, 24, (0, 2))
            act_e.wait_ge(bank0_read, use(U_MO + 1) + 1)
            act_e.wait_ge(bank1_read, use(U_MO + 1) + 1)
            norm(3, xs, xn)
            act_e.wait_ge(rinv_ready, 4)
            for a in range(TT):
                i = act_e.activation(xn[:, a, :], xs[:, a, :], ACT.Copy, scale=st[:, 14 + a:15 + a])
            i.then_inc(xn_ready, 1)
            act_e.wait_ge(top_ready, 1)
            for a in range(TT):
                i = act_e.activation(tope[:, a, :], topv[:, a, 0:TOP_K], ACT.Exp,
                                     bias=few[:, a:a + 1], accum_out=few[:, 2 + a:3 + a])
            i.then_inc(gexp_ready, 1)

            def step(b, j, i, prev, cur, nxt):
                if cur:
                    act_e.wait_ge(actT_full, i + 1)
                    if prev:
                        act_e.wait_ge(expert_used, 6 * i + 4)
                    act_e.activation(actT, bank[3][:, :], ACT.Copy).then_inc(actT_ready, 1)
                    act_e.wait_ge(comb_full, i + 1)
                    act_e.activation(comb[:, j % 2, :], bank[5][:, 0:T], ACT.Copy).then_inc(comb_ready, 1)
                if nxt:
                    act_e.wait_ge(glu_ready, i + 2)
                    act_e.activation(sig, glu, ACT.Sigmoid, scale=ALPHA).then_inc(sig_ready, 1)
                if cur:
                    act_e.wait_ge(expert_used, 6 * i + (10 if nxt else 6))
                    if prev:
                        act_e.wait_ge(spread_full, 2 * i)
                    act_e.activation(yb, bank[2][:, :], ACT.Copy).then_inc(y_ready, 1)

            step(0, -1, -1, False, False, True)
            for j in range(STEPS):
                step(0, j, j, j > 0, True, True)
            act_e.wait_ge(route_ready, 1)
            middle = act_e.value_load(middle_count[0:1, 0:1], min_val=E // STEPS - 2,
                                   max_val=ROUNDS * E // STEPS - 2)
            with act_e.Fori(1, middle + 1) as b:
                for j in range(STEPS):
                    step(b, j, STEPS * b + j, True, True, True)
            b = middle + 1
            for j in range(STEPS):
                step(b, j, STEPS * b + j, True, True, j < STEPS - 1)
            act_e.wait_ge(added, 2 * STEPS * b + 2 * STEPS)
            norm(4, xs, xn)

        @block.gpsimd
        def _(pool):
            def keep_past(t):
                v = t.rearrange("p (b n) -> p b n", b=3)[:, 0:3:2, :]
                return pool.affine_select(out=v, in_=v, pattern=[[0, 2], [1, P]],
                                          compare_op=ALU.is_gt, fill=0.0, base=0,
                                          channel_multiplier=-1)

            for n in range(2, 7):
                if n >= 3:
                    for hh in range(2):
                        pool.wait_ge(w_ready, 2 * (n - 3) + hh + 1)
                        keep_past(sp_w[:, hh, :]).then_inc(w_masked, 1)
                if n < 6:
                    for hh in range(2):
                        pool.wait_ge(l_ready, 2 * (n - 2) + hh + 1)
                        keep_past(sp_l[:, hh, :]).then_inc(l_masked, 1)

        @block.vector
        def _(dve):
            steps_done = [0]

            def link(ins):
                steps_done[0] += 1
                ins.then_inc(dve_step, 1)
                dve.wait_ge(dve_step, steps_done[0])

            def fold(ap):
                return ap.rearrange("p c t -> p (c t)")

            def mean_square(k):
                dve.wait_ge(sq_ready, k + 1)
                dve.tensor_scalar(st[:, 4 * k:4 * k + 2], st[:, 4 * k:4 * k + 2], 1.0 / D, EPS,
                                  ALU.mult, ALU.add).then_inc(ms_ready, 1)
                dve.wait_ge(rt_ready, k + 1)
                dve.reciprocal(st[:, 4 * k + 2:4 * k + 4],
                               st[:, 4 * k + 2:4 * k + 4]).then_inc(rinv_ready, 1)
                dve.wait_ge(rinv_ready, k + 1)

            def norm(k, src, dst):
                mean_square(k)
                for a in range(TT):
                    i = dve.tensor_scalar(dst[:, a, :], src[:, a, :], st[:, 4 * k + 2 + a:4 * k + 3 + a],
                                          None, ALU.mult)
                i.then_inc(xn_ready, 1)

            def low_of_unit(n, quarters):
                for q in quarters:
                    dve.wait_ge(high_ready, 4 * n + q + 1)
                    slot = n % DENSE_SLOTS
                    dve.tensor_tensor(quarter(n, slot, q), quarter(n, slot, q, ring),
                                      f32(quarter(n, HIGH_SLOT, q)),
                                      ALU.subtract).then_inc(low_ready, 1)

            def turned_to(high, low, k, g0):
                if k < 2:
                    dve.wait_ge(turned, 4 * k + 4)
                for p in range(4):
                    dve.wait_ge(turned_high, 4 * k + p + 1)
                    for c in range(2):
                        i = dve.scalar_tensor_tensor(
                            low[:, 2 * p + c, :], bank[2 + p][:, c * T:c * T + T],
                            gT[:, g0 + 2 * p + c:g0 + 2 * p + c + 1], f32(high[:, 2 * p + c, :]),
                            ALU.mult, ALU.subtract)
                    i.then_inc(turned_low, 1)

            def from_bank1(n, dst, scale=None):
                await_full(dve, n, 1)
                if scale is None:
                    dve.tensor_copy(dst, bank[1][:, :]).then_inc(bank1_read, 1)
                else:
                    dve.tensor_scalar(dst, bank[1][:, :], scale, None, ALU.mult).then_inc(bank1_read, 1)

            dve.wait_ge(small_in, 16 * 12)
            dve.tensor_copy(posf, posi[:, :]).then_inc(pos_ready, 1)
            for r in range(2):
                i = dve.tensor_tensor_reduce(scr[:, 4608 + HEAD * r:4608 + HEAD * r + HEAD],
                                             lamr[:, 2 * r, :], lamr[:, 2 * r + 1, :], 1.0, 0.0,
                                             ALU.mult, ALU.add, st[:, 80 + r:81 + r])
            i.then_inc(lam_dots, 1)
            dve.wait_ge(gain_rows_T, 1)
            dve.tensor_copy(gT[:, :], bank[6][:, 0:33])
            dve.tensor_copy(gperm[:, :].rearrange("p (u j) -> p j u", j=2),
                            bank[6][:, 40:48].rearrange("p (j u) -> p j u", j=2)).then_inc(gain_ready, 1)
            norm(0, xs, xn)
            dve.wait_ge(gain_ready, 1)
            dve.tensor_scalar(st[:, 88:89], gT[:, 32:33], 1.0 - LAMBDA_INIT, None, ALU.mult)
            turned_to(hT_high, hT_low, 0, 0)
            low_of_unit(0, range(4))

            for n in range(U_UPS):
                low_of_unit(n + 1, (0, 1, 2))
                if n == U_SBQ:
                    from_bank1(n, fold(qT[:, 2:4, :]), HEAD ** -0.5)
                elif n == U_SBK:
                    from_bank1(n, fold(kT[:, 2:4, :]))
                elif n == U_SBV:
                    from_bank1(n, vs[:, 1, :])
                elif n == U_DQ:
                    from_bank1(n, fold(raw[:, 0, 2:4, :]), HEAD ** -0.5)
                elif n == U_DK:
                    from_bank1(n, fold(raw[:, 1, 2:4, :]))
                elif n == U_DV:
                    from_bank1(n, vd[:, 1, :])
                elif n < U_MK:
                    g = n - U_GSB
                    from_bank1(n, fold(sg[:, g // 2, 4 * (g % 2) + 2:4 * (g % 2) + 4, :]))
                else:
                    from_bank1(n, fold(kTm[:, 4 * (n - U_MK) + 2:4 * (n - U_MK) + 4, :]))
                low_of_unit(n + 1, (3,))
                if n == 0:
                    dve.wait_ge(const_in, 16)
                    dve.wait_ge(pos_spread, 1)
                    link(dve.tensor_scalar(ang[:, T:2 * T], bank[7][:, 0:T], cst[:, C_INV:C_INV + 1], None,
                                           ALU.mult))
                    link(dve.tensor_scalar(angn[:, T:2 * T], ang[:, T:2 * T], 1.0 / (2 * math.pi), ROUNDER,
                                           ALU.mult, ALU.add))
                    link(dve.tensor_scalar(angn[:, 0:T], ang[:, T:2 * T], 1.0 / (2 * math.pi), 0.25,
                                           ALU.mult, ALU.add))
                    link(dve.tensor_scalar(angn[:, 0:T], angn[:, 0:T], ROUNDER, None, ALU.add))
                    link(dve.tensor_scalar(angn[:, :], angn[:, :], ROUNDER, None, ALU.subtract))
                    link(dve.scalar_tensor_tensor(ang[:, 0:T], angn[:, 0:T], -TWO_PI_A, ang[:, T:2 * T],
                                                  ALU.mult, ALU.add))
                    link(dve.scalar_tensor_tensor(ang[:, T:2 * T], angn[:, T:2 * T], -TWO_PI_A,
                                                  ang[:, T:2 * T], ALU.mult, ALU.add))
                    for part in (TWO_PI_B, TWO_PI_C):
                        link(dve.scalar_tensor_tensor(ang[:, :], angn[:, :], -part, ang[:, :], ALU.mult,
                                                      ALU.add))
                    link(dve.tensor_scalar(ang[:, 0:T], ang[:, 0:T], math.pi / 2, None, ALU.add))
                    dve.tensor_scalar(ang[:, :], ang[:, :], 3.1415925, -3.1415925, ALU.min,
                                      ALU.max).then_inc(ang_ready, 1)
                    norm(1, ms, ms)
                    dve.wait_ge(lam_exp, 1)
                    link(dve.tensor_tensor(st[:, 84:85], st[:, 83:84], st[:, 82:83], ALU.subtract))
                    dve.tensor_scalar(st[:, 84:85], st[:, 84:85], LAMBDA_INIT, None,
                                      ALU.subtract).then_inc(lam_ready, 1)
                if n == 1:
                    turned_to(hmT_high, hmT_low, 1, 16)
                if n in (4, 5):
                    if n == 4:
                        dve.wait_ge(rope_ready, 1)
                        dve.wait_ge(bank0_read, U_DQ + 1)
                    else:
                        dve.wait_ge(bank0_read, U_DK + 1)
                    cos2 = cosT.unsqueeze(1).to_broadcast([P, 2, T])
                    sin2 = sinT.unsqueeze(1).to_broadcast([P, 2, T])
                    for g in range(2):
                        rot = bank[6][:, :].rearrange("p (c t) -> p c t", c=2)
                        dve.tensor_tensor(rtmp[:, 0], raw[:, n - 4, 2 * g:2 * g + 2, :], cos2, ALU.mult)
                        dve.wait_ge(rot_full, 2 * (n - 4) + g + 1)
                        link(dve.tensor_tensor(rtmp[:, 1], rot, sin2, ALU.mult))
                        dve.tensor_tensor(dqk[:, n - 4, 2 * g:2 * g + 2, :], rtmp[:, 0], rtmp[:, 1],
                                          ALU.add).then_inc(rot_read, 1)
                        dve.wait_ge(rot_read, 2 * (n - 4) + g + 1)
                if 4 <= n < 8:
                    p = n - 4
                    dve.wait_ge(sbo_full, p + 1)
                    link(dve.tensor_copy(oT_high[:, p, :], bank[7][:, 0:T]))
                    dve.tensor_tensor(oT_low[:, p, :], bank[7][:, 0:T], f32(oT_high[:, p, :]),
                                      ALU.subtract).then_inc(sbo_read, 1)
                if 2 <= n < 6:
                    for hh in range(2):
                        h = 2 * (n - 2) + hh
                        dve.wait_ge(soft_ready, h + 1)
                        if n > 2:
                            dve.wait_ge(after_full, h - 1)
                        dve.scalar_tensor_tensor(sp_l[:, hh, :], bank[2 + 2 * ((n - 2) % 2) + hh][:, 0:384],
                                                 0.0, sp_t[:, hh, :], ALU.max, ALU.add).then_inc(l_ready, 1)
                if 8 <= n < 12:
                    h = n - 8
                    dve.wait_ge(do_full, h + 1)
                    dve.tensor_copy(od[:, :, P * h:P * h + P],
                                    bank[5][:, 0:T].rearrange("p (a d) -> p a d", a=TT)).then_inc(do_read, 1)
                if 6 <= n < 10:
                    h = n - 6
                    dve.wait_ge(dz_full, h + 1)
                    if h > 0:
                        dve.wait_ge(dexp_ready, h)
                    for c in range(2):
                        for a in range(TT):
                            k = 24 + 2 * c + a
                            cols = slice(0, P) if a == 0 else slice(P, P + T)
                            i = dve.tensor_reduce(st[:, k:k + 1], bank[2 + c][:, cols], AX, ALU.max,
                                                  negate=True)
                    i.then_inc(dmax_ready, 1)
                    dve.wait_ge(dexp_ready, h + 1)
                    link(dve.reciprocal(st[:, 32:36], st[:, 28:32]))
                    link(dve.tensor_scalar(st[:, 34:36], st[:, 34:36], st[:, 84:85], None, ALU.mult))
                    if h > 0:
                        dve.wait_ge(dpT_full, h)
                    for a in range(TT):
                        cols = slice(0, P) if a == 0 else slice(P, P + T)
                        link(dve.tensor_scalar(d_e[:, 0, cols], d_e[:, 0, cols], st[:, 32 + a:33 + a],
                                               None, ALU.mult))
                        i = dve.scalar_tensor_tensor(d_p[:, cols], d_e[:, 1, cols],
                                                     st[:, 34 + a:35 + a], d_e[:, 0, cols], ALU.mult,
                                                     ALU.add)
                    i.then_inc(dp_ready, 1)
            dve.wait_ge(dsq_ready, DIFF_HEADS)
            dve.tensor_scalar(st[:, 40:48], st[:, 40:48], 1.0 / P, EPS, ALU.mult,
                              ALU.add).then_inc(dms_ready, 1)
            dve.wait_ge(drt_ready, 1)
            link(dve.reciprocal(st[:, 48:56], st[:, 48:56]))
            for h in range(DIFF_HEADS):
                for a in range(TT):
                    i = dve.tensor_scalar(odn[:, a, P * h:P * h + P], od[:, a, P * h:P * h + P],
                                          st[:, 48 + 2 * h + a:49 + 2 * h + a], None, ALU.mult)
            i.then_inc(don_ready, 1)

            def gated(n, g):
                for b in range(2):
                    part = fold(sg[:, n - U_UPS, 4 * g + 2 * b:4 * g + 2 * b + 2, :])
                    await_full(dve, n, b, g)
                    dve.tensor_tensor(part, bank[b][:, :], part, ALU.mult).then_inc(
                        (bank0_read, bank1_read)[b], 1)

            def mixed(g):
                first, second = (fold(sg[:, n, 4 * g:4 * g + 4, :]) for n in range(2))
                for read in (bank0_read, bank1_read):
                    dve.wait_ge(read, use(U_UPD, g) + 1)
                dve.tensor_tensor(first, first, second, ALU.add).then_inc(mixed_sum, 1)
                dve.wait_ge(mixed_rounded, g + 1)
                dve.tensor_tensor(fold(mixed_low[:, 4 * g:4 * g + 4, :]), first,
                                  f32(fold(mixed_high[:, 4 * g:4 * g + 4, :])),
                                  ALU.subtract).then_inc(mixed_ready, 1)

            dve.wait_ge(gate_ready, 1)
            gated(U_UPS, 0)
            low_of_unit(U_UPD, (0, 1))
            for g in range(2):
                dve.wait_ge(doT_high, g + 1)
                dve.scalar_tensor_tensor(fold(oT_low[:, 4 + 2 * g:6 + 2 * g, :]), bank[4 + 2 * g][:, :],
                                         st[:, 88:89], f32(fold(oT_high[:, 4 + 2 * g:6 + 2 * g, :])), ALU.mult,
                                         ALU.subtract).then_inc(doT_read, 1)
            gated(U_UPS, 1)
            low_of_unit(U_UPD, (2, 3))
            gated(U_UPD, 0)
            low_of_unit(U_OUT, (0,))
            mixed(0)
            low_of_unit(U_OUT, (1,))
            gated(U_UPD, 1)
            mixed(1)
            low_of_unit(U_OUT, (2, 3))

            def add_to_x(n, b):
                await_full(dve, n, b)
                g = (n - U_OUT) % 2
                part = xs[:, b, HALF * g:HALF * g + HALF]
                dve.tensor_tensor(part, bank[b][:, :], part, ALU.add).then_inc(
                    (bank0_read, bank1_read)[b], 1)

            add_to_x(U_OUT, 0)
            low_of_unit(U_OUT + 1, (0, 1, 2, 3))
            add_to_x(U_OUT, 1)
            add_to_x(U_OUT + 1, 0)
            low_of_unit(U_MQ, (0, 1, 2, 3))
            add_to_x(U_OUT + 1, 1)
            turned_to(hT_high, hT_low, 2, 8)
            mean_square(2)
            for n in (U_MQ, U_MQ + 1):
                low_of_unit(n + 1, (0, 1, 2))
                from_bank1(n, fold(oT[:, 4 * (n - U_MQ) + 2:4 * (n - U_MQ) + 4, :]), MEM_HEAD ** -0.5)
                low_of_unit(n + 1, (3,))

            def mem_max(h):
                dve.wait_ge(mz_full, h + 1)
                k = 60 + 4 * (h % 2)
                for a in range(TT):
                    i = dve.tensor_reduce(st[:, k + a:k + a + 1], bank[2 + 2 * (h % 2) + a][:, 0:T], AX,
                                          ALU.max, negate=True)
                link(i)
                dve.tensor_tensor(st[:, k:k + 2], st[:, k:k + 2], st[:, 10:12],
                                  ALU.mult).then_inc(mmax_ready, 1)

            def mem_probs(h):
                k = 60 + 4 * (h % 2)
                dve.wait_ge(mexp_ready, h + 1)
                to = 70 + 2 * (h % 2)
                link(dve.reciprocal(st[:, to:to + 2], st[:, k + 2:k + 4]))
                for a in range(TT):
                    i = dve.tensor_scalar(m_p[:, h % 2, a, :], m_p[:, h % 2, a, :],
                                          st[:, to + a:to + a + 1], None, ALU.mult)
                i.then_inc(mp_ready, 1)

            def mem_out(h):
                dve.wait_ge(mo_high, h + 1)
                dve.tensor_tensor(fold(hT_low[:, 2 * h:2 * h + 2, :]), bank[MEM_O[h]][:, :],
                                  f32(fold(hT_high[:, 2 * h:2 * h + 2, :])), ALU.subtract).then_inc(mo_read, 1)

            mem_max(0)
            mem_max(1)
            mem_probs(0)
            mem_probs(1)
            low_of_unit(U_MV + 1, (0, 1, 2, 3))
            from_bank1(U_MV, vm[:, 1, 0:HALF])
            mem_max(2)
            mem_out(0)
            mem_max(3)
            mem_probs(2)
            mem_out(1)
            mem_probs(3)
            low_of_unit(U_MO, (0, 1, 2, 3))
            from_bank1(U_MV + 1, vm[:, 1, HALF:D])
            mem_out(2)
            mem_out(3)
            add_to_x(U_MO, 0)
            low_of_unit(U_MO + 1, (0, 1, 2, 3))
            add_to_x(U_MO, 1)
            add_to_x(U_MO + 1, 0)
            add_to_x(U_MO + 1, 1)
            for p in (1, 3):
                dve.wait_ge(turned, 12 + p + 1)
                for c in range(2 * p, 2 * p + 2):
                    i = dve.tensor_scalar(hT[:, c, :], bank[2 + p][:, (c % 2) * T:(c % 2) * T + T],
                                          gT[:, 24 + c:25 + c], None, ALU.mult)
                i.then_inc(turned_low, 1)
            mean_square(3)
            dve.wait_ge(late_in, 16 * 8)

            dve.wait_ge(logit_full, 1)
            for a in range(TT):
                i = dve.scalar_tensor_tensor(lg[:, a, :], bank[6][:, a * E:a * E + E],
                                             st[:, 14 + a:15 + a], brow, ALU.mult, ALU.add)
            link(i)
            for a in range(TT):
                i = dve.max(topv[:, a, :], lg[:, a, :])
            link(i)
            link(dve.tensor_scalar(few[:, 0:2], topv[:, :, 0], -1.0, None, ALU.mult))
            for a in range(TT):
                i = dve.max_index(topi[:, a, :], topv[:, a, :], lg[:, a, :])
            i.then_inc(top_ready, 1)
            dve.wait_ge(top_ready, 1)
            link(dve.tensor_copy(topf, topi[:, :, :]))
            iota = cst[:, C_IOTA:C_IOTA + E]
            for a in range(TT):
                link(dve.tensor_scalar(chosen[:, a, :], iota, topf[:, a, 0:1], None, ALU.is_equal))
                for k in range(1, TOP_K):
                    i = dve.scalar_tensor_tensor(chosen[:, a, :], iota, topf[:, a, k:k + 1],
                                                 chosen[:, a, :], ALU.is_equal, ALU.add)
                    if k < TOP_K - 1:
                        link(i)
                if a < TT - 1:
                    link(i)
            i.then_inc(chosen_ready, 1)
            dve.wait_ge(gexp_ready, 1)
            link(dve.reciprocal(few[:, 4:6], few[:, 2:4]))
            for a in range(TT):
                link(dve.tensor_scalar(tope[:, a, :], tope[:, a, :], few[:, 4 + a:5 + a], None, ALU.mult))
                link(dve.tensor_scalar(gates[:, a, :], iota, topf[:, a, 0:1], tope[:, a, 0:1],
                                       ALU.is_equal, ALU.mult))
                for k in range(1, TOP_K):
                    link(dve.tensor_scalar(hotg, iota, topf[:, a, k:k + 1], tope[:, a, k:k + 1],
                                           ALU.is_equal, ALU.mult))
                    link(dve.tensor_tensor(gates[:, a, :], gates[:, a, :], hotg, ALU.add))
                link(dve.tensor_copy(gate_of[:, a, :].rearrange("p (r e) -> p r e", e=E),
                                     gates[:, a, :].unsqueeze(1).to_broadcast([P, ROUNDS, E])))
            dve.wait_ge(rank_full, 1)
            for a in range(TT):
                link(dve.scalar_tensor_tensor(hot, bank[7][:, a * E:a * E + E], NOT_CHOSEN,
                                              chosen[:, a, :], ALU.add, ALU.mult))
                link(dve.scalar_tensor_tensor(
                    slot_of[:, a, :].rearrange("p (r e) -> p r e", e=E),
                    hot.unsqueeze(1).to_broadcast([P, ROUNDS, E]), NOT_CHOSEN,
                    cst[:, C_R64:C_R64 + ROUNDS * E].rearrange("p (r e) -> p r e", e=E),
                    ALU.subtract, ALU.subtract))
            link(dve.tensor_reduce(few[:, 6:7], bank[7][:, 2 * E:3 * E], AX, ALU.max))
            for r in range(1, ROUNDS):
                i = dve.tensor_scalar(few[:, 6 + r:7 + r], few[:, 6:7], float(SLOTS * r),
                                      float(E // STEPS), ALU.is_gt, ALU.mult)
            link(i)
            link(dve.tensor_reduce(few[:, 10:11], few[:, 7:10], AX, ALU.add))
            dve.tensor_scalar(middle_count[0:1, 0:1], few[0:1, 10:11], float(E // STEPS - 2), None,
                              ALU.add).then_inc(route_ready, 1)

            def col(ap, i):
                return ap[:, bass.ds(i, 1)]

            def picks(i, j):
                for a in range(TT):
                    ins = dve.tensor_scalar(pick[:, a, :], cst[:, C_SLOT:C_SLOT + SLOTS],
                                            col(slot_of[:, a, :], i), None, ALU.is_equal)
                ins.then_inc(pick_ready, 1)
                dve.tensor_scalar(esel[:, j % 4, :], cst[:, C_BLK:C_BLK + 4],
                                  col(cst[:, C_EIDX:C_EIDX + ROUNDS * E], i), None,
                                  ALU.is_equal).then_inc(esel_ready, 1)

            def gathered(i, j):
                dve.wait_ge(xe_full, i + 1)
                dve.tensor_tensor(xe[:, j % 2], bank[4][:, :].rearrange("p (k s) -> p k s", k=KC),
                                  gperm[:, :].unsqueeze(2).to_broadcast([P, KC, SLOTS]),
                                  ALU.mult).then_inc(xe_ready, 1)

            def add_spread(a):
                for h in range(2):
                    part = xs[:, a, HALF * h:HALF * h + HALF]
                    ins = dve.tensor_tensor(part, bank[6 + h][:, :], part, ALU.add)
                ins.then_inc(added, 1)

            def step(b, j, i, prev, cur, nxt, nxt2):
                if prev:
                    dve.wait_ge(spread_full, 2 * i - 1)
                    add_spread(0)
                if nxt2:
                    picks(i + 2, j + 2)
                if nxt:
                    if cur:
                        dve.wait_ge(comb_full, i + 1)
                    for a in range(TT):
                        ins = dve.tensor_scalar(pickg[:, a, :], cst[:, C_SLOT:C_SLOT + P],
                                                col(slot_of[:, a, :], i + 1),
                                                col(gate_of[:, a, :], i + 1), ALU.is_equal, ALU.mult)
                    ins.then_inc(pickg_ready, 1)
                if prev:
                    dve.wait_ge(spread_full, 2 * i)
                    add_spread(1)
                if nxt:
                    dve.wait_ge(expert_used, 6 * i + 8 if cur else 4)
                    dve.tensor_scalar(glu, bank[0][:, :], LIMIT, None, ALU.min).then_inc(glu_ready, 1)
                    dve.tensor_scalar(lin, bank[1][:, :], LIMIT, -LIMIT, ALU.min, ALU.max)
                    if nxt2:
                        gathered(i + 2, j + 2)
                    dve.wait_ge(sig_ready, i + 2)
                    dve.tensor_tensor(glu, glu, sig, ALU.mult).then_inc(gated_ready, 1)
                    dve.wait_ge(gated_ready, i + 2)
                    dve.scalar_tensor_tensor(act, lin, 1.0, glu, ALU.add, ALU.mult).then_inc(act_ready, 1)

            dve.wait_ge(route_ready, 1)
            picks(0, 0)
            gathered(0, 0)
            step(0, -1, -1, False, False, True, True)
            for j in range(STEPS):
                step(0, j, j, j > 0, True, True, True)
            middle = dve.value_load(middle_count[0:1, 0:1], min_val=E // STEPS - 2,
                                   max_val=ROUNDS * E // STEPS - 2)
            with dve.Fori(1, middle + 1) as b:
                for j in range(STEPS):
                    step(b, j, STEPS * b + j, True, True, True, True)
            b = middle + 1
            for j in range(STEPS):
                step(b, j, STEPS * b + j, True, True, j < STEPS - 1, j < STEPS - 2)
            n = STEPS * b + STEPS
            for a in range(TT):
                dve.wait_ge(spread_full, 2 * n - 1 + a)
                add_spread(a)
            mean_square(4)
            dve.wait_ge(late_in, 16 * 8)
            for a in range(TT):
                i = dve.scalar_tensor_tensor(xn[:, a, :], xs[:, a, :], st[:, 18 + a:19 + a], gfin,
                                             ALU.mult, ALU.mult)
            i.then_inc(xn_ready, 2)


_INS = ["x", "mem", "positions", "norm_mix", "w_in", "lambda_q1", "lambda_k1", "lambda_q2",
        "lambda_k2", "diff_subln", "w_up_sb", "w_up_diff", "w_out", "norm_mem_q", "norm_mem_kv",
        "w_mem_q", "w_mem_kv", "w_mem_o", "norm_ffn", "w_router", "b_router", "w_gate_up",
        "b_gate_up", "w_down", "b_down", "norm_final"]


def kernel(**inputs):
    import concourse.bacc as bacc
    from concourse.bass_utils import run_bass_kernel_spmd

    nc = bacc.Bacc("TRN2", target_bir_lowering=False, num_devices=1)
    arrays = {"in_consts": constants()}
    arrays.update((f"in_{name}", np.ascontiguousarray(inputs[name])) for name in _INS)
    args = [nc.dram_tensor(name, a.shape, mybir.dt.from_np(a.dtype), kind="ExternalInput").ap()
            for name, a in arrays.items()]
    out = nc.dram_tensor("out", (1, T, D), F32, kind="ExternalOutput").ap()
    layer(nc, *args, out)
    return run_bass_kernel_spmd(nc, [arrays], core_ids=[0]).results[0]["out"]
```

```python
import math
from contextlib import ExitStack

import numpy as np

import concourse.bass as bass
from concourse import mybir

F32 = mybir.dt.float32
F32R = mybir.dt.float32r
I32 = mybir.dt.int32
U32 = mybir.dt.uint32
ALU = mybir.AluOpType
ACT = mybir.ActivationFunctionType
AX = mybir.AxisListType.X

P = 128
D = 1024
T = 256
TT = T // P
KC = D // P
HALF = 512
CHUNK = 64
EPS = 1e-6
SB_HEADS, DIFF_HEADS, MEM_HEADS = 8, 4, 4
HEAD = 64
MEM_HEAD = D // MEM_HEADS
LAMBDA_INIT = 0.8 - 0.6 * math.exp(0.0)
E = 32
TOP_K = 4
SLOTS = 64
ROUNDS = T // SLOTS
LIMIT, ALPHA = 7.0, 1.702
NOT_CHOSEN = 1024.0
STEPS = 4

(U_SBQ, U_SBK, U_SBV, U_DQ, U_DK, U_DV, U_GSB, _, U_GDF, _, U_MK, _,
 U_UPS, U_UPD, U_OUT, _, U_MQ, _, U_MV, _, U_MO, _) = range(22)
UNITS = 22
RING = 8
UNIT = 4096
DENSE_SLOTS = 3
HIGH_SLOT = 3
QUARTER = UNIT // 4
MEM_PT, MEM_O = (6, 6, 6, 2), (7, 7, 7, 3)
MOE_SLOT = [5, 6, 7, 1, 4, 2, 0, 3]

C_ID, C_ONE, C_NTRI, C_NONE, C_ROT, C_STRI, C_SLOT, C_DMASK = (P * i for i in range(8))
C_IOTA = 8 * P
C_EIDX = C_IOTA + E
C_R64 = C_EIDX + ROUNDS * E
C_BLK = C_R64 + ROUNDS * E
C_INV = C_BLK + 4
C_COLS = C_INV + 1

TWO_PI_A = 6.28125
TWO_PI_B = float(np.float32(2 * math.pi - TWO_PI_A) // 2.0 ** -20 * 2.0 ** -20)
TWO_PI_C = float(np.float32(2 * math.pi - TWO_PI_A - TWO_PI_B))
ROUNDER = 1.5 * 2.0 ** 23


def constants():
    c = np.zeros((P, C_COLS), np.float32)
    p = np.arange(P)
    c[:, C_ID:C_ID + P] = np.eye(P)
    c[:, C_NTRI:C_NTRI + P] = -(p[:, None] >= p[None, :]).astype(np.float32)
    c[:, C_NONE:C_NONE + P] = -1.0
    for m in range(P):
        if m % HEAD < HEAD // 2:
            c[m + HEAD // 2, C_ROT + m] = -1.0
        else:
            c[m - HEAD // 2, C_ROT + m] = 1.0
    c[:, C_STRI:C_STRI + P] = p[:, None] < p[None, :]
    c[:, C_ONE:C_ONE + P] = 1.0
    c[:, C_SLOT:C_SLOT + P] = p[None, :] % SLOTS
    c[:, C_DMASK:C_DMASK + P] = np.where(p[None, :] // CHUNK > p[:, None] // CHUNK, -1e30, 0.0)
    c[:, C_IOTA:C_IOTA + E] = np.arange(E)
    i = np.arange(ROUNDS * E)
    c[:, C_EIDX:C_EIDX + ROUNDS * E] = i % E
    c[:, C_R64:C_R64 + ROUNDS * E] = SLOTS * (i // E)
    c[:, C_BLK:C_BLK + 4] = p[:, None] - 32 * np.arange(4)[None, :]
    half = HEAD // 2
    c[:, C_INV] = np.float32(10000.0) ** (-(p % half).astype(np.float32) / np.float32(half))
    return c


def kind(n):
    if n in (U_UPS, U_UPD):
        return "U"
    return "N" if n in (U_SBV, U_DV, U_OUT, U_OUT + 1, U_MV, U_MV + 1, U_MO, U_MO + 1) else "T"


def use(n, g=0):
    return n + g + min(max(n - U_UPS, 0), 2)


def layer(nc, consts, x, mem, positions, norm_mix, w_in, lambda_q1, lambda_k1, lambda_q2,
          lambda_k2, diff_subln, w_up_sb, w_up_diff, w_out, norm_mem_q, norm_mem_kv, w_mem_q,
          w_mem_kv, w_mem_o, norm_ffn, w_router, b_router, w_gate_up, b_gate_up, w_down, b_down,
          norm_final, out):
    ctx = ExitStack()

    def sb(name, shape, dt=F32):
        return ctx.enter_context(nc.sbuf_tensor(name, shape, dt))

    def sb_split(name, shape, slots=1):
        at = -(-nc.sbuf_base // 32) * 32
        size = 4 * int(np.prod(shape[1:])) // slots
        whole = sb(name, shape)
        split = [nc.alloc_sbuf_tensor_at(f"{name}_split{i}", shape if slots == 1 else [P, *shape[2:]],
                                         F32R, offset=at + size * i).ap() for i in range(slots)]
        return whole, split if slots > 1 else split[0]

    def sem(name):
        return ctx.enter_context(nc.semaphore(name))

    with ctx:
        ring, ring_split = sb_split("ring", [P, RING, UNIT], RING)
        cst = sb("cst", [P, C_COLS])
        xs = sb("xs", [P, TT, D])
        xn, xn_split = sb_split("xn", [P, TT, D])
        extra_at = -(-nc.sbuf_base // 32) * 32
        hT, hT_split = sb_split("hT", [P, KC, T])
        oT, oT_split = sb_split("oT", [P, KC, T])
        extra = nc.alloc_sbuf_tensor_at("extra", [P, UNIT], F32, offset=extra_at).ap()
        kTm = sb("kTm", [P, KC, T])
        vm = sb("vm", [P, TT, D])
        scr = sb("scr", [P, 5632])
        wr = sb("wr", [P, KC, E])
        mask_split = ctx.enter_context(nc.sbuf_tensor("mask_split", [P, 2, P], F32R))
        gT = sb("gT", [P, 33])
        gperm = sb("gperm", [P, KC])
        st = sb("st", [P, 96])
        middle_count = sb("middle_count", [1, 2], I32)
        topi = sb("topi", [P, TT, 8], U32)

        def region(slot, at, n):
            return ring[:, slot, at:at + n]

        ms = region(4, 2048, 2048).rearrange("p (a d) -> p a d", a=TT)
        qT = region(5, 0, 1024).rearrange("p (c t) -> p c t", c=4)
        kT = region(5, 1024, 1024).rearrange("p (c t) -> p c t", c=4)
        vs = region(5, 2048, 1024).rearrange("p (a d) -> p a d", a=TT)
        vd = region(5, 3072, 1024).rearrange("p (a d) -> p a d", a=TT)
        dqk = region(6, 0, 2048).rearrange("p (n c t) -> p n c t", n=2, c=4)
        raw = region(6, 2048, 2048).rearrange("p (n c t) -> p n c t", n=2, c=4)
        sg = ring[:, 7, :].rearrange("p (n k t) -> p n k t", n=2, k=KC)

        def f32(ap):
            return ap.bitcast(F32)

        hT_high = hT_split
        hT_low = xn_split.rearrange("p a (k t) -> p (a k) t", t=T)
        hmT_high = ring_split[4][:, 0:2048].rearrange("p (k t) -> p k t", k=KC)
        hmT_low = ring_split[4][:, 2048:4096].rearrange("p (k t) -> p k t", k=KC)
        oT_high = oT_split
        rT = oT
        oT_low = ring_split[5][:, 0:2048].rearrange("p (k t) -> p k t", k=KC)
        mixed_low, mixed_high = (ring_split[7][:, 2048 * n:2048 * n + 2048]
                                 .rearrange("p (k t) -> p k t", k=KC) for n in range(2))

        def quarter(n, slot, q, whole=None):
            w = ring_split[slot] if whole is None else whole[:, slot, :]
            if slot == HIGH_SLOT:
                w = w[:, QUARTER * q:QUARTER * q + QUARTER]
                return w.rearrange("p (k n) -> p k n", k={"T": KC, "N": 2, "U": 4}[kind(n)])
            if kind(n) == "U":
                return w.rearrange("p (k n) -> p k n", k=4)[:, :, T * q:T * q + T]
            w = w.rearrange("p (k n) -> p k n", k=KC)
            return w[:, :, P * q:P * q + P] if kind(n) == "T" else w[:, 2 * q:2 * q + 2, :]

        lamr = scr[:, 4736:4992].rearrange("p (r d) -> p r d", r=4)
        gffn = scr[0:4, 4992:5248]
        posi = scr[0:1, 5248:5504].bitcast(I32)
        grows = scr[0:33, 5504:5632]
        sp_t = scr[:, 0:768].rearrange("p (h n) -> p h n", h=2)
        sp_l = scr[:, 768:1536].rearrange("p (h n) -> p h n", h=2)
        sp_w = scr[:, 1536:2304].rearrange("p (h n) -> p h n", h=2)
        cosT = scr[:, 2304:2560]
        sinT = scr[:, 2560:2816]
        ang = scr[:, 2816:3328]
        angn = scr[:, 3328:3840]
        rtmp = scr[:, 2816:3840].rearrange("p (a c t) -> p a c t", a=2, c=2)
        d_e = scr[:, 3840:4608].rearrange("p (c n) -> p c n", c=2)
        d_p = scr[:, 4608:4992]
        d_pT = scr[:, 4992:5376]
        od = scr[:, 0:1024].rearrange("p (a d) -> p a d", a=TT)
        odn = scr[:, 1024:2048].rearrange("p (a d) -> p a d", a=TT)
        m_p = scr[:, 0:1024].rearrange("p (g a m) -> p g a m", g=2, a=TT)
        m_pT = scr[:, 1024:2048].rearrange("p (g m t) -> p g m t", g=2, m=TT)
        xe = scr[:, 0:1024].rearrange("p (g t h s) -> p g t h s", g=2, t=4, h=2)
        glu = scr[:, 1024:1536]
        lin = scr[:, 1536:2048]
        sig = scr[:, 2048:2560]
        act = scr[:, 2560:3072]
        actT = scr[:, 3072:3584]
        yb = scr[:, 3584:4096]
        comb = scr[:, 4096:4608].rearrange("p (g t) -> p g t", g=2)
        pick = scr[:, 4608:4736].rearrange("p (a s) -> p a s", a=TT)
        pickg = scr[:, 4736:4992].rearrange("p (a s) -> p a s", a=TT)
        xg = scr[:, 5120:5632]
        esel = scr[:, 4992:5008].rearrange("p (g b) -> p g b", g=4)
        same = scr[:, 2048:2304].rearrange("p (a k e) -> p a k e", a=TT, k=TOP_K)
        gfin = hT[:, 0:4, :].rearrange("p k t -> p (k t)")
        bgu = vm[:, 0, 0:HALF]
        bdn = vm[:, 0, HALF:2 * HALF]
        slot_of = vm[:, 1, 0:256].rearrange("p (a i) -> p a i", a=TT)
        gate_of = vm[:, 1, 256:512].rearrange("p (a i) -> p a i", a=TT)
        lg = vm[:, 1, 512:576].rearrange("p (a e) -> p a e", a=TT)
        chosen = vm[:, 1, 576:640].rearrange("p (a e) -> p a e", a=TT)
        gates = vm[:, 1, 640:704].rearrange("p (a e) -> p a e", a=TT)
        hot = vm[:, 1, 704:768]
        topv = vm[:, 1, 800:816].rearrange("p (a k) -> p a k", a=TT)
        topf = vm[:, 1, 816:832].rearrange("p (a k) -> p a k", a=TT)
        tope = vm[:, 1, 832:840].rearrange("p (a k) -> p a k", a=TT)
        few = vm[:, 1, 840:856]
        brow = vm[:, 1, 856:888]

        ident = cst[:, C_ID:C_ID + P]
        ones = cst[:, C_ONE:C_ONE + P]
        one = cst[:, C_ONE:C_ONE + 1]
        posf = scr[0:1, 3840:4096]

        bank = [ctx.enter_context(nc.psum_tensor(f"bank{i}", [P, HALF], F32)) for i in range(8)]

        ident_in, const_in = sem("ident_in"), sem("const_in")
        gains_in, small_in, router_in = sem("gains_in"), sem("small_in"), sem("router_in")
        first_in = [sem(f"first_in{q}") for q in range(4)]
        x_in = [sem(f"x_in{a}") for a in range(TT)]
        mem_in, late_in = sem("mem_in"), sem("late_in")
        unit_in = [sem(f"unit_in{k}") for k in range(DENSE_SLOTS)]
        high_ready, low_ready, quarter_used = sem("high_ready"), sem("low_ready"), sem("quarter_used")
        expert_in = [sem(f"expert_in{k}") for k in range(RING)]
        extra_in, final_gain_in = sem("extra_in"), sem("final_gain_in")
        expert_used = sem("expert_used")
        out_done = sem("out_done")
        dve_step, act_step, filler_ready = sem("dve_step"), sem("act_step"), sem("filler_ready")
        mask_ready = sem("mask_ready")
        gain_rows_T, gain_ready = sem("gain_rows_T"), sem("gain_ready")
        pos_ready, pos_spread, ang_ready, rope_ready = (
            sem("pos_ready"), sem("pos_spread"), sem("ang_ready"), sem("rope_ready"))
        lam_dots, lam_exp = sem("lam_dots"), sem("lam_exp")
        sq_ready, ms_ready, rt_ready, xn_ready = (
            sem("sq_ready"), sem("ms_ready"), sem("rt_ready"), sem("xn_ready"))
        turned, turned_high, turned_low = sem("turned"), sem("turned_high"), sem("turned_low")
        rinv_ready = sem("rinv_ready")
        tile0_full, bank0_read, bank1_read = sem("tile0_full"), sem("bank0_read"), sem("bank1_read")
        rot_full, rot_read = sem("rot_full"), sem("rot_read")
        z_full, soft_ready, l_ready, l_masked = (
            sem("z_full"), sem("soft_ready"), sem("l_ready"), sem("l_masked"))
        after_full, w_ready, w_masked = sem("after_full"), sem("w_ready"), sem("w_masked")
        sbo_full, sbo_read = sem("sbo_full"), sem("sbo_read")
        dz_full, dmax_ready, dexp_ready, dp_ready = (
            sem("dz_full"), sem("dmax_ready"), sem("dexp_ready"), sem("dp_ready"))
        dpT_full, dpT_read, do_full, do_read = (
            sem("dpT_full"), sem("dpT_read"), sem("do_full"), sem("do_read"))
        dsq_ready, dms_ready, drt_ready, don_ready = (
            sem("dsq_ready"), sem("dms_ready"), sem("drt_ready"), sem("don_ready"))
        doT_full, doT_high, doT_read = sem("doT_full"), sem("doT_high"), sem("doT_read")
        gate_ready, mixed_sum, mixed_rounded, mixed_ready = (
            sem("gate_ready"), sem("mixed_sum"), sem("mixed_rounded"), sem("mixed_ready"))
        mz_full, mmax_ready, mexp_ready, mp_ready = (
            sem("mz_full"), sem("mmax_ready"), sem("mexp_ready"), sem("mp_ready"))
        mpT_full, mpT_read, mo_full, mo_high, mo_read = (
            sem("mpT_full"), sem("mpT_read"), sem("mo_full"), sem("mo_high"), sem("mo_read"))
        logit_full, top_ready, gexp_ready, chosen_ready = (
            sem("logit_full"), sem("top_ready"), sem("gexp_ready"), sem("chosen_ready"))
        rank_full, count_full, route_ready = sem("rank_full"), sem("count_full"), sem("route_ready")
        pick_ready, pickg_ready, esel_ready = sem("pick_ready"), sem("pickg_ready"), sem("esel_ready")
        xg_full, xg_ready, xe_full, xe_ready = (
            sem("xg_full"), sem("xg_ready"), sem("xe_full"), sem("xe_ready"))
        glu_ready, sig_ready, gated_ready, act_ready = (
            sem("glu_ready"), sem("sig_ready"), sem("gated_ready"), sem("act_ready"))
        actT_full, actT_ready = sem("actT_full"), sem("actT_ready")
        comb_full, comb_ready, y_ready = sem("comb_full"), sem("comb_ready"), sem("y_ready")
        spread_full, added = sem("spread_full"), sem("added")

        block = ctx.enter_context(nc.Block())


        def expert_unit(b, m):
            if isinstance(b, int) and m == 8:
                return extra, extra_in, 16
            k = m if isinstance(b, int) and m < 8 else m - 1
            slot = MOE_SLOT[k % 8]
            return ring[:, slot, :], expert_in[slot], 48 * b + 16 * (k // 8 + 1)

        def await_full(eng, n, b, g=0):
            if kind(n) == "N" and b == 0:
                eng.wait_ge(tile0_full, sum(kind(m) == "N" for m in range(n + 1)))
            else:
                eng.wait_ge(quarter_used, 4 * n + (2 * g + b + 1 if kind(n) == "U" else 2 * b + 2))

        def turned_rest(eng, p, a, done):
            eng.wait_ge(turned, 13 + 2 * a + p)
            for c in range(2):
                to = rT[:, 2 * p + c, a * P:a * P + P]
                src = bank[2 + p][:, c * T + a * P:c * T + a * P + P]
                gain = gT[:, 24 + 2 * p + c:25 + 2 * p + c]
                if p == 2:
                    i = eng.activation(to, src, ACT.Copy, scale=gain)
                else:
                    i = eng.tensor_scalar(to, src, gain, None, ALU.mult)
            i.then_inc(done, 1)

        @block.sync
        def _(sp):
            def first_quarter(q):
                sp.dma_start(ring[:, 0, :].rearrange("p (k n) -> p k n", k=KC)[:, :, P * q:P * q + P],
                             w_in[0].rearrange("(k p) n -> p k n", p=P)[:, :, P * q:P * q + P]
                             ).then_inc(first_in[q], 16)

            for a in range(TT):
                sp.dma_start(xs[:, a, :], x[0, P * a:P * a + P, :]).then_inc(x_in[a], 16)
            sp.dma_start(cst[:, 0:2 * P], consts[:, 0:2 * P]).then_inc(ident_in, 16)
            first_quarter(0)
            for r, g in enumerate((norm_mix, norm_mem_q, norm_mem_kv, norm_ffn)):
                sp.dma_start(grows[8 * r:8 * r + 8, :],
                             g.rearrange("a (k p) -> (a k) p", p=P)).then_inc(gains_in, 16)
            sp.dma_start(grows[32:33, :], diff_subln).then_inc(gains_in, 16)
            sp.dma_start(gffn[:, :], norm_ffn.rearrange("a (u n) -> (a u) n", u=4)
                         ).then_inc(gains_in, 16)
            first_quarter(1)
            sp.dma_start(posi[:, :], positions).then_inc(small_in, 16)
            for r, g in enumerate((lambda_q1, lambda_k1, lambda_q2, lambda_k2)):
                sp.dma_start(lamr[:, r, :], g.partition_broadcast(P)
                             .rearrange("p a d -> p (a d)")).then_inc(small_in, 16)
            first_quarter(2)
            first_quarter(3)
            sp.dma_start(cst[:, 2 * P:], consts[:, 2 * P:]).then_inc(const_in, 16)

            def by_columns(w, c0):
                return w.rearrange("(k p) n -> p k n", p=P)[:, :, c0:c0 + HALF]

            def load_gate_up(b, m, e, q):
                to, arrived, _ = expert_unit(b, m)
                sp.dma_start(to, w_gate_up[0, e, 256 * q:256 * q + 256, :]
                             .rearrange("(p j) n -> p (j n)", j=2)).then_inc(arrived, 16)

            def load_down(b, m, e, q):
                to, arrived, _ = expert_unit(b, m)
                sp.dma_start(to, w_down[0, e, HALF * q:HALF * q + HALF, :]
                             .rearrange("(p j) n -> p (j n)", j=4)).then_inc(arrived, 16)

            def await_place(b, m):
                if isinstance(b, int) and m < 8:
                    sp.wait_ge(quarter_used, 4 * (20, 21, 22, 22)[m - 4])
                elif isinstance(b, int) and m == 8:
                    sp.wait_ge(logit_full, 1)
                else:
                    sp.wait_ge(expert_used, 24 * b + (m - 8 if isinstance(b, int) and m <= 16 else m - 7))

            for n in range(UNITS):
                if n < U_MK:
                    src = by_columns(w_in[0], HALF * n)
                elif n < U_UPS:
                    src = by_columns(w_mem_kv[0], HALF * (n - U_MK))
                elif n < U_OUT:
                    src = (w_up_sb if n == U_UPS else w_up_diff)[0].rearrange("(k p) n -> p k n", p=P)
                elif n < U_MQ:
                    src = by_columns(w_out[0], HALF * (n - U_OUT))
                elif n < U_MV:
                    src = by_columns(w_mem_q[0], HALF * (n - U_MQ))
                elif n < U_MO:
                    src = by_columns(w_mem_kv[0], D + HALF * (n - U_MV))
                else:
                    src = by_columns(w_mem_o[0], HALF * (n - U_MO))
                if n >= DENSE_SLOTS:
                    sp.wait_ge(quarter_used, 4 * (n - DENSE_SLOTS + 1))
                dst = ring[:, n % DENSE_SLOTS, :].rearrange("p (k n) -> p k n", k=src.shape[1])
                if n > 0:
                    sp.dma_start(dst, src).then_inc(unit_in[n % DENSE_SLOTS], 16)
                if n == 4:
                    sp.dma_start(wr[:, :, :], w_router[0].rearrange("(k p) e -> p k e", p=P)
                                 ).then_inc(router_in, 16)
                if n == 1:
                    sp.dma_start(ms[:, :, :], mem[0].rearrange("(a p) d -> p a d", p=P)).then_inc(mem_in, 16)
                if 18 <= n < 21:
                    load_gate_up(0, n - 18, 0, n - 18)

            sp.wait_ge(quarter_used, 4 * (U_MV + 2))
            load_gate_up(0, 3, 0, 3)
            late = [(brow, b_router.partition_broadcast(P).rearrange("p a d -> p (a d)"))]
            late += [(bgu[32 * k:32 * k + 32, :], b_gate_up[0, :, HALF * k:HALF * k + HALF])
                    for k in range(4)]
            late += [(bdn[32 * k:32 * k + 32, :], b_down[0, :, HALF * k:HALF * k + HALF])
                     for k in range(2)]
            def steps(b, first, last):
                for j in range(STEPS):
                    if not (last and j == STEPS - 1):
                        for q in range(4):
                            m = 6 * j + 4 + q
                            if first and m == 5:
                                sp.wait_ge(mo_read, MEM_HEADS)
                                for to, of in late:
                                    sp.dma_start(to, of).then_inc(late_in, 16)
                            await_place(b, m)
                            load_gate_up(b, m, (STEPS * b + j + 1) % E, q)
                    for q in range(2):
                        m = 6 * j + 8 + q
                        await_place(b, m)
                        load_down(b, m, (STEPS * b + j) % E, q)

            steps(0, True, False)
            sp.wait_ge(route_ready, 1)
            middle = sp.value_load(middle_count[0:1, 0:1], min_val=E // STEPS - 2,
                                   max_val=ROUNDS * E // STEPS - 2)
            with sp.Fori(1, middle + 1) as b:
                steps(b, False, False)
            sp.wait_ge(expert_used, 9)
            sp.dma_start(gfin, norm_final.rearrange("(a d) -> a d", a=1).partition_broadcast(P)
                         .rearrange("p a d -> p (a d)")).then_inc(final_gain_in, 16)
            steps(middle + 1, False, True)
            for a in range(TT):
                sp.wait_ge(xn_ready, 4 + a)
                sp.dma_start(out[0, P * a:P * a + P, :], xn[:, a, :]).then_inc(out_done, 16)
            sp.wait_ge(out_done, 16 * TT)

        @block.tensor
        def _(pe):
            def turn(k, src, half, ready):
                for a in range(TT):
                    ready(a)
                    for c in range(4 * half, 4 * half + 4):
                        if k == 1 and a == 0 and c % 2 == 0:
                            pe.wait_ge(turned_low, c // 2 + 1)
                        at = (c % 2) * T + a * P
                        i = pe.transpose(bank[2 + c // 2][:, at:at + P],
                                         src[:, a, c * P:c * P + P], ident)
                        if a == TT - 1 and c % 2:
                            i.then_inc(turned, 1)

            def three(to, lhs, rhs, start, stop):
                pe.matmul(to, lhs[0], rhs[0], start=start, stop=False, skip_group_check=True)
                pe.matmul(to, lhs[0], rhs[1], start=False, stop=False, skip_group_check=True)
                return pe.matmul(to, lhs[1], rhs[0], start=False, stop=stop,
                                 skip_group_check=True)

            def await_quarter(n, q):
                pe.wait_ge(low_ready, 4 * n + q + 1)

            def await_bank(b, u):
                if u > 0:
                    pe.wait_ge((bank0_read, bank1_read)[b], u)

            def project_T(n, h, low, ks=(0, KC), qs=(0, 4), ready=None):
                for q in range(*qs):
                    b, at = q // 2, (q % 2) * T
                    if ks[0] == 0:
                        await_quarter(n, q)
                        if at == 0:
                            await_bank(b, use(n))
                    w = quarter(n, HIGH_SLOT, q), quarter(n, n % DENSE_SLOTS, q)
                    for k in range(*ks):
                        if q == 0 and ready and k % 2 == 0:
                            ready(k)
                        i = three(bank[b][:, at:at + T], [x[:, k, :] for x in w],
                                  (h[:, k, :], low[:, k, :]),
                                  k == 0 and (at == 0 or ks[1] == KC), k == KC - 1)
                    if ks[1] == KC:
                        i.then_inc(quarter_used, 1)

            def project(n, h, low, ready=None, between=None, within=None):
                for a in range(TT):
                    await_bank(a, use(n))
                    for k in range(KC):
                        if a == 0 and k % 2 == 0:
                            await_quarter(n, k // 2)
                        if a == 0 and ready:
                            ready(k)
                        if a == 1 and k == 4 and within:
                            within()
                        w = quarter(n, HIGH_SLOT, k // 2), quarter(n, n % DENSE_SLOTS, k // 2)
                        i = three(bank[a][:, :], [x[:, k, a * P:a * P + P] for x in (h, low)],
                                  [x[:, k % 2, :] for x in w], k == 0, k == KC - 1)
                        if a == 1 and k % 2:
                            i.then_inc(quarter_used, 1)
                    if a == 0:
                        i.then_inc(tile0_full, 1)
                        if between:
                            between()

            def project_up(n, q0, h, low, base):
                for q in (q0, q0 + 1):
                    await_quarter(n, q)
                    await_bank(q % 2, use(n, q // 2))
                    w = quarter(n, HIGH_SLOT, q), quarter(n, n % DENSE_SLOTS, q)
                    for o in range(2):
                        for k in range(4):
                            i = three(bank[q % 2][:, T * o:T * o + T],
                                      [x[:, k, P * o:P * o + P] for x in w],
                                      (h[:, base + k, :], low[:, base + k, :]), k == 0, k == 3)
                    i.then_inc(quarter_used, 1)

            def sb_scores(p):
                for hh in range(2):
                    h = 2 * p + hh
                    zb = bank[2 + 2 * (p % 2) + hh]
                    rows = slice(HEAD * hh, HEAD * hh + HEAD)
                    if p >= 2:
                        pe.wait_ge(w_ready, h - 3)
                    if p == 0:
                        pe.wait_ge(turned_low, 8)
                        pe.wait_ge(bank0_read, use(U_SBK + 1))
                        pe.wait_ge(bank1_read, use(U_SBK + 1))
                    pe.matmul(zb[:, 0:T], kT[rows, p, 0:P], qT[rows, p, :],
                              start=True, stop=False, skip_group_check=True)
                    pe.matmul(zb[:, T:T + P], kT[rows, p, P:T], qT[rows, p, P:T], start=False,
                              stop=False, skip_group_check=True).then_inc(z_full, 1)

            def sb_after(p):
                for hh in range(2):
                    h = 2 * p + hh
                    zb = bank[2 + 2 * (p % 2) + hh]
                    pe.wait_ge(l_masked, h + 1)
                    ntri, nones = cst[:, C_NTRI:C_NTRI + P], cst[:, C_NONE:C_NONE + P]
                    pe.matmul(zb[:, 0:T], ntri, sp_l[:, hh, 0:T], start=False, stop=False,
                              skip_group_check=True)
                    pe.matmul(zb[:, P:T], nones, sp_l[:, hh, T:T + P], start=False, stop=False,
                              skip_group_check=True)
                    pe.matmul(zb[:, T:T + P], ntri, sp_l[:, hh, T:T + P], start=False, stop=True,
                              skip_group_check=True).then_inc(after_full, 1)

            def sb_values(p):
                if p > 0:
                    pe.wait_ge(sbo_read, p)
                pe.wait_ge(w_masked, 2 * p + 2)
                for key in range(TT):
                    first = P * key
                    at = slice(T * key, T * key + T - first)
                    for hh in range(2):
                        h = 2 * p + hh
                        i = pe.matmul(bank[7][HEAD * hh:HEAD * hh + HEAD, first:T],
                                      vs[:, key, HEAD * h:HEAD * h + HEAD], sp_w[:, hh, at],
                                      start=(key == 0), stop=(key == 1), skip_group_check=True)
                i.then_inc(sbo_full, 1)

            def rotate(n, g):
                if n or g:
                    pe.wait_ge(rot_read, 2 * n + g)
                else:
                    pe.wait_ge(gain_ready, 1)
                pe.wait_ge((bank0_read, bank1_read)[g], use((U_DQ, U_DK)[n]) + 1)
                pe.matmul(bank[6][:, :], cst[:, C_ROT:C_ROT + P],
                          raw[:, n, 2 * g:2 * g + 2, :].rearrange("p c t -> p (c t)"),
                          start=True, stop=True).then_inc(rot_full, 1)

            def diff_scores(h):
                pe.wait_ge(rot_read, 4)
                if h == 0:
                    pe.wait_ge(mask_ready, 1)
                    pe.wait_ge(w_ready, 6)
                else:
                    pe.wait_ge(dexp_ready, h)
                for c in range(2):
                    zb = bank[2 + c]
                    rows = slice(HEAD * c, HEAD * c + HEAD)
                    pe.matmul(zb[:, 0:P], dqk[rows, 0, h, 0:P], dqk[rows, 1, h, 0:P],
                              start=True, stop=False, skip_group_check=True)
                    pe.matmul(zb[:, P:P + T], dqk[rows, 0, h, P:T], dqk[rows, 1, h, :],
                              start=False, stop=False, skip_group_check=True)
                    pe.matmul(zb[:, 0:P], mask_split[:, 0, :], mask_split[:, 1, :],
                              start=False, stop=False, skip_group_check=True)
                    i = pe.matmul(zb[:, T:T + P], mask_split[:, 0, :], mask_split[:, 1, :],
                                  start=False, stop=True, skip_group_check=True)
                i.then_inc(dz_full, 1)

            def diff_turn(h):
                pe.wait_ge(dp_ready, h + 1)
                if h == 0:
                    pe.wait_ge(w_ready, 8)
                else:
                    pe.wait_ge(dpT_read, h)
                for k in range(3):
                    i = pe.transpose(bank[4][:, k * P:k * P + P], d_p[:, k * P:k * P + P], ident)
                i.then_inc(dpT_full, 1)

            def diff_values(h):
                pe.wait_ge(dpT_read, h + 1)
                if h > 0:
                    pe.wait_ge(do_read, h)
                cols = slice(P * h, P * h + P)
                pe.matmul(bank[5][:, 0:P], d_pT[:, 0:P], vd[:, 0, cols], start=True, stop=True)
                pe.matmul(bank[5][:, P:T], d_pT[:, P:T], vd[:, 0, cols], start=True, stop=False)
                pe.matmul(bank[5][:, P:T], d_pT[:, T:T + P], vd[:, 1, cols], start=False,
                          stop=True).then_inc(do_full, 1)

            def keep_busy(n, src, b):
                for _ in range(n):
                    pe.matmul(bank[b][:, 0:T], src[:, 0:P], src[:, 0:T], start=True, stop=True)

            pe.wait_ge(filler_ready, 1)
            keep_busy(9, hT.rearrange("p k t -> p (k t)"), 0)
            pe.wait_ge(ident_in, 16)
            pe.wait_ge(gains_in, 16 * 6)
            pe.transpose(bank[6][:, 0:33], grows[:, :], cst[0:33, C_ID:C_ID + 33])
            for j in range(2):
                i = pe.transpose(bank[6][:, 40 + 4 * j:44 + 4 * j], gffn[:, j:T:2],
                                 cst[0:4, C_ID:C_ID + 4])
            i.then_inc(gain_rows_T, 1)
            for half in range(2):
                turn(0, xn, half, lambda a: pe.wait_ge(xn_ready, 1))
            pe.wait_ge(pos_ready, 1)
            pe.matmul(bank[7][:, 0:T], cst[0:1, C_ONE:C_ONE + P], posf, start=True,
                      stop=True).then_inc(pos_spread, 1)
            keep_busy(5, xs[:, 0, :], 0)
            for n in range(U_UPS):
                if n == 0:
                    project_T(n, hT_high, hT_low, ready=lambda k: pe.wait_ge(turned_low, k // 2 + 1))
                elif n in (U_SBV, U_DV):
                    project(n, hT_high, hT_low)
                elif n < U_MK:
                    project_T(n, hT_high, hT_low)
                else:
                    project_T(n, hmT_high, hmT_low)
                if n == 1:
                    pe.wait_ge(const_in, 16)
                    for half in range(2):
                        turn(1, ms, half, lambda a: pe.wait_ge(xn_ready, 2))
                if n in (4, 5):
                    rotate(n - 4, 0)
                if 4 <= n < 8:
                    sb_values(n - 4)
                if 3 <= n < 7:
                    sb_after(n - 3)
                if 2 <= n < 6:
                    sb_scores(n - 2)
                if n in (4, 5):
                    rotate(n - 4, 1)
                if 8 <= n < 12:
                    diff_values(n - 8)
                if 7 <= n < 11:
                    diff_turn(n - 7)
                if 6 <= n < 10:
                    diff_scores(n - 6)
            pe.wait_ge(sbo_read, 4)
            project_up(U_UPS, 0, oT_high, oT_low, 0)
            pe.wait_ge(don_ready, 1)
            for h in range(DIFF_HEADS):
                for a in range(TT):
                    b = 4 + 2 * (h // 2)
                    at = (h % 2) * T + a * P
                    i = pe.transpose(bank[b][:, at:at + P], odn[:, a, P * h:P * h + P], ident)
            i.then_inc(doT_full, 1)
            project_up(U_UPS, 2, oT_high, oT_low, 0)
            pe.wait_ge(doT_read, 2)
            project_up(U_UPD, 0, oT_high, oT_low, 4)
            project_up(U_UPD, 2, oT_high, oT_low, 4)

            def await_mixed(k):
                if k % 2 == 0:
                    pe.wait_ge(mixed_ready, k // 2 + 1)

            project(U_OUT, mixed_high, mixed_low, await_mixed)

            def await_added(n):
                return lambda a: pe.wait_ge((bank0_read, bank1_read)[a], use(n) + 1)

            project(U_OUT + 1, mixed_high, mixed_low, None,
                    lambda: turn(2, xs, 0, await_added(U_OUT)))
            pe.wait_ge(turned_low, 10)
            project_T(U_MQ, hT_high, hT_low, (0, 4), (0, 2))
            turn(2, xs, 1, await_added(U_OUT + 1))
            project_T(U_MQ, hT_high, hT_low, (0, 4), (2, 4))
            pe.wait_ge(turned_low, 12)
            project_T(U_MQ, hT_high, hT_low, (4, KC))
            project_T(U_MQ + 1, hT_high, hT_low)

            def mem_scores(h):
                for a in range(TT):
                    zb = bank[2 + 2 * (h % 2) + a]
                    if h >= 2:
                        pe.wait_ge(mexp_ready, h - 1)
                    for c in range(2):
                        i = pe.matmul(zb[:, 0:T], oT[:, 2 * h + c, a * P:a * P + P],
                                      kTm[:, 2 * h + c, :], start=(c == 0), stop=(c == 1))
                i.then_inc(mz_full, 1)

            def mem_turn(h):
                pe.wait_ge(mp_ready, h + 1)
                if h == 3:
                    pe.wait_ge(mexp_ready, 3)
                elif h > 0:
                    pe.wait_ge(mpT_read, h)
                for m in range(TT):
                    for a in range(TT):
                        i = pe.transpose(bank[MEM_PT[h]][:, m * T + a * P:m * T + a * P + P],
                                         m_p[:, h % 2, a, m * P:m * P + P], ident)
                i.then_inc(mpT_full, 1)

            def mem_values(h):
                pe.wait_ge(mpT_read, h + 1)
                if h in (1, 2):
                    pe.wait_ge(mo_read, h)
                for c in range(2):
                    for m in range(TT):
                        d0 = MEM_HEAD * h + P * c
                        i = pe.matmul(bank[MEM_O[h]][:, c * T:c * T + T], vm[:, m, d0:d0 + P],
                                      m_pT[:, h % 2, m, :], start=(m == 0), stop=(m == TT - 1))
                i.then_inc(mo_full, 1)

            def await_read(n):
                pe.wait_ge(bank0_read, use(n) + 1)
                pe.wait_ge(bank1_read, use(n) + 1)

            await_read(U_MQ)
            mem_scores(0)
            mem_scores(1)
            project(U_MV, hmT_high, hmT_low)
            mem_turn(0)
            await_read(U_MQ + 1)
            mem_scores(2)
            await_read(U_MV)
            mem_values(0)
            mem_turn(1)
            mem_scores(3)
            mem_values(1)
            project(U_MV + 1, hmT_high, hmT_low)
            mem_turn(2)
            mem_turn(3)
            await_read(U_MV + 1)
            mem_values(2)
            mem_values(3)

            def await_head(k):
                if k % 2 == 0:
                    pe.wait_ge(mo_read, k // 2 + 1)

            project(U_MO, hT_high, hT_low, await_head)

            def router(a, ks):
                for k in range(*ks):
                    i = pe.matmul(bank[6][:, a * E:a * E + E], rT[:, k, a * P:a * P + P], wr[:, k, :],
                                  start=(a == 0 and k == 0), stop=(k == KC - 1),
                                  skip_group_check=True)
                return i

            pe.wait_ge(router_in, 16)

            def early_router():
                turn_rest(0)
                pe.wait_ge(turned_high, 13)
                pe.wait_ge(turned_low, 13)
                for a in range(TT):
                    router(a, (0, 4))

            def turn_rest(a):
                await_added(U_MO + 1)(a)
                for c in range(4, KC):
                    at = (c % 2) * T + a * P
                    i = pe.transpose(bank[2 + c // 2][:, at:at + P], xs[:, a, c * P:c * P + P], ident)
                    if c % 2:
                        i.then_inc(turned, 1)

            project(U_MO + 1, hT_high, hT_low, None,
                    lambda: turn(3, xs, 0, await_added(U_MO)), early_router)
            for a in range(TT):
                pe.wait_ge(turned_high, 14 + a)
                pe.wait_ge(turned_low, 14 + a)
                i = router(a, (4, KC))
                if a == 0:
                    turn_rest(1)
            i.then_inc(logit_full, 1)
            keep_busy(5, xs[:, 0, :], 5)
            pe.wait_ge(chosen_ready, 1)
            stri = cst[:, C_STRI:C_STRI + P]
            pe.matmul(bank[7][:, 0:E], stri, chosen[:, 0, :], start=True, stop=True)
            pe.matmul(bank[7][:, E:2 * E], stri, chosen[:, 1, :], start=True, stop=False)
            pe.matmul(bank[7][:, E:2 * E], ones, chosen[:, 0, :], start=False,
                      stop=True).then_inc(rank_full, 1)
            pe.matmul(bank[6][:, 0:E], ones, chosen[:, 0, :], start=True, stop=False)
            pe.matmul(bank[6][:, 0:E], ones, chosen[:, 1, :], start=False, stop=True).then_inc(count_full, 1)

            def gather(i):
                pe.wait_ge(pick_ready, i + 1)
                for a in range(TT):
                    for h in range(2):
                        ins = pe.matmul(bank[4][SLOTS * h:SLOTS * h + SLOTS, :], pick[:, a, :],
                                        xn[:, a, HALF * h:HALF * h + HALF], start=(a == 0),
                                        stop=(a == TT - 1))
                ins.then_inc(xg_full, 1)

            def gather_turn(i):
                pe.wait_ge(xg_ready, i + 1)
                for t in range(4):
                    at = 256 * (t // 2) + t % 2
                    ins = pe.transpose(bank[4][:, t * P:t * P + P], xg[:, at:at + 256 - t % 2:2], ident)
                ins.then_inc(xe_full, 1)

            def spread(i, a, buf, b=6, y=yb):
                for h in range(2):
                    rows = slice(SLOTS * h, SLOTS * h + SLOTS)
                    ins = pe.matmul(bank[b + h][:, :], comb[rows, buf, a * P:a * P + P],
                                    y[rows, :], start=True, stop=True)
                ins.then_inc(spread_full, 1)

            def step(b, j, i, prev, cur, nxt, nxt2):
                if cur:
                    pe.wait_ge(act_ready, i + 1)
                    if prev:
                        pe.wait_ge(actT_ready, i)
                    for r in range(4):
                        ins = pe.transpose(bank[3][:, r * P:r * P + P], act[:, r:HALF:4], ident)
                    ins.then_inc(actT_full, 1)
                    pe.wait_ge(pickg_ready, i + 1)
                    if prev:
                        pe.wait_ge(comb_ready, i)
                    for a in range(TT):
                        ins = pe.transpose(bank[5][:, a * P:a * P + P], pickg[:, a, :], ident)
                    ins.then_inc(comb_full, 1)
                if prev:
                    pe.wait_ge(y_ready, i)
                    pe.wait_ge(comb_ready, i)
                    if prev == "second":
                        pe.wait_ge(added, 2 * i - 2)
                    spread(i - 1, 0, (j - 1) % 2)
                if nxt:
                    pe.wait_ge(esel_ready, i + 2)
                    for k in range(4):
                        pe.matmul(bank[k // 2][SLOTS * (k % 2):SLOTS * (k % 2) + SLOTS, :],
                                  esel[:, (j + 1) % 4, k:k + 1].broadcast_to([P, SLOTS]), bgu,
                                  start=True, stop=False)
                    pe.wait_ge(xe_ready, i + 2)
                    for q in range(4):
                        w, arrived, count = expert_unit(b, 6 * j + 4 + q if j >= 0 else q)
                        pe.wait_ge(arrived, count)
                        w = w.rearrange("p (j n) -> p j n", j=2)
                        for r in range(2):
                            for k in range(4):
                                ins = pe.matmul(
                                    bank[k // 2][SLOTS * (k % 2):SLOTS * (k % 2) + SLOTS, :],
                                    xe[:, (j + 1) % 2, 2 * (q % 2) + r, q // 2, :],
                                    w[:, r, HALF * k:HALF * k + HALF],
                                    start=False, stop=(q == 3 and r == 1))
                        ins.then_inc(expert_used, 1)
                        if q == 1 and prev:
                            pe.wait_ge(added, 2 * i - 1)
                            spread(i - 1, 1, (j - 1) % 2)
                if nxt2:
                    pe.wait_ge(xe_ready, i + 2)
                    gather(i + 2)
                if nxt2 and not cur:
                    gather_turn(i + 2)
                if cur:
                    if prev:
                        pe.wait_ge(y_ready, i)
                    for h in range(2):
                        pe.matmul(bank[2][SLOTS * h:SLOTS * h + SLOTS, :],
                                  esel[:, j % 4, h:h + 1].broadcast_to([P, SLOTS]), bdn,
                                  start=True, stop=False)
                    pe.wait_ge(actT_ready, i + 1)
                    for q in range(2):
                        w, arrived, count = expert_unit(b, 6 * j + 8 + q)
                        pe.wait_ge(arrived, count)
                        w = w.rearrange("p (j n) -> p j n", j=4)
                        for r in range(4):
                            for h in range(2):
                                ins = pe.matmul(bank[2][SLOTS * h:SLOTS * h + SLOTS, :],
                                                actT[:, P * r + SLOTS * q:P * r + SLOTS * q + SLOTS],
                                                w[:, r, HALF * h:HALF * h + HALF],
                                                start=False, stop=(q == 1 and r == 3))
                        ins.then_inc(expert_used, 1)
                        if q == 0 and nxt2:
                            gather_turn(i + 2)
                        if q == 1 and not nxt:
                            pe.wait_ge(added, 2 * i - 1)
                            spread(i - 1, 1, (j - 1) % 2)

            pe.wait_ge(late_in, 16 * 7)
            pe.wait_ge(xn_ready, 3)
            gather(0)
            gather_turn(0)
            step(0, -1, -1, None, False, True, True)
            for j in range(STEPS):
                step(0, j, j, (None, "first", "second", "second")[j], True, True, True)
            middle = pe.value_load(middle_count[0:1, 0:1], min_val=E // STEPS - 2,
                                   max_val=ROUNDS * E // STEPS - 2)
            with pe.Fori(1, middle + 1) as b:
                for j in range(STEPS):
                    step(b, j, STEPS * b + j, "second", True, True, True)
            b = middle + 1
            for j in range(STEPS):
                step(b, j, STEPS * b + j, "second", True, j < STEPS - 1, j < STEPS - 2)
            n = STEPS * b + STEPS
            pe.wait_ge(y_ready, n)
            spread(n - 1, 0, 1, 0, xg)
            pe.wait_ge(added, 2 * n - 2)
            spread(n - 1, 1, 1, 6, xg)

        @block.scalar
        def _(act_e):
            steps_done = [0]

            def link(ins):
                steps_done[0] += 1
                ins.then_inc(act_step, 1)
                act_e.wait_ge(act_step, steps_done[0])

            def high_of_unit(n, quarters):
                for q in quarters:
                    if n == 0:
                        act_e.wait_ge(first_in[q], 16)
                    elif q == 0:
                        act_e.wait_ge(unit_in[n % DENSE_SLOTS],
                                      16 * (n // DENSE_SLOTS + (n % DENSE_SLOTS > 0)))
                    if n > 0:
                        act_e.wait_ge(quarter_used, 4 * (n - 1) + q + 1)
                    act_e.activation(quarter(n, HIGH_SLOT, q), quarter(n, n % DENSE_SLOTS, q, ring),
                                     ACT.Copy).then_inc(high_ready, 1)

            def turned_to(dst, k, g0, pairs=range(4)):
                for p in pairs:
                    act_e.wait_ge(turned, 4 * k + p + 1)
                    for c in range(2):
                        i = act_e.activation(dst[:, 2 * p + c, :], bank[2 + p][:, c * T:c * T + T],
                                             ACT.Copy, scale=gT[:, g0 + 2 * p + c:g0 + 2 * p + c + 1])
                    i.then_inc(turned_high, 1)

            def from_bank0(n, dst, scale=1.0):
                await_full(act_e, n, 0)
                act_e.activation(dst, bank[0][:, :], ACT.Copy, scale=scale).then_inc(bank0_read, 1)

            def mem_turned(h):
                act_e.wait_ge(mpT_full, h + 1)
                if h >= 2:
                    act_e.wait_ge(mo_full, h - 1)
                act_e.activation(m_pT[:, h % 2].rearrange("p m t -> p (m t)"), bank[MEM_PT[h]][:, :],
                                 ACT.Copy).then_inc(mpT_read, 1)

            act_e.wait_ge(filler_ready, 1)
            act_e.activation(st[:, 92:93], hT[:, 0, 0:1], ACT.Sqrt)
            for a in range(TT):
                act_e.wait_ge(x_in[a], 16)
                i = act_e.activation(xn[:, a, :], xs[:, a, :], ACT.Square, accum_out=st[:, a:a + 1])
            i.then_inc(sq_ready, 1)
            act_e.wait_ge(ms_ready, 1)
            act_e.activation(st[:, 2:4], st[:, 0:2], ACT.Sqrt).then_inc(rt_ready, 1)
            act_e.wait_ge(ident_in, 16)
            act_e.wait_ge(gain_ready, 1)
            turned_to(hT_high, 0, 0, (0, 1))
            high_of_unit(0, (0,))
            turned_to(hT_high, 0, 0, (2, 3))
            high_of_unit(0, (1, 2, 3))
            def fold(ap):
                return ap.rearrange("p c t -> p (c t)")

            for n in range(U_UPS):
                high_of_unit(n + 1, (0, 1))
                if n == U_SBQ:
                    from_bank0(n, fold(qT[:, 0:2, :]), HEAD ** -0.5)
                elif n == U_SBK:
                    from_bank0(n, fold(kT[:, 0:2, :]))
                elif n == U_SBV:
                    from_bank0(n, vs[:, 0, :])
                elif n == U_DQ:
                    from_bank0(n, fold(raw[:, 0, 0:2, :]), HEAD ** -0.5)
                elif n == U_DK:
                    from_bank0(n, fold(raw[:, 1, 0:2, :]))
                elif n == U_DV:
                    from_bank0(n, vd[:, 0, :])
                elif n < U_MK:
                    g = n - U_GSB
                    from_bank0(n, fold(sg[:, g // 2, 4 * (g % 2):4 * (g % 2) + 2, :]))
                else:
                    from_bank0(n, fold(kTm[:, 4 * (n - U_MK):4 * (n - U_MK) + 2, :]))
                high_of_unit(n + 1, (2, 3))
                if n == 0:
                    act_e.wait_ge(mem_in, 16)
                    for a in range(TT):
                        i = act_e.activation(kTm[:, 4 * a:4 * a + 4, :].rearrange("p k t -> p (k t)"),
                                             ms[:, a, :], ACT.Square, accum_out=st[:, 4 + a:5 + a])
                    i.then_inc(sq_ready, 1)
                    act_e.wait_ge(ms_ready, 2)
                    act_e.activation(st[:, 6:8], st[:, 4:6], ACT.Sqrt).then_inc(rt_ready, 1)
                    act_e.wait_ge(const_in, 16)
                    act_e.wait_ge(ang_ready, 1)
                    act_e.activation(scr[:, 2304:2816], ang, ACT.Sin).then_inc(rope_ready, 1)
                if n == 1:
                    turned_to(hmT_high, 1, 16)
                    act_e.wait_ge(lam_dots, 1)
                    act_e.activation(st[:, 82:84], st[:, 80:82], ACT.Exp).then_inc(lam_exp, 1)
                if n == 10:
                    act_e.wait_ge(bank1_read, use(U_MK))
                    for g in range(2):
                        i = act_e.activation(sg[:, g], sg[:, g], ACT.Sigmoid)
                    i.then_inc(gate_ready, 1)
                if 3 <= n < 7:
                    for hh in range(2):
                        h = 2 * (n - 3) + hh
                        act_e.wait_ge(after_full, h + 1)
                        if n > 3:
                            act_e.wait_ge(sbo_full, n - 3)
                        act_e.activation(sp_w[:, hh, :], bank[2 + 2 * ((n - 3) % 2) + hh][:, 0:384],
                                         ACT.Exp).then_inc(w_ready, 1)
                if 2 <= n < 6:
                    for hh in range(2):
                        h = 2 * (n - 2) + hh
                        act_e.wait_ge(z_full, h + 1)
                        if n > 2:
                            act_e.wait_ge(l_ready, h - 1)
                        t = sp_t[:, hh, :]
                        link(act_e.activation(t, bank[2 + 2 * ((n - 2) % 2) + hh][:, 0:384], ACT.Abs))
                        link(act_e.activation(t, t, ACT.Exp, scale=-1.0))
                        act_e.activation(t, t, ACT.Ln, bias=one).then_inc(soft_ready, 1)
                if 7 <= n < 11:
                    act_e.wait_ge(dpT_full, n - 6)
                    if n > 7:
                        act_e.wait_ge(do_full, n - 7)
                    act_e.activation(d_pT, bank[4][:, 0:384], ACT.Copy).then_inc(dpT_read, 1)
                if 6 <= n < 10:
                    h = n - 6
                    act_e.wait_ge(dmax_ready, h + 1)
                    for c in range(2):
                        for a in range(TT):
                            k = 24 + 2 * c + a
                            cols = slice(0, P) if a == 0 else slice(P, P + T)
                            i = act_e.activation(d_e[:, c, cols], bank[2 + c][:, cols], ACT.Exp,
                                                 bias=st[:, k:k + 1], accum_out=st[:, k + 4:k + 5])
                    i.then_inc(dexp_ready, 1)
                if 8 <= n < 12:
                    h = n - 8
                    act_e.wait_ge(do_read, h + 1)
                    for a in range(TT):
                        i = act_e.activation(odn[:, a, P * h:P * h + P], od[:, a, P * h:P * h + P],
                                             ACT.Square, accum_out=st[:, 40 + 2 * h + a:41 + 2 * h + a])
                    i.then_inc(dsq_ready, 1)
            act_e.wait_ge(dms_ready, 1)
            act_e.activation(st[:, 48:56], st[:, 40:48], ACT.Sqrt).then_inc(drt_ready, 1)
            high_of_unit(U_UPD, (0, 1))
            act_e.wait_ge(doT_full, 1)
            for g in range(2):
                act_e.activation(fold(oT_high[:, 4 + 2 * g:6 + 2 * g, :]), bank[4 + 2 * g][:, :],
                                 ACT.Copy, scale=st[:, 88:89]).then_inc(doT_high, 1)
            high_of_unit(U_UPD, (2, 3))
            for c in range(4):
                high_of_unit(U_OUT, (c,))
                act_e.wait_ge(mixed_sum, c + 1)
                act_e.activation(fold(mixed_high[:, 2 * c:2 * c + 2, :]), fold(sg[:, 0, 2 * c:2 * c + 2, :]),
                                 ACT.Copy).then_inc(mixed_rounded, 1)
            high_of_unit(U_OUT + 1, range(4))
            turned_to(hT_high, 2, 8, (0, 1))
            high_of_unit(U_MQ, range(4))
            turned_to(hT_high, 2, 8, (2, 3))
            for a in range(TT):
                act_e.wait_ge((bank0_read, bank1_read)[a], use(U_OUT + 1) + 1)
                i = act_e.activation(scr[:, D * (a + 1):D * (a + 2)], xs[:, a, :], ACT.Square,
                                     accum_out=st[:, 8 + a:9 + a])
            i.then_inc(sq_ready, 1)
            act_e.wait_ge(ms_ready, 3)
            act_e.activation(st[:, 10:12], st[:, 8:10], ACT.Sqrt).then_inc(rt_ready, 1)
            for n in (U_MQ, U_MQ + 1):
                high_of_unit(n + 1, (0, 1))
                from_bank0(n, fold(oT[:, 4 * (n - U_MQ):4 * (n - U_MQ) + 2, :]), MEM_HEAD ** -0.5)
                high_of_unit(n + 1, (2, 3))

            def mem_exp(h):
                act_e.wait_ge(mmax_ready, h + 1)
                if h >= 2:
                    act_e.wait_ge(mpT_full, h - 1)
                for a in range(TT):
                    k = 60 + 4 * (h % 2) + a
                    i = act_e.activation(m_p[:, h % 2, a, :], bank[2 + 2 * (h % 2) + a][:, 0:T], ACT.Exp,
                                         bias=st[:, k:k + 1], scale=st[:, 10 + a:11 + a],
                                         accum_out=st[:, k + 2:k + 3])
                i.then_inc(mexp_ready, 1)

            def mem_out(h):
                act_e.wait_ge(mo_full, h + 1)
                act_e.activation(fold(hT_high[:, 2 * h:2 * h + 2, :]), bank[MEM_O[h]][:, :],
                                 ACT.Copy).then_inc(mo_high, 1)

            mem_exp(0)
            mem_exp(1)
            from_bank0(U_MV, vm[:, 0, 0:HALF])
            high_of_unit(U_MV + 1, range(4))
            mem_turned(0)
            mem_exp(2)
            mem_out(0)
            mem_turned(1)
            mem_exp(3)
            act_e.activation(st[:, 90:91], one, ACT.Sqrt)
            mem_out(1)
            from_bank0(U_MV + 1, vm[:, 0, HALF:D])
            high_of_unit(U_MO, (0, 1, 2))
            mem_turned(2)
            mem_turned(3)
            high_of_unit(U_MO, (3,))
            mem_out(2)
            mem_out(3)
            high_of_unit(U_MO + 1, range(4))
            turned_to(rT, 3, 24, (0,))
            for a in range(TT):
                turned_rest(act_e, 2, a, turned_high)
                act_e.wait_ge((bank0_read, bank1_read)[a], use(U_MO + 1) + 1)
                i = act_e.activation(scr[:, D * (a + 1):D * (a + 2)], xs[:, a, :], ACT.Square,
                                     accum_out=st[:, 12 + a:13 + a])
            i.then_inc(sq_ready, 1)
            act_e.wait_ge(ms_ready, 4)
            act_e.activation(st[:, 14:16], st[:, 12:14], ACT.Sqrt).then_inc(rt_ready, 1)
            act_e.wait_ge(rinv_ready, 4)
            for a in range(TT):
                i = act_e.activation(xn[:, a, :], xs[:, a, :], ACT.Copy, scale=st[:, 14 + a:15 + a])
            i.then_inc(xn_ready, 1)
            act_e.wait_ge(top_ready, 1)
            for a in range(TT):
                i = act_e.activation(tope[:, a, :], topv[:, a, 0:TOP_K], ACT.Exp,
                                     bias=few[:, a:a + 1], accum_out=few[:, 2 + a:3 + a])
            i.then_inc(gexp_ready, 1)

            def gathered(i):
                act_e.wait_ge(xg_full, i + 1)
                if not isinstance(i, int) or i > 0:
                    act_e.wait_ge(xe_full, i)
                act_e.activation(xg, bank[4][:, :], ACT.Copy).then_inc(xg_ready, 1)

            gathered(0)

            def step(b, j, i, prev, cur, nxt, nxt2):
                if cur:
                    act_e.wait_ge(actT_full, i + 1)
                    if prev:
                        act_e.wait_ge(expert_used, 6 * i + 4)
                    act_e.activation(actT, bank[3][:, :], ACT.Copy).then_inc(actT_ready, 1)
                    act_e.wait_ge(comb_full, i + 1)
                    act_e.activation(comb[:, j % 2, :], bank[5][:, 0:T], ACT.Copy).then_inc(comb_ready, 1)
                if nxt:
                    act_e.wait_ge(glu_ready, i + 2)
                    act_e.activation(sig, glu, ACT.Sigmoid, scale=ALPHA).then_inc(sig_ready, 1)
                if nxt2:
                    gathered(i + 2)
                if cur:
                    act_e.wait_ge(expert_used, 6 * i + (10 if nxt else 6))
                    if prev and nxt:
                        act_e.wait_ge(spread_full, 2 * i)
                    act_e.activation(yb if nxt else xg, bank[2][:, :], ACT.Copy).then_inc(y_ready, 1)

            step(0, -1, -1, False, False, True, True)
            for j in range(STEPS):
                step(0, j, j, j > 0, True, True, True)
            act_e.wait_ge(route_ready, 1)
            middle = act_e.value_load(middle_count[0:1, 0:1], min_val=E // STEPS - 2,
                                   max_val=ROUNDS * E // STEPS - 2)
            with act_e.Fori(1, middle + 1) as b:
                for j in range(STEPS):
                    step(b, j, STEPS * b + j, True, True, True, True)
            b = middle + 1
            for j in range(STEPS):
                step(b, j, STEPS * b + j, True, True, j < STEPS - 1, j < STEPS - 2)
            act_e.activation(st[:, 91:92], one, ACT.Sqrt)
            for a in range(TT):
                act_e.wait_ge(added, 2 * STEPS * b + 2 * STEPS - 1 + a)
                act_e.activation(xn[:, a, :], xs[:, a, :], ACT.Square,
                                 accum_out=st[:, 16 + a:17 + a]).then_inc(sq_ready, 1)
                act_e.wait_ge(ms_ready, 5 + a)
                act_e.activation(st[:, 18 + a:19 + a], st[:, 16 + a:17 + a], ACT.Sqrt).then_inc(rt_ready, 1)

        @block.gpsimd
        def _(pool):
            def keep_past(t):
                v = t.rearrange("p (b n) -> p b n", b=3)[:, 0:3:2, :]
                return pool.affine_select(out=v, in_=v, pattern=[[0, 2], [1, P]],
                                          compare_op=ALU.is_gt, fill=0.0, base=0,
                                          channel_multiplier=-1)

            pool.memset(hT[:, 0, :], 1.0).then_inc(filler_ready, 1)
            pool.wait_ge(ident_in, 16)
            pool.wait_ge(const_in, 16)
            pool.tensor_copy(mask_split[:, 0, :], ident)
            pool.tensor_copy(mask_split[:, 1, :], cst[:, C_DMASK:C_DMASK + P]).then_inc(mask_ready, 1)
            for n in range(2, 7):
                if n >= 3:
                    for hh in range(2):
                        pool.wait_ge(w_ready, 2 * (n - 3) + hh + 1)
                        keep_past(sp_w[:, hh, :]).then_inc(w_masked, 1)
                if n < 6:
                    for hh in range(2):
                        pool.wait_ge(l_ready, 2 * (n - 2) + hh + 1)
                        keep_past(sp_l[:, hh, :]).then_inc(l_masked, 1)
            for c in range(4):
                first, second = (sg[:, n, 2 * c:2 * c + 2, :].rearrange("p c t -> p (c t)")
                                 for n in range(2))
                pool.wait_ge((bank0_read, bank1_read)[c % 2], use(U_UPD, c // 2) + 1)
                pool.tensor_tensor(first, first, second, ALU.add).then_inc(mixed_sum, 1)

        @block.vector
        def _(dve):
            steps_done = [0]

            def link(ins):
                steps_done[0] += 1
                ins.then_inc(dve_step, 1)
                dve.wait_ge(dve_step, steps_done[0])

            def fold(ap):
                return ap.rearrange("p c t -> p (c t)")

            def mean_square(k):
                dve.wait_ge(sq_ready, k + 1)
                dve.tensor_scalar(st[:, 4 * k:4 * k + 2], st[:, 4 * k:4 * k + 2], 1.0 / D, EPS,
                                  ALU.mult, ALU.add).then_inc(ms_ready, 1)
                dve.wait_ge(rt_ready, k + 1)
                dve.reciprocal(st[:, 4 * k + 2:4 * k + 4],
                               st[:, 4 * k + 2:4 * k + 4]).then_inc(rinv_ready, 1)
                dve.wait_ge(rinv_ready, k + 1)

            def norm(k, src, dst):
                mean_square(k)
                for a in range(TT):
                    i = dve.tensor_scalar(dst[:, a, :], src[:, a, :], st[:, 4 * k + 2 + a:4 * k + 3 + a],
                                          None, ALU.mult)
                i.then_inc(xn_ready, 1)

            def low_of_unit(n, quarters):
                for q in quarters:
                    dve.wait_ge(high_ready, 4 * n + q + 1)
                    slot = n % DENSE_SLOTS
                    dve.tensor_tensor(quarter(n, slot, q), quarter(n, slot, q, ring),
                                      f32(quarter(n, HIGH_SLOT, q)),
                                      ALU.subtract).then_inc(low_ready, 1)

            def turned_to(high, low, k, g0, pairs=range(4)):
                if k < 2:
                    dve.wait_ge(turned, 4 * k + 4)
                for p in pairs:
                    dve.wait_ge(turned_high, 4 * k + p + 1)
                    for c in range(2):
                        i = dve.scalar_tensor_tensor(
                            low[:, 2 * p + c, :], bank[2 + p][:, c * T:c * T + T],
                            gT[:, g0 + 2 * p + c:g0 + 2 * p + c + 1], f32(high[:, 2 * p + c, :]),
                            ALU.mult, ALU.subtract)
                    i.then_inc(turned_low, 1)

            def from_bank1(n, dst, scale=None):
                await_full(dve, n, 1)
                if scale is None:
                    dve.tensor_copy(dst, bank[1][:, :]).then_inc(bank1_read, 1)
                else:
                    dve.tensor_scalar(dst, bank[1][:, :], scale, None, ALU.mult).then_inc(bank1_read, 1)

            norm(0, xs, xn)
            dve.wait_ge(gain_rows_T, 1)
            dve.tensor_copy(gT[:, :], bank[6][:, 0:33])
            dve.tensor_copy(gperm[:, :].rearrange("p (u j h) -> p j h u", j=2, h=2),
                            bank[6][:, 40:48].rearrange("p (j h u) -> p j h u", j=2, h=2)
                            ).then_inc(gain_ready, 1)
            dve.wait_ge(small_in, 16 * 5)
            dve.tensor_copy(posf, posi[:, :]).then_inc(pos_ready, 1)
            dve.wait_ge(gain_ready, 1)
            dve.tensor_scalar(st[:, 88:89], gT[:, 32:33], 1.0 - LAMBDA_INIT, None, ALU.mult)

            def rotary(n, g):
                if n == 0 and g == 0:
                    dve.wait_ge(rope_ready, 1)
                if g == 0:
                    dve.wait_ge(bank0_read, use((U_DQ, U_DK)[n]) + 1)
                if n or g:
                    dve.wait_ge(rot_read, 2 * n + g)
                cos2 = cosT.unsqueeze(1).to_broadcast([P, 2, T])
                sin2 = sinT.unsqueeze(1).to_broadcast([P, 2, T])
                rot = bank[6][:, :].rearrange("p (c t) -> p c t", c=2)
                dve.tensor_tensor(rtmp[:, 0], raw[:, n, 2 * g:2 * g + 2, :], cos2, ALU.mult)
                dve.wait_ge(rot_full, 2 * n + g + 1)
                link(dve.tensor_tensor(rtmp[:, 1], rot, sin2, ALU.mult))
                dve.tensor_tensor(dqk[:, n, 2 * g:2 * g + 2, :], rtmp[:, 0], rtmp[:, 1],
                                  ALU.add).then_inc(rot_read, 1)

            turned_to(hT_high, hT_low, 0, 0, (0, 1))
            low_of_unit(0, (0,))
            turned_to(hT_high, hT_low, 0, 0, (2, 3))
            low_of_unit(0, (1, 2, 3))

            dve.wait_ge(const_in, 16)
            dve.wait_ge(pos_spread, 1)
            link(dve.tensor_scalar(ang[:, T:2 * T], bank[7][:, 0:T], cst[:, C_INV:C_INV + 1], None,
                                   ALU.mult))
            link(dve.tensor_scalar(angn[:, T:2 * T], ang[:, T:2 * T], 1.0 / (2 * math.pi), ROUNDER,
                                   ALU.mult, ALU.add))
            link(dve.tensor_scalar(angn[:, 0:T], ang[:, T:2 * T], 1.0 / (2 * math.pi), 0.25,
                                   ALU.mult, ALU.add))
            link(dve.tensor_scalar(angn[:, 0:T], angn[:, 0:T], ROUNDER, None, ALU.add))
            link(dve.tensor_scalar(angn[:, :], angn[:, :], ROUNDER, None, ALU.subtract))
            link(dve.scalar_tensor_tensor(ang[:, 0:T], angn[:, 0:T], -TWO_PI_A, ang[:, T:2 * T],
                                          ALU.mult, ALU.add))
            link(dve.scalar_tensor_tensor(ang[:, T:2 * T], angn[:, T:2 * T], -TWO_PI_A,
                                          ang[:, T:2 * T], ALU.mult, ALU.add))
            for part in (TWO_PI_B, TWO_PI_C):
                link(dve.scalar_tensor_tensor(ang[:, :], angn[:, :], -part, ang[:, :], ALU.mult,
                                              ALU.add))
            link(dve.tensor_scalar(ang[:, 0:T], ang[:, 0:T], math.pi / 2, None, ALU.add))
            dve.tensor_scalar(ang[:, :], ang[:, :], 3.1415925, -3.1415925, ALU.min,
                              ALU.max).then_inc(ang_ready, 1)

            for n in range(U_UPS):
                low_of_unit(n + 1, (0, 1, 2))
                if n == U_SBQ:
                    from_bank1(n, fold(qT[:, 2:4, :]), HEAD ** -0.5)
                elif n == U_SBK:
                    from_bank1(n, fold(kT[:, 2:4, :]))
                elif n == U_SBV:
                    from_bank1(n, vs[:, 1, :])
                elif n == U_DQ:
                    from_bank1(n, fold(raw[:, 0, 2:4, :]), HEAD ** -0.5)
                elif n == U_DK:
                    from_bank1(n, fold(raw[:, 1, 2:4, :]))
                elif n == U_DV:
                    from_bank1(n, vd[:, 1, :])
                elif n < U_MK:
                    g = n - U_GSB
                    from_bank1(n, fold(sg[:, g // 2, 4 * (g % 2) + 2:4 * (g % 2) + 4, :]))
                else:
                    from_bank1(n, fold(kTm[:, 4 * (n - U_MK) + 2:4 * (n - U_MK) + 4, :]))
                low_of_unit(n + 1, (3,))
                if n == 0:
                    norm(1, ms, ms)
                    for r in range(2):
                        i = dve.tensor_tensor_reduce(scr[:, 4608 + HEAD * r:4608 + HEAD * r + HEAD],
                                                     lamr[:, 2 * r, :], lamr[:, 2 * r + 1, :], 1.0, 0.0,
                                                     ALU.mult, ALU.add, st[:, 80 + r:81 + r])
                    i.then_inc(lam_dots, 1)
                if n == 1:
                    turned_to(hmT_high, hmT_low, 1, 16)
                    dve.wait_ge(lam_exp, 1)
                    link(dve.tensor_tensor(st[:, 84:85], st[:, 83:84], st[:, 82:83], ALU.subtract))
                    link(dve.tensor_scalar(st[:, 84:85], st[:, 84:85], LAMBDA_INIT, None, ALU.subtract))
                if n in (4, 5):
                    rotary(n - 4, 0)
                if 4 <= n < 8:
                    p = n - 4
                    dve.wait_ge(sbo_full, p + 1)
                    link(dve.tensor_copy(oT_high[:, p, :], bank[7][:, 0:T]))
                    dve.tensor_tensor(oT_low[:, p, :], bank[7][:, 0:T], f32(oT_high[:, p, :]),
                                      ALU.subtract).then_inc(sbo_read, 1)
                if 2 <= n < 6:
                    for hh in range(2):
                        h = 2 * (n - 2) + hh
                        dve.wait_ge(soft_ready, h + 1)
                        if n > 2:
                            dve.wait_ge(after_full, h - 1)
                        dve.scalar_tensor_tensor(sp_l[:, hh, :], bank[2 + 2 * ((n - 2) % 2) + hh][:, 0:384],
                                                 0.0, sp_t[:, hh, :], ALU.max, ALU.add).then_inc(l_ready, 1)
                if n in (4, 5):
                    rotary(n - 4, 1)
                if 8 <= n < 12:
                    h = n - 8
                    dve.wait_ge(do_full, h + 1)
                    dve.tensor_copy(od[:, :, P * h:P * h + P],
                                    bank[5][:, 0:T].rearrange("p (a d) -> p a d", a=TT)).then_inc(do_read, 1)
                if 6 <= n < 10:
                    h = n - 6
                    dve.wait_ge(dz_full, h + 1)
                    if h > 0:
                        dve.wait_ge(dexp_ready, h)
                    for c in range(2):
                        for a in range(TT):
                            k = 24 + 2 * c + a
                            cols = slice(0, P) if a == 0 else slice(P, P + T)
                            i = dve.tensor_reduce(st[:, k:k + 1], bank[2 + c][:, cols], AX, ALU.max,
                                                  negate=True)
                    i.then_inc(dmax_ready, 1)
                    dve.wait_ge(dexp_ready, h + 1)
                    link(dve.reciprocal(st[:, 32:36], st[:, 28:32]))
                    link(dve.tensor_scalar(st[:, 34:36], st[:, 34:36], st[:, 84:85], None, ALU.mult))
                    if h > 0:
                        dve.wait_ge(dpT_full, h)
                    for a in range(TT):
                        cols = slice(0, P) if a == 0 else slice(P, P + T)
                        link(dve.tensor_scalar(d_e[:, 0, cols], d_e[:, 0, cols], st[:, 32 + a:33 + a],
                                               None, ALU.mult))
                        i = dve.scalar_tensor_tensor(d_p[:, cols], d_e[:, 1, cols],
                                                     st[:, 34 + a:35 + a], d_e[:, 0, cols], ALU.mult,
                                                     ALU.add)
                    i.then_inc(dp_ready, 1)
            dve.wait_ge(dsq_ready, DIFF_HEADS)
            dve.tensor_scalar(st[:, 40:48], st[:, 40:48], 1.0 / P, EPS, ALU.mult,
                              ALU.add).then_inc(dms_ready, 1)
            dve.wait_ge(drt_ready, 1)
            link(dve.reciprocal(st[:, 48:56], st[:, 48:56]))
            for h in range(DIFF_HEADS):
                for a in range(TT):
                    i = dve.tensor_scalar(odn[:, a, P * h:P * h + P], od[:, a, P * h:P * h + P],
                                          st[:, 48 + 2 * h + a:49 + 2 * h + a], None, ALU.mult)
            i.then_inc(don_ready, 1)

            def gated(n, c):
                part = fold(sg[:, n - U_UPS, 2 * c:2 * c + 2, :])
                await_full(dve, n, c % 2, c // 2)
                dve.tensor_tensor(part, bank[c % 2][:, :], part, ALU.mult).then_inc(
                    (bank0_read, bank1_read)[c % 2], 1)

            def mixed_rest(c):
                first, high, low = (fold(ap[:, 2 * c:2 * c + 2, :])
                                    for ap in (sg[:, 0], mixed_high, mixed_low))
                dve.wait_ge(mixed_rounded, c + 1)
                dve.tensor_tensor(low, first, f32(high), ALU.subtract).then_inc(mixed_ready, 1)

            dve.wait_ge(gate_ready, 1)
            gated(U_UPS, 0)
            gated(U_UPS, 1)
            low_of_unit(U_UPD, (0, 1))
            for g in range(2):
                dve.wait_ge(doT_high, g + 1)
                dve.scalar_tensor_tensor(fold(oT_low[:, 4 + 2 * g:6 + 2 * g, :]), bank[4 + 2 * g][:, :],
                                         st[:, 88:89], f32(fold(oT_high[:, 4 + 2 * g:6 + 2 * g, :])),
                                         ALU.mult, ALU.subtract).then_inc(doT_read, 1)
            gated(U_UPS, 2)
            gated(U_UPS, 3)
            low_of_unit(U_UPD, (2, 3))
            gated(U_UPD, 0)
            gated(U_UPD, 1)
            for c in range(4):
                low_of_unit(U_OUT, (c,))
                mixed_rest(c)
                if c < 2:
                    gated(U_UPD, c + 2)

            def add_to_x(n, b):
                await_full(dve, n, b)
                g = (n - U_OUT) % 2
                part = xs[:, b, HALF * g:HALF * g + HALF]
                dve.tensor_tensor(part, bank[b][:, :], part, ALU.add).then_inc(
                    (bank0_read, bank1_read)[b], 1)

            add_to_x(U_OUT, 0)
            low_of_unit(U_OUT + 1, (0, 1, 2))
            add_to_x(U_OUT, 1)
            low_of_unit(U_OUT + 1, (3,))
            add_to_x(U_OUT + 1, 0)
            turned_to(hT_high, hT_low, 2, 8, (0, 1))
            low_of_unit(U_MQ, (0, 1, 2))
            add_to_x(U_OUT + 1, 1)
            low_of_unit(U_MQ, (3,))
            turned_to(hT_high, hT_low, 2, 8, (2, 3))
            mean_square(2)
            for n in (U_MQ, U_MQ + 1):
                low_of_unit(n + 1, (0, 1, 2))
                from_bank1(n, fold(oT[:, 4 * (n - U_MQ) + 2:4 * (n - U_MQ) + 4, :]), MEM_HEAD ** -0.5)
                low_of_unit(n + 1, (3,))

            def mem_max(h):
                dve.wait_ge(mz_full, h + 1)
                k = 60 + 4 * (h % 2)
                for a in range(TT):
                    i = dve.tensor_reduce(st[:, k + a:k + a + 1], bank[2 + 2 * (h % 2) + a][:, 0:T], AX,
                                          ALU.max, negate=True)
                link(i)
                dve.tensor_tensor(st[:, k:k + 2], st[:, k:k + 2], st[:, 10:12],
                                  ALU.mult).then_inc(mmax_ready, 1)

            def mem_probs(h):
                k = 60 + 4 * (h % 2)
                dve.wait_ge(mexp_ready, h + 1)
                to = 70 + 2 * (h % 2)
                link(dve.reciprocal(st[:, to:to + 2], st[:, k + 2:k + 4]))
                for a in range(TT):
                    i = dve.tensor_scalar(m_p[:, h % 2, a, :], m_p[:, h % 2, a, :],
                                          st[:, to + a:to + a + 1], None, ALU.mult)
                i.then_inc(mp_ready, 1)

            def mem_out(h):
                dve.wait_ge(mo_high, h + 1)
                dve.tensor_tensor(fold(hT_low[:, 2 * h:2 * h + 2, :]), bank[MEM_O[h]][:, :],
                                  f32(fold(hT_high[:, 2 * h:2 * h + 2, :])), ALU.subtract).then_inc(mo_read, 1)

            mem_max(0)
            mem_max(1)
            mem_probs(0)
            mem_probs(1)
            low_of_unit(U_MV + 1, (0, 1))
            from_bank1(U_MV, vm[:, 1, 0:HALF])
            low_of_unit(U_MV + 1, (2, 3))
            mem_max(2)
            mem_out(0)
            mem_max(3)
            mem_probs(2)
            mem_out(1)
            mem_probs(3)
            low_of_unit(U_MO, (0, 1))
            from_bank1(U_MV + 1, vm[:, 1, HALF:D])
            low_of_unit(U_MO, (2, 3))
            mem_out(2)
            mem_out(3)
            add_to_x(U_MO, 0)
            low_of_unit(U_MO + 1, (0, 1, 2))
            add_to_x(U_MO, 1)
            low_of_unit(U_MO + 1, (3,))
            dve.wait_ge(turned, 12 + 2)
            for c in (2, 3):
                i = dve.tensor_scalar(rT[:, c, :], bank[3][:, (c % 2) * T:(c % 2) * T + T],
                                      gT[:, 24 + c:25 + c], None, ALU.mult)
            i.then_inc(turned_low, 1)
            for a in range(TT):
                add_to_x(U_MO + 1, a)
                turned_rest(dve, 3, a, turned_low)
            mean_square(3)
            dve.wait_ge(late_in, 16 * 7)

            def col(ap, i):
                return ap[:, bass.ds(i, 1)]

            def picks(i, j):
                for a in range(TT):
                    ins = dve.tensor_scalar(pick[:, a, :], cst[:, C_SLOT:C_SLOT + SLOTS],
                                            col(slot_of[:, a, :], i), None, ALU.is_equal)
                ins.then_inc(pick_ready, 1)
                dve.tensor_scalar(esel[:, j % 4, :], cst[:, C_BLK:C_BLK + 4],
                                  col(cst[:, C_EIDX:C_EIDX + ROUNDS * E], i), None,
                                  ALU.is_equal).then_inc(esel_ready, 1)

            dve.wait_ge(logit_full, 1)
            for a in range(TT):
                i = dve.scalar_tensor_tensor(lg[:, a, :], bank[6][:, a * E:a * E + E],
                                             st[:, 14 + a:15 + a], brow, ALU.mult, ALU.add)
            link(i)
            for a in range(TT):
                i = dve.max(topv[:, a, :], lg[:, a, :])
            link(i)
            link(dve.tensor_scalar(few[:, 0:2], topv[:, :, 0], -1.0, None, ALU.mult))
            for a in range(TT):
                i = dve.max_index(topi[:, a, :], topv[:, a, :], lg[:, a, :])
            i.then_inc(top_ready, 1)
            dve.wait_ge(top_ready, 1)
            link(dve.tensor_copy(topf, topi[:, :, :]))
            by_choice = [P, TT, TOP_K, E]
            iota = cst[:, C_IOTA:C_IOTA + E].unsqueeze(1).unsqueeze(1).to_broadcast(by_choice)
            link(dve.tensor_tensor(same, topf[:, :, 0:TOP_K].unsqueeze(3).to_broadcast(by_choice), iota,
                                   ALU.is_equal))
            dve.tensor_reduce(chosen, same.rearrange("p a k e -> p a e k"), AX,
                              ALU.add).then_inc(chosen_ready, 1)
            dve.wait_ge(rank_full, 1)
            link(dve.scalar_tensor_tensor(hot, bank[7][:, 0:2 * E], NOT_CHOSEN,
                                          chosen.rearrange("p a e -> p (a e)"), ALU.add, ALU.mult))
            by_round = [P, ROUNDS, E]
            for a in range(TT):
                i = dve.scalar_tensor_tensor(
                    slot_of[:, a, :].rearrange("p (r e) -> p r e", e=E),
                    hot[:, a * E:a * E + E].unsqueeze(1).to_broadcast(by_round), NOT_CHOSEN,
                    cst[:, C_R64:C_R64 + ROUNDS * E].rearrange("p (r e) -> p r e", e=E),
                    ALU.subtract, ALU.subtract)
            link(i)
            picks(0, 0)
            dve.wait_ge(gexp_ready, 1)
            link(dve.reciprocal(few[:, 4:6], few[:, 2:4]))
            link(dve.tensor_tensor(tope, tope, few[:, 4:6].unsqueeze(2).to_broadcast([P, TT, TOP_K]),
                                   ALU.mult))
            link(dve.tensor_tensor(same, same, tope.unsqueeze(3).to_broadcast(by_choice), ALU.mult))
            link(dve.tensor_reduce(gates, same.rearrange("p a k e -> p a e k"), AX, ALU.add))
            link(dve.tensor_copy(gate_of.rearrange("p a (r e) -> p a r e", e=E),
                                 gates.unsqueeze(2).to_broadcast([P, TT, ROUNDS, E])))
            dve.wait_ge(count_full, 1)
            link(dve.tensor_reduce(few[:, 6:7], bank[6][:, 0:E], AX, ALU.max))
            for r in range(1, ROUNDS):
                i = dve.tensor_scalar(few[:, 6 + r:7 + r], few[:, 6:7], float(SLOTS * r),
                                      float(E // STEPS), ALU.is_gt, ALU.mult)
            link(i)
            link(dve.tensor_reduce(few[:, 10:11], few[:, 7:10], AX, ALU.add))
            dve.tensor_scalar(middle_count[0:1, 0:1], few[0:1, 10:11], float(E // STEPS - 2), None,
                              ALU.add).then_inc(route_ready, 1)

            def gathered(i, j):
                dve.wait_ge(xe_full, i + 1)
                dve.tensor_tensor(xe[:, j % 2].rearrange("p t h s -> p (t h) s"),
                                  bank[4][:, :].rearrange("p (k s) -> p k s", k=KC),
                                  gperm[:, :].unsqueeze(2).to_broadcast([P, KC, SLOTS]),
                                  ALU.mult).then_inc(xe_ready, 1)

            def add_spread(a, b=6):
                for h in range(2):
                    part = xs[:, a, HALF * h:HALF * h + HALF]
                    ins = dve.tensor_tensor(part, bank[b + h][:, :], part, ALU.add)
                ins.then_inc(added, 1)

            def step(b, j, i, prev, cur, nxt, nxt2):
                if prev:
                    dve.wait_ge(spread_full, 2 * i - 1)
                    add_spread(0)
                if nxt2:
                    picks(i + 2, j + 2)
                if nxt:
                    if cur:
                        dve.wait_ge(comb_full, i + 1)
                    for a in range(TT):
                        ins = dve.tensor_scalar(pickg[:, a, :], cst[:, C_SLOT:C_SLOT + P],
                                                col(slot_of[:, a, :], i + 1),
                                                col(gate_of[:, a, :], i + 1), ALU.is_equal, ALU.mult)
                    ins.then_inc(pickg_ready, 1)
                if prev:
                    dve.wait_ge(spread_full, 2 * i)
                    add_spread(1)
                if nxt:
                    dve.wait_ge(expert_used, 6 * i + 8 if cur else 4)
                    dve.tensor_scalar(glu, bank[0][:, :], LIMIT, None, ALU.min).then_inc(glu_ready, 1)
                    dve.tensor_scalar(lin, bank[1][:, :], LIMIT, -LIMIT, ALU.min, ALU.max)
                    dve.wait_ge(sig_ready, i + 2)
                    dve.tensor_tensor(glu, glu, sig, ALU.mult).then_inc(gated_ready, 1)
                    dve.wait_ge(gated_ready, i + 2)
                    dve.scalar_tensor_tensor(act, lin, 1.0, glu, ALU.add, ALU.mult).then_inc(act_ready, 1)
                    if nxt2:
                        gathered(i + 2, j + 2)

            dve.wait_ge(route_ready, 1)
            gathered(0, 0)
            step(0, -1, -1, False, False, True, True)
            for j in range(STEPS):
                step(0, j, j, j > 0, True, True, True)
            middle = dve.value_load(middle_count[0:1, 0:1], min_val=E // STEPS - 2,
                                   max_val=ROUNDS * E // STEPS - 2)
            with dve.Fori(1, middle + 1) as b:
                for j in range(STEPS):
                    step(b, j, STEPS * b + j, True, True, True, True)
            b = middle + 1
            for j in range(STEPS):
                step(b, j, STEPS * b + j, True, True, j < STEPS - 1, j < STEPS - 2)
            n = STEPS * b + STEPS
            for a in range(TT):
                dve.wait_ge(spread_full, 2 * n - 1 + a)
                add_spread(a, (0, 6)[a])
            dve.wait_ge(final_gain_in, 16)
            for a in range(TT):
                mean, rinv = st[:, 16 + a:17 + a], st[:, 18 + a:19 + a]
                dve.wait_ge(sq_ready, 5 + a)
                dve.tensor_scalar(mean, mean, 1.0 / D, EPS, ALU.mult, ALU.add).then_inc(ms_ready, 1)
                dve.wait_ge(rt_ready, 5 + a)
                link(dve.reciprocal(rinv, rinv))
                dve.scalar_tensor_tensor(xn[:, a, :], xs[:, a, :], rinv, gfin, ALU.mult,
                                         ALU.mult).then_inc(xn_ready, 1)


_INS = ["x", "mem", "positions", "norm_mix", "w_in", "lambda_q1", "lambda_k1", "lambda_q2",
        "lambda_k2", "diff_subln", "w_up_sb", "w_up_diff", "w_out", "norm_mem_q", "norm_mem_kv",
        "w_mem_q", "w_mem_kv", "w_mem_o", "norm_ffn", "w_router", "b_router", "w_gate_up",
        "b_gate_up", "w_down", "b_down", "norm_final"]


def kernel(**inputs):
    import concourse.bacc as bacc
    from concourse.bass_utils import run_bass_kernel_spmd

    nc = bacc.Bacc("TRN2", target_bir_lowering=False, num_devices=1)
    arrays = {"in_consts": constants()}
    arrays.update((f"in_{name}", np.ascontiguousarray(inputs[name])) for name in _INS)
    args = [nc.dram_tensor(name, a.shape, mybir.dt.from_np(a.dtype), kind="ExternalInput").ap()
            for name, a in arrays.items()]
    out = nc.dram_tensor("out", (1, T, D), F32, kind="ExternalOutput").ap()
    layer(nc, *args, out)
    return run_bass_kernel_spmd(nc, [arrays], core_ids=[0]).results[0]["out"]
```
